# Optimizing a Trainium2 kernel written in Bass

```python
import math
import jax, jax.numpy as jnp
from jax import lax
import numpy as np

D_MODEL = 1024
BATCH = 1
SEQ = 1024
DEPTH = 1

CHUNK = 64
EPS = 1e-6

DN_HEADS = 4
DN_DK = 128
DN_DV = 128
DN_QK_W = DN_HEADS * DN_DK
DN_V_W = DN_HEADS * DN_DV
DN_QKV_W = 2 * DN_QK_W + DN_V_W
CONV_WIDTH = 4

SWA_Q_HEADS = 8
SWA_KV_HEADS = 2
SWA_HEAD_DIM = 64
SWA_Q_W = SWA_Q_HEADS * SWA_HEAD_DIM
SWA_KV_W = SWA_KV_HEADS * SWA_HEAD_DIM
SWA_WINDOW = 128
SWA_WINDOW_CHUNKS = SWA_WINDOW // CHUNK

PEER_HEADS = 8
PEER_N_KEYS = 128
PEER_N_EXPERTS = PEER_N_KEYS * PEER_N_KEYS
PEER_D_KEY = 256
PEER_D_HALF = PEER_D_KEY // 2
PEER_TOPK = 16
PEER_TOKEN_BLOCK = 128

IN_SIZES = (DN_QKV_W, DN_HEADS, DN_HEADS, DN_V_W, SWA_Q_W, SWA_KV_W, SWA_KV_W, D_MODEL, D_MODEL)
IN_WIDTH = sum(IN_SIZES)

kernel_name = 'hybrid_deltanet_swa_peer_block'

def rms_norm(x, gain):
    xf = x.astype(jnp.float32)
    y = xf * lax.rsqrt(jnp.mean(xf * xf, axis=-1, keepdims=True) + EPS)
    return (y * gain.astype(jnp.float32)).astype(x.dtype)

def l2_normalize(t):
    tf = t.astype(jnp.float32)
    return tf * lax.rsqrt(jnp.sum(tf * tf, axis=-1, keepdims=True) + EPS)

def split_columns(t, sizes):
    out = []
    start = 0
    for s in sizes:
        out.append(t[..., start:start + s])
        start += s
    return out

def causal_depthwise_conv(x, w):
    K = w.shape[1]
    S_ = x.shape[1]
    xp = jnp.pad(x, ((0, 0), (K - 1, 0), (0, 0)))
    y = xp[:, 0:S_] * w[:, 0]
    for j in range(1, K):
        y = y + xp[:, j:j + S_] * w[:, j]
    return y

def gated_delta_rule_chunked(q, k, v, log_decay, beta):
    f32 = jnp.float32
    B_, S_, H, dk = q.shape
    dv = v.shape[-1]
    n = S_ // CHUNK

    def to_chunks(t):
        return t.astype(f32).reshape(B_, n, CHUNK, H, -1).transpose(1, 0, 3, 2, 4)

    qc = to_chunks(q) * (dk ** -0.5)
    kc = to_chunks(k)
    vc = to_chunks(v)
    g = log_decay.astype(f32).reshape(B_, n, CHUNK, H).transpose(1, 0, 3, 2)
    bt = beta.astype(f32).reshape(B_, n, CHUNK, H).transpose(1, 0, 3, 2)
    g = jnp.cumsum(g, axis=-1)

    idx = jnp.arange(CHUNK)
    incl = idx[:, None] >= idx[None, :]
    strict = idx[:, None] > idx[None, :]
    gam = jnp.exp(jnp.where(incl, g[..., :, None] - g[..., None, :], -jnp.inf))

    kb = kc * bt[..., None]
    lower = jnp.where(strict, jnp.einsum('nbhid,nbhjd->nbhij', kb, kc) * gam, 0.0)
    eye = jnp.eye(CHUNK, dtype=f32)
    t_inv = lax.linalg.triangular_solve(eye + lower, jnp.broadcast_to(eye, lower.shape),
                                        left_side=True, lower=True, unit_diagonal=True)
    u = jnp.einsum('nbhij,nbhje->nbhie', t_inv, vc * bt[..., None])
    w = jnp.einsum('nbhij,nbhjd->nbhid', t_inv, kb * jnp.exp(g)[..., None])
    a_qk = jnp.where(incl, jnp.einsum('nbhid,nbhjd->nbhij', qc, kc) * gam, 0.0)
    q_dec = qc * jnp.exp(g)[..., None]
    g_last = g[..., -1]
    k_dec = kc * jnp.exp(g_last[..., None] - g)[..., None]

    def step(state, inp):
        q_d, k_d, u_c, w_c, a_c, gl = inp
        v_new = u_c - jnp.einsum('bhcd,bhde->bhce', w_c, state)
        o = jnp.einsum('bhcd,bhde->bhce', q_d, state) + jnp.einsum('bhij,bhje->bhie', a_c, v_new)
        state = state * jnp.exp(gl)[..., None, None] + jnp.einsum('bhcd,bhce->bhde', k_d, v_new)
        return state, o

    s0 = jnp.zeros((B_, H, dk, dv), f32)
    _, o = lax.scan(step, s0, (q_dec, k_dec, u, w, a_qk, g_last))
    return o.transpose(1, 0, 3, 2, 4).reshape(B_, S_, H, dv)

def swa_sink_attention(q, k, v, sinks):
    f32 = jnp.float32
    B_, S_, Hq, d = q.shape
    Hkv = k.shape[2]
    G = Hq // Hkv
    n = S_ // CHUNK
    qc = q.astype(f32).reshape(B_, n, CHUNK, Hkv, G, d) * (d ** -0.5)
    kc = k.astype(f32).reshape(B_, n, CHUNK, Hkv, d)
    vc = v.astype(f32).reshape(B_, n, CHUNK, Hkv, d)

    def shifted(t, j):
        return jnp.pad(t, ((0, 0), (j, 0), (0, 0), (0, 0), (0, 0)))[:, :n]

    shifts = list(range(SWA_WINDOW_CHUNKS - 1, -1, -1))
    kw = jnp.concatenate([shifted(kc, j) for j in shifts], axis=2)
    vw = jnp.concatenate([shifted(vc, j) for j in shifts], axis=2)
    chunk_id = jnp.arange(n)
    valid = jnp.concatenate([jnp.broadcast_to((chunk_id >= j)[:, None], (n, CHUNK)) for j in shifts], axis=1)

    s = jnp.einsum('bnqhgd,bnkhd->bnhgqk', qc, kw)
    s = jnp.where(valid[None, :, None, None, None, :], s, -jnp.inf)
    sink = sinks.astype(f32).reshape(Hkv, G)[None, None, :, :, None, None]
    m = jnp.maximum(jnp.max(s, axis=-1, keepdims=True), sink)
    p = jnp.exp(s - m)
    denom = jnp.sum(p, axis=-1, keepdims=True) + jnp.exp(sink - m)
    o = jnp.einsum('bnhgqk,bnkhd->bnqhgd', p / denom, vw)
    return o.reshape(B_, S_, Hq * d)

def peer_ffn(x, w_q, sub_keys, u_emb, v_emb):
    f32 = jnp.float32
    B_, S_, D = x.shape
    T = B_ * S_
    K = PEER_TOPK
    xt = x.reshape(T // PEER_TOKEN_BLOCK, PEER_TOKEN_BLOCK, D)

    def block(xb):
        q = (xb @ w_q).astype(f32).reshape(PEER_TOKEN_BLOCK, PEER_HEADS, 2, PEER_D_HALF)
        s = jnp.einsum('thpd,hpnd->thpn', q, sub_keys.astype(f32))
        sv, si = lax.top_k(s, K)
        cand = sv[:, :, 0, :, None] + sv[:, :, 1, None, :]
        cv, ci = lax.top_k(cand.reshape(PEER_TOKEN_BLOCK, PEER_HEADS, K * K), K)
        i1 = jnp.take_along_axis(si[:, :, 0], ci // K, axis=-1)
        i2 = jnp.take_along_axis(si[:, :, 1], ci % K, axis=-1)
        e = i1 * PEER_N_KEYS + i2
        gate = jax.nn.softmax(cv, axis=-1)
        act = jax.nn.gelu(jnp.einsum('thkd,td->thk', u_emb[e], xb).astype(f32), approximate=False)
        return jnp.einsum('thk,thkd->td', (gate * act).astype(xb.dtype), v_emb[e])

    out = lax.map(block, xt)
    return out.reshape(B_, S_, D)

def setup_inputs(seed: int = 0) -> dict:
    key = jax.random.key(seed)
    ks = jax.random.split(key, 24)
    f32 = jnp.float32
    L = DEPTH
    D = D_MODEL

    def nrm(k, shape, scale):
        return jax.random.normal(k, shape, f32) * scale

    dt = jnp.exp(jax.random.uniform(ks[8], (L, DN_HEADS), f32, math.log(1e-3), math.log(1e-1)))
    return {
        'x': nrm(ks[0], (BATCH, SEQ, D), 1.0),
        'c': nrm(ks[1], (BATCH, D), 1.0),
        'ada_w': nrm(ks[2], (L, D, 6 * D), 0.5 * D ** -0.5),
        'ada_b': nrm(ks[3], (L, 6 * D), 0.02),
        'norm1_gain': 1.0 + nrm(ks[4], (L, D), 0.02),
        'w_in': nrm(ks[5], (L, D, IN_WIDTH), D ** -0.5),
        'conv_w': nrm(ks[6], (L, DN_QKV_W, CONV_WIDTH), CONV_WIDTH ** -0.5),
        'dn_a_log': jnp.log(jax.random.uniform(ks[7], (L, DN_HEADS), f32, 1.0, 16.0)),
        'dn_dt_bias': dt + jnp.log(-jnp.expm1(-dt)),
        'dn_out_gain': 1.0 + nrm(ks[9], (L, DN_DV), 0.02),
        'swa_sinks': nrm(ks[10], (L, SWA_Q_HEADS), 1.0),
        'w_dn_up': nrm(ks[11], (L, DN_V_W, D), DN_V_W ** -0.5),
        'w_swa_up': nrm(ks[12], (L, SWA_Q_W, D), SWA_Q_W ** -0.5),
        'w_out': nrm(ks[13], (L, D, D), D ** -0.5),
        'norm2_gain': 1.0 + nrm(ks[14], (L, D), 0.02),
        'peer_w_q': nrm(ks[15], (L, D, PEER_HEADS * PEER_D_KEY), D ** -0.5),
        'peer_sub_keys': nrm(ks[16], (L, PEER_HEADS, 2, PEER_N_KEYS, PEER_D_HALF), PEER_D_HALF ** -0.5),
        'peer_u': nrm(ks[17], (L, PEER_N_EXPERTS, D), D ** -0.5),
        'peer_v': nrm(ks[18], (L, PEER_N_EXPERTS, D), PEER_HEADS ** -0.5),
        'final_gain': 1.0 + nrm(ks[19], (D,), 0.02),
    }

def reference(x, c, ada_w, ada_b, norm1_gain, w_in, conv_w, dn_a_log, dn_dt_bias, dn_out_gain,
              swa_sinks, w_dn_up, w_swa_up, w_out, norm2_gain, peer_w_q, peer_sub_keys, peer_u,
              peer_v, final_gain):
    f32 = jnp.float32
    B_, S_, D = x.shape
    for l in range(DEPTH):
        mod = jax.nn.silu(c) @ ada_w[l] + ada_b[l]
        shift1, scale1, gate1, shift2, scale2, gate2 = jnp.split(mod[:, None, :], 6, axis=-1)

        h = rms_norm(x, norm1_gain[l]) * (1.0 + scale1) + shift1
        dn_qkv, dn_a, dn_b, dn_z, sw_q, sw_k, sw_v, g_dn, g_sw = split_columns(h @ w_in[l], IN_SIZES)

        dn_qkv = jax.nn.silu(causal_depthwise_conv(dn_qkv, conv_w[l]))
        dq, dk, dv = split_columns(dn_qkv, (DN_QK_W, DN_QK_W, DN_V_W))
        dq = l2_normalize(dq.reshape(B_, S_, DN_HEADS, DN_DK))
        dk = l2_normalize(dk.reshape(B_, S_, DN_HEADS, DN_DK))
        dv = dv.reshape(B_, S_, DN_HEADS, DN_DV)
        log_decay = -jnp.exp(dn_a_log[l].astype(f32)) * jax.nn.softplus(dn_a.astype(f32) + dn_dt_bias[l].astype(f32))
        beta = jax.nn.sigmoid(dn_b.astype(f32))
        o_dn = gated_delta_rule_chunked(dq, dk, dv, log_decay, beta).astype(x.dtype)
        o_dn = rms_norm(o_dn, dn_out_gain[l]) * jax.nn.silu(dn_z.reshape(B_, S_, DN_HEADS, DN_DV))
        y_dn = o_dn.reshape(B_, S_, DN_V_W) @ w_dn_up[l]

        o_sw = swa_sink_attention(sw_q.reshape(B_, S_, SWA_Q_HEADS, SWA_HEAD_DIM),
                                  sw_k.reshape(B_, S_, SWA_KV_HEADS, SWA_HEAD_DIM),
                                  sw_v.reshape(B_, S_, SWA_KV_HEADS, SWA_HEAD_DIM),
                                  swa_sinks[l]).astype(x.dtype)
        y_sw = o_sw @ w_swa_up[l]

        merged = jax.nn.sigmoid(g_dn) * y_dn + jax.nn.sigmoid(g_sw) * y_sw
        x = x + gate1 * (merged @ w_out[l])

        h2 = rms_norm(x, norm2_gain[l]) * (1.0 + scale2) + shift2
        x = x + gate2 * peer_ffn(h2, peer_w_q[l], peer_sub_keys[l], peer_u[l], peer_v[l])
    return rms_norm(x, final_gain)


_drawn_inputs = setup_inputs


def setup_inputs(seed=0):
    import zlib

    import numpy as np

    out = dict(_drawn_inputs(seed))
    spreads = {}
    factors = {'ada_b': 3.793,
     'norm1_gain': 8.0,
     'dn_out_gain': 8.0,
     'swa_sinks': 8.0,
     'norm2_gain': 51.134,
     'final_gain': 7.845}
    for name, (base, spread) in spreads.items():
        noise = np.random.default_rng([zlib.crc32(name.encode()), seed]).standard_normal(out[name].shape)
        drawn = base * np.exp(spread * noise) if base else spread * noise
        out[name] = __import__('jax').numpy.asarray(drawn.astype(out[name].dtype))
    for name, factor in factors.items():
        out[name] = (out[name] * factor).astype(out[name].dtype)
    return out
```

```python
from contextlib import ExitStack

import numpy as np
import concourse.bass as bass
from concourse import mybir

P = 128
D = 1024
T = 1024
HALF = 512
DC = D // P
TILES = T // P
CHUNK = 64
EPS = 1e-6
H = 4
QH = 8
HD = 64
IN_JOBS = 21
SMALL = 8 + P
PH = 8
NK = 128
TOPK = 16
GROUP = 2
GROUPS = NK // GROUP
BIG = 1.0e30
LOWEST = -3.0e38

F32 = mybir.dt.float32
F32R = mybir.dt.float32r
U32 = mybir.dt.uint32
ALU = mybir.AluOpType
ACT = mybir.ActivationFunctionType
AX = mybir.AxisListType

CONSTS = ["c_keep", "c_masks"]
PARAMS = ["p_cols", "p_rows"]


def block_kernel(nc, a, out):
    KB = 1024
    base = 16512
    limit = 229368

    def at(name, shape, kb, dtype=F32):
        size = 4 * int(np.prod(shape[1:]))
        off = base + int(kb * KB)
        assert off + size <= limit, (name, off + size - limit)
        return nc.alloc_sbuf_tensor_at(name, list(shape), dtype, offset=off)

    ctx = ExitStack()
    with ctx:
        def sem(name):
            return ctx.enter_context(nc.semaphore(name))

        ps = ctx.enter_context(nc.psum_tensor("ps", [P, 8, 512], F32))

        keep = at("keep", [P, 3 * P], 0)
        ident, iota, ones = keep[:, 0:P], keep[:, P:2 * P], keep[:, 2 * P:3 * P]
        cols = at("cols", [P, 145], 1.5)
        C_, ADAB, G1, G2, GF, CONV, OGAIN = (cols[:, 0:8], cols[:, 8:56], cols[:, 56:64], cols[:, 64:72],
                                             cols[:, 72:80], cols[:, 80:128], cols[:, 128:129])
        rows = cols[:, 129:145]
        mod = at("mod", [P, 48], 2.25)
        silc = at("silc", [P, 8], 2.5)
        amp1 = at("amp1", [P, 8], 2.5625)
        amp2 = at("amp2", [P, 8], 2.625)
        O = 4

        xT = at("xT", [P, DC, T], O + 0)
        hT = at("hT", [P, DC, T], O + 32)
        qkv = at("qkv", [P, 12, T], O + 64)
        zq = at("zq", [P, 8, T], O + 112)
        swk = at("swk", [P, P + T], O + 144)
        vtok = at("vtok", [P, 1 + TILES, P], O + 148.5)
        masks = at("masks", [P, 4 * P + 6 * P + 4 * P], O + 153)
        tri, blk, neg = masks[:, 0:P], masks[:, P:2 * P], masks[:, 2 * P:3 * P]
        level = [masks[:, (3 + s) * P:(4 + s) * P] for s in range(6)]
        wmask = masks[:, 9 * P:11 * P]
        wmask0 = masks[:, 11 * P:13 * P]
        slab = at("slab", [P, 2, DC, 512], O + 64)
        wjob = at("wjob", [P, 3, DC, P], O + 161)
        sq = at("sq", [P, 2, T], O + 173)
        rstd = at("rstd", [P, 2, T], O + 181)
        pre = at("pre", [P, 3, 3 + T], O + 173)
        cacc = at("cacc", [P, 3, T], O + 185.25)
        wsmall = at("wsmall", [P, DC, SMALL], O + 197.25)
        ab = at("ab", [P, TILES, 8], O + 203)

        def dn(name, k, shape=(P, H, P)):
            return at(name, shape, O + 161 + 2 * k)
        ldb, btb, kn, qn, vv, gm, gam = [dn(n, k) for k, n in enumerate(["ldb", "btb", "kn", "qn", "vv", "gm", "gam"])]
        egrow, qdec, LT, AT, X, XT, t1 = [dn(n, 7 + k) for k, n in enumerate(["egrow", "qdec", "LT", "AT", "X", "XT", "t1"])]
        vb, kbe, kd, u, wT, St = [dn(n, 14 + k) for k, n in enumerate(["vb", "kbe", "kd", "u", "wT", "St"])]
        bt = gm
        vz = at("vz", [P, 2, H, P], O + 161 + 2 * 0)
        small = at("small", [P, 12, 32], O + 201.5)
        (adt, aab, lns, ld, beta, gcol, ngcol, dlt, eg, ekd, beg, nea) = [small[:, k, :] for k in range(12)]

        qz = at("qz", [P, QH, P], O + 161)
        vbuf = at("vbuf", [P, 2, P], O + 165)
        mbuf = at("mbuf", [P, 2 * P], O + 166)
        prob = at("prob", [P, QH, 2 * P], O + 167)
        probT = at("probT", [P, QH, 2, P], O + 175)
        prob2 = at("prob2", [P, QH, 2 * P], O + 183)
        stat = at("stat", [P, 6, QH], O + 191)

        wup = at("wup", [P, 2, 24, P], O + 161)
        sig = at("sig", [P, 2, 2, HALF], O + 185)
        mtmp = at("mtmp", [P, 2, 2, HALF], O + 193)
        merged = at("merged", [P, DC, T], O + 80)

        qT = at("qT", [P, 16, T], O + 64)
        qbuf = at("qbuf", [P, 16, P], O + 0)
        sc = at("sc", [P, 16, P], O + 8)
        sc2 = at("sc2", [P, 16, P], O + 16)
        subk = at("subk", [P, 16, P], O + 24)
        oneL = at("oneL", [P, 8, P], O + 16)
        oneR = at("oneR", [P, 8, P], O + 20)
        Gsb = at("Gsb", [P, NK, P], O + 128)
        sv = at("sv", [P, 16, TOPK], O + 192)
        si = at("si", [P, 16, TOPK], O + 193, U32)
        sif = at("sif", [P, 16, TOPK], O + 194)
        cv = at("cv", [P, PH, TOPK], O + 195)
        ci = at("ci", [P, PH, TOPK], O + 195.5, U32)
        cab = at("cab", [P, 2, PH * TOPK], O + 196, U32)
        cabf = at("cabf", [P, 2, PH * TOPK], O + 197)
        pick = at("pick", [P, 3, PH * TOPK], O + 198)
        rT = at("rT", [P, 3, P], O + 199.5)
        gsum = at("gsum", [P, 2, PH], O + 201)

        carrier = at("carrier", [P, 1], O + 202)

        acc = at("acc", [P, DC, T], O + 0)
        ust = at("ust", [P, 2, DC, P], O + 32)
        vst = at("vst", [P, 2, D], O + 40)
        gst = at("gst", [P, 2, T], O + 48)
        actb = at("actb", [P, 2, T], O + 56)
        h2hi = at("h2hi", [P, DC, T], O + 64, F32R)
        h2lo = at("h2lo", [P, DC, T], O + 96, F32R)
        uhi = at("uhi", [P, 2, DC, P], O + 128, F32R)
        ulo = at("ulo", [P, 2, DC, P], O + 136, F32R)
        vhi = at("vhi", [P, 2, D], O + 144, F32R)
        vlo = at("vlo", [P, 2, D], O + 152, F32R)
        whi = at("whi", [P, 2, 2, T], O + 160, F32R)
        wlo = at("wlo", [P, 2, 2, T], O + 176, F32R)
        wbuf = at("wbuf", [P, 2, T], O + 192)

        x2 = at("x2", [P, DC, T], O + 64)
        oT = at("oT", [P, DC, T], O + 96)
        esq = at("esq", [P, 2, T], O + 128)
        erstd = at("erstd", [P, 2, T], O + 136)

        x2_dram = nc.dram_tensor("x2_scratch", [D, T], F32, kind="Internal").ap()
        g_dram = nc.dram_tensor("gate_scratch", [NK, NK, T], F32, kind="Internal").ap()

        const_in, x_in, small_in, subk_in = sem("const_in"), sem("x_in"), sem("small_in"), sem("subk_in")
        slab_in = [sem(f"slab_in{s}") for s in range(2)]
        wjob_in = [sem(f"wjob_in{s}") for s in range(3)]
        wup_in = [sem(f"wup_in{s}") for s in range(2)]
        wout_in = [sem(f"wout_in{s}") for s in range(2)]
        wq_in = [sem(f"wq_in{s}") for s in range(2)]
        ust_in = [sem(f"ust_in{s}") for s in range(2)]
        vst_in = [sem(f"vst_in{s}") for s in range(2)]
        gst_in = [sem(f"gst_in{s}") for s in range(2)]
        x2_out, x2_in, g_out, y_out = sem("x2_out"), sem("x2_in"), sem("g_out"), sem("y_out")
        silc_ready, ada_mm, ada_add, mod_ready = sem("silc_ready"), sem("ada_mm"), sem("ada_add"), sem("mod_ready")
        nsq = [sem(f"norm{k}_squared") for k in range(3)]
        nmm = [sem(f"norm{k}_summed") for k in range(3)]
        nrt = [sem(f"norm{k}_root") for k in range(3)]
        nsc = [sem(f"norm{k}_scaled") for k in range(3)]
        nout = [sem(f"norm{k}_out") for k in range(3)]
        in_mm, in_copied, conv_step, conv_done, qkv_ready = (sem("in_mm"), sem("in_copied"), sem("conv_step"),
                                                             sem("conv_done"), sem("qkv_ready"))
        pads_zero, sm_mm, sm_copied = sem("pads_zero"), sem("sm_mm"), sem("sm_copied")
        l2_sq, l2_mm, l2_root, l2_inv, l2_done = sem("l2_sq"), sem("l2_mm"), sem("l2_root"), sem("l2_inv"), sem("l2_done")
        gate_vec, gate_act, gate_mm = sem("gate_vec"), sem("gate_act"), sem("gate_mm")
        dn_vec, dn_act, dn_mm = sem("dn_vec"), sem("dn_act"), sem("dn_mm")
        sw_vec, sw_act, sw_mm = sem("sw_vec"), sem("sw_act"), sem("sw_mm")
        gn_sq, gn_mm, gn_root, gn_vec, z_silu = sem("gn_sq"), sem("gn_mm"), sem("gn_root"), sem("gn_vec"), sem("z_silu")
        up_mm, up_sig, up_vec, up_done = sem("up_mm"), sem("up_sig"), sem("up_vec"), sem("up_done")
        wo_mm, x2_done = sem("wo_mm"), sem("x2_done")
        q_mm, q_copied = sem("q_mm"), sem("q_copied")
        qbuf_ready, sc_mm, sc_copied, rt_vec, rt_exp, rt_mm = (sem("qbuf_ready"), sem("sc_mm"), sem("sc_copied"),
                                                               sem("rt_vec"), sem("rt_exp"), sem("rt_mm"))
        one_ready, g_mm, g_copied = sem("one_ready"), sem("g_mm"), sem("g_copied")
        h2_hi, h2_lo, acc_zero = sem("h2_hi"), sem("h2_lo"), sem("acc_zero")
        uhi_ready, u_ready, u_mm, act_ready, w_ready, whi_ready, wlo_ready = (
            sem("uhi_ready"), sem("u_ready"), sem("u_mm"), sem("act_ready"), sem("w_ready"), sem("whi_ready"), sem("wlo_ready"))
        vhi_ready, v_ready, v_mm, flushed = sem("vhi_ready"), sem("v_ready"), sem("v_mm"), sem("flushed")
        x3_done = sem("x3_done")

        block = ctx.enter_context(nc.Block())

        DNV, DNA, DNM = 43, 15, 23
        SWV, SWA_, SWM = 12, 5, 3
        RTV = 26
        G_PER_TILE = P

        def halves(ap3, bank):
            return ps[:, bank:bank + 2, :].rearrange("p b n -> p (b n)")

        @block.sync
        def _(sp):
            sp.dma_start(keep[:], a["c_keep"]).then_inc(const_in, 16)
            sp.dma_start(cols[:], a["p_cols"]).then_inc(const_in, 16)
            sp.dma_start(masks[:, 0:13 * P], a["c_masks"]).then_inc(const_in, 16)
            sp.dma_start(xT[:], a["xT"].rearrange("(c p) t -> p c t", p=P)).then_inc(x_in, 16)
            ada = a["ada_w"].rearrange("(k p) n -> p k n", p=P)
            with sp.Fori(0, 6) as i:
                for s in range(2):
                    if s == 0:
                        sp.wait_ge(ada_mm, 2 * i)
                    sp.dma_start(slab[:, s], ada[:, :, bass.ds((2 * i + s) * 512, 512)]).then_inc(slab_in[s], 16)
            sp.dma_start(wsmall[:], a["w_small"]).then_inc(small_in, 16)
            with sp.Fori(0, IN_JOBS // 3) as i:
                for s in range(3):
                    sp.wait_ge(in_mm, 3 * i)
                    sp.dma_start(wjob[:, s], a["w_in"][bass.ds(3 * i + s, 1)].rearrange("o p k m -> p (o k) m")).then_inc(wjob_in[s], 16)
            sp.wait_ge(gn_vec, 3 * H)
            with sp.Fori(0, DC // 2) as i:
                for s in range(2):
                    sp.wait_ge(up_mm, 4 * i)
                    sp.dma_start(wup[:, s], a["w_up"][bass.ds(2 * i + s, 1)].rearrange("o p k m -> p (o k) m")).then_inc(wup_in[s], 16)
            sp.wait_ge(up_mm, 2 * DC)
            with sp.Fori(0, DC // 2) as i:
                for s in range(2):
                    sp.wait_ge(wo_mm, 2 * i)
                    sp.dma_start(wjob[:, s], a["w_out"][bass.ds(2 * i + s, 1)].rearrange("o p k m -> p (o k) m")).then_inc(wout_in[s], 16)
            sp.wait_ge(x2_done, DC)
            sp.dma_start(x2_dram.rearrange("(c p) t -> p c t", p=P), xT[:]).then_inc(x2_out, 16)
            with sp.Fori(0, 8) as i:
                for s in range(2):
                    if s == 0:
                        sp.wait_ge(q_mm, 2 * i)
                    sp.dma_start(wjob[:, s], a["w_q"][bass.ds(2 * i + s, 1)].rearrange("o p k m -> p (o k) m")).then_inc(wq_in[s], 16)
            sp.wait_ge(x2_out, 16)
            sp.wait_ge(nout[1], DC)
            sp.dma_start(subk[:], a["sub_k"]).then_inc(subk_in, 16)
            with sp.Fori(0, TILES) as i:
                sp.wait_ge(g_copied, 32 * i + 32)
                sp.dma_start(g_dram[:, :, bass.ds(i * P, P)].rearrange("j i t -> i j t"), Gsb[:]).then_inc(g_out, 16)
            sp.wait_ge(g_out, 16 * TILES)

            def load_u(g, s, first=False):
                if not first:
                    sp.wait_ge(uhi_ready, 2 * g + s - 1)
                    sp.wait_ge(u_ready, 2 * g + s - 1)
                sp.dma_start(ust[:, s], a["u"][bass.ds(2 * g + s, 1)].rearrange("o p k m -> p (o k) m")).then_inc(ust_in[s], 16)

            def load_g(g, s, first=False):
                if not first:
                    sp.wait_ge(w_ready, 2 * g + s - 1)
                sp.dma_start(gst[:, s], g_dram[bass.ds(2 * g + s, 1)].rearrange("o i t -> (o i) t")).then_inc(gst_in[s], 16)

            def load_v(g, s, first=False):
                if not first:
                    sp.wait_ge(vhi_ready, 2 * g + s - 1)
                    sp.wait_ge(v_ready, 2 * g + s - 1)
                sp.dma_start(vst[:, s], a["v"][bass.ds(2 * g + s, 1)].rearrange("o p n -> (o p) n")).then_inc(vst_in[s], 16)

            sp.wait_ge(h2_lo, DC)
            for s in range(2):
                load_u(0, s, True)
                load_g(0, s, True)
            for s in range(2):
                load_v(0, s, True)
            with sp.Fori(1, GROUPS) as g:
                for s in range(2):
                    load_u(g, s)
                    load_g(g, s)
                for s in range(2):
                    load_v(g, s)
            sp.wait_ge(v_mm, 16 * GROUPS)
            sp.dma_start(x2[:], x2_dram.rearrange("(c p) t -> p c t", p=P)).then_inc(x2_in, 16)
            sp.wait_ge(nout[2], DC)
            sp.dma_start(out.rearrange("(c p) t -> p c t", p=P), oT[:]).then_inc(y_out, 16)
            sp.wait_ge(y_out, 16)

        @block.gpsimd
        def _(pool):
            with pool.Fori(0, TILES) as i:
                pool.wait_ge(q_copied, 16)
                pool.wait_ge(x2_out, 16)
                pool.wait_ge(rt_vec, RTV * i)
                pool.tensor_copy(qbuf[:], qT[:, :, bass.ds(i * P, P)]).then_inc(qbuf_ready, 1)
            pool.wait_ge(sc_mm, TILES)
            pool.wait_ge(g_mm, T)
            pool.wait_ge(rt_vec, RTV * TILES)
            pool.memset(acc[:], 0.0).then_inc(acc_zero, 1)

        @block.tensor
        def _(pe):
            pe.wait_ge(silc_ready, 1)
            with pe.Fori(0, 6) as i:
                for s in range(2):
                    pe.wait_ge(slab_in[s], 16 * i + 16)
                    pe.wait_ge(ada_add, 2 * i)
                    for m in range(4):
                        for k in range(DC):
                            mm = pe.matmul(ps[:, s, m:m + 1], slab[:, s, k, m * P:(m + 1) * P], silc[:, k:k + 1],
                                           start=(k == 0), stop=(k == DC - 1))
                    mm.then_inc(ada_mm, 1)

            def norm_sum(n, src):
                for c in range(DC):
                    pe.wait_ge(nsq[n], c + 1)
                    for h in range(2):
                        mm = pe.matmul(ps[:, 6 + h, :], ones, src[:, c % 2, h * HALF:(h + 1) * HALF],
                                       start=(c == 0), stop=(c == DC - 1))
                    mm.then_inc(nmm[n], 1)

            norm_sum(0, sq)

            pe.wait_ge(nout[0], DC)
            with pe.Fori(0, IN_JOBS // 3) as i:
                for s in range(3):
                    pe.wait_ge(wjob_in[s], 16 * i + 16)
                    pe.wait_ge(in_copied, 3 * i)
                    for h in range(2):
                        for k in range(DC):
                            mm = pe.matmul(ps[:, 2 * s + h, :], wjob[:, s, k, :], hT[:, k, h * HALF:(h + 1) * HALF],
                                           start=(k == 0), stop=(k == DC - 1))
                    mm.then_inc(in_mm, 1)
            pe.wait_ge(small_in, 16)
            for t in range(TILES):
                if t >= 2:
                    pe.wait_ge(sm_copied, 2 * (t - 1))
                else:
                    pe.wait_ge(nrt[0], 1)
                for k in range(DC):
                    mm = pe.matmul(ps[:, 6 + t % 2, 0:SMALL], hT[:, k, t * P:(t + 1) * P], wsmall[:, k, :],
                                   start=(k == 0), stop=(k == DC - 1))
                mm.then_inc(sm_mm, 1)
            with pe.Fori(0, 4) as i:
                for s in range(2):
                    pe.wait_ge(l2_sq, 2 * i + s + 1)
                    pe.wait_ge(l2_root, 2 * i)
                    for h in range(2):
                        mm = pe.matmul(ps[:, 2 * s + h, :], ones, sq[:, s, h * HALF:(h + 1) * HALF], start=True, stop=True)
                    mm.then_inc(l2_mm, 1)
            pe.wait_ge(gate_vec, 4)
            pe.wait_ge(l2_root, 8)
            pe.matmul(ps[:, 0, 0:32], tri, ld, start=True, stop=True)
            pe.matmul(ps[:, 0, 32:64], blk, ld, start=True, stop=True).then_inc(gate_mm, 1)

            pe.wait_ge(gate_vec, 9)
            with pe.Fori(0, TILES) as i:
                v0, a0 = DNV * i, DNA * i

                def heads(bank, f, width=P):
                    for h in range(H):
                        m = f(h, ps[:, bank, h * width:(h + 1) * width])
                    return m
                pe.wait_ge(dn_act, a0)
                pe.wait_ge(dn_vec, v0 + 5)
                heads(0, lambda h, o: pe.matmul(o, ldb[:, h], tri, start=True, stop=True)).then_inc(dn_mm, 1)
                heads(1, lambda h, o: pe.matmul(o, btb[:, h], ident, start=True, stop=True)).then_inc(dn_mm, 1)
                heads(2, lambda h, o: pe.matmul(o, kn[:, h], kn[:, h], start=True, stop=True)).then_inc(dn_mm, 1)
                heads(3, lambda h, o: pe.matmul(o, kn[:, h], qn[:, h], start=True, stop=True)).then_inc(dn_mm, 1)
                heads(4, lambda h, o: pe.transpose(o, kn[:, h], ident)).then_inc(dn_mm, 1)
                heads(5, lambda h, o: pe.transpose(o, vv[:, h], ident)).then_inc(dn_mm, 1)
                for s in range(6):
                    pe.wait_ge(dn_vec, v0 + 17 + 3 * s)
                    heads(0, lambda h, o: pe.matmul(o, bt[:, h], X[:, h], start=True, stop=True)).then_inc(dn_mm, 1)
                    pe.wait_ge(dn_act, a0 + 6 + s)
                    if s < 5:
                        heads(1, lambda h, o: pe.matmul(o, XT[:, h], t1[:, h], start=True, stop=True))
                    heads(2, lambda h, o: pe.matmul(o, t1[:, h], XT[:, h], start=True, stop=True)).then_inc(dn_mm, 1)
                pe.wait_ge(dn_vec, v0 + 33)
                heads(3, lambda h, o: pe.matmul(o, XT[:, h], vb[:, h], start=True, stop=True))
                heads(4, lambda h, o: pe.matmul(o, kbe[:, h], XT[:, h], start=True, stop=True)).then_inc(dn_mm, 1)
                pe.wait_ge(dn_act, a0 + 13)
                for c in range(2):
                    lo = c * CHUNK
                    if c:
                        pe.wait_ge(dn_vec, v0 + 38)
                        pe.wait_ge(dn_act, a0 + 14)
                    heads(5, lambda h, o: pe.matmul(o, wT[:, h], St[:, h], start=True, stop=True)).then_inc(dn_mm, 1)
                    pe.wait_ge(dn_vec, v0 + 34 + 5 * c)
                    for h in range(H):
                        o = ps[:, 6, h * CHUNK:(h + 1) * CHUNK]
                        pe.matmul(o, St[:, h], qdec[:, h, lo:lo + CHUNK], start=True, stop=False)
                        pe.matmul(o, vz[:, c, h], AT[:, h, lo:lo + CHUNK], start=False, stop=True)
                    heads(7, lambda h, o: pe.matmul(o, kd[:, h], vz[:, c, h], start=True, stop=True)).then_inc(dn_mm, 1)

            pe.wait_ge(dn_act, DNA * TILES)
            pe.wait_ge(dn_vec, DNV * TILES)
            with pe.Fori(0, TILES) as i:
                v0, a0 = SWV * i, SWA_ * i
                pe.wait_ge(sw_act, a0)
                pe.wait_ge(sw_vec, v0 + 3)
                for h in range(QH):
                    mm = pe.matmul(ps[:, h // 2, (h % 2) * 256:(h % 2) * 256 + 256], qz[:, h], swk[:, bass.ds(i * P, 2 * P)],
                                   start=True, stop=True)
                mm.then_inc(sw_mm, 1)
                pe.wait_ge(sw_vec, v0 + 11)
                for h in range(QH):
                    for b in range(2):
                        j = 2 * h + b
                        mm = pe.transpose(ps[:, 4 + j // 4, (j % 4) * P:(j % 4 + 1) * P], prob2[:, h, b * P:(b + 1) * P], ident)
                mm.then_inc(sw_mm, 1)
                pe.wait_ge(sw_act, a0 + 3)
                for h in range(QH):
                    for b in range(2):
                        mm = pe.matmul(ps[:, h // 4, (h % 4) * P:(h % 4 + 1) * P], vbuf[:, b], probT[:, h, b],
                                       start=(b == 0), stop=(b == 1))
                mm.then_inc(sw_mm, 1)

            pe.wait_ge(sw_act, SWA_ * TILES)
            for c in range(H):
                pe.wait_ge(gn_sq, c + 1)
                if c >= 2:
                    pe.wait_ge(gn_root, c - 1)
                for h in range(2):
                    mm = pe.matmul(ps[:, 2 * (c % 2) + h, :], ones, sq[:, c % 2, h * HALF:(h + 1) * HALF], start=True, stop=True)
                mm.then_inc(gn_mm, 1)

            pe.wait_ge(gn_vec, 3 * H)
            with pe.Fori(0, DC // 2) as i:
                for s in range(2):
                    pe.wait_ge(wup_in[s], 16 * i + 16)
                    for h in range(2):
                        if s == 0:
                            pe.wait_ge(up_done, 4 * i)
                        else:
                            pe.wait_ge(up_done, 4 * i + 1 + h)
                        tok = slice(h * HALF, (h + 1) * HALF)
                        for bank, w0, n, src in ((0, 0, DC, hT), (1, 8, DC, hT), (2, 16, H, qkv), (3, 20, H, zq)):
                            for k in range(n):
                                x = src[:, 4 + k, tok] if src is zq else src[:, k, tok]
                                mm = pe.matmul(ps[:, 4 * h + bank, :], wup[:, s, w0 + k, :], x, start=(k == 0), stop=(k == n - 1))
                        mm.then_inc(up_mm, 1)

            def project(n, w_in_sem, done, read, x, step):
                with pe.Fori(0, n) as i:
                    for s in range(2):
                        pe.wait_ge(w_in_sem[s], 16 * i + 16)
                        pe.wait_ge(read, 2 * i)
                        for h in range(2):
                            for k in range(DC):
                                mm = pe.matmul(ps[:, 2 * s + h, :], wjob[:, s, k, :], x[:, k, h * HALF:(h + 1) * HALF],
                                               start=(k == 0), stop=(k == DC - 1))
                        mm.then_inc(done, 1)

            pe.wait_ge(up_done, 2 * DC)
            project(DC // 2, wout_in, wo_mm, x2_done, merged, 2)
            norm_sum(1, sq)
            pe.wait_ge(nout[1], DC)
            project(8, wq_in, q_mm, q_copied, hT, 2)

            pe.wait_ge(subk_in, 16)
            with pe.Fori(0, TILES) as i:
                pe.wait_ge(qbuf_ready, i + 1)
                pe.wait_ge(rt_vec, RTV * i)
                for j in range(16):
                    mm = pe.matmul(ps[:, j // 4, (j % 4) * P:(j % 4 + 1) * P], qbuf[:, j], subk[:, j], start=True, stop=True)
                mm.then_inc(sc_mm, 1)
                pe.wait_ge(rt_vec, RTV * i + RTV - 1)
                for j in range(3):
                    mm = pe.transpose(ps[:, 0, j * P:(j + 1) * P], pick[:, j, :], ident)
                mm.then_inc(rt_mm, 1)
                with pe.Fori(0, P // 16) as j:
                    n0 = 16 * (8 * i + j)
                    for t in range(16):
                        pe.wait_ge(one_ready, n0 + t + 1)
                        if t % 4 == 0:
                            pe.wait_ge(g_copied, 4 * (8 * i + j) + t // 4 - 3) if t == 12 else pe.wait_ge(g_copied, 4 * (8 * i + j))
                        pe.matmul(ps[:, 4 + t // 4, (t % 4) * P:(t % 4 + 1) * P], oneL[:, t % 8], oneR[:, t % 8],
                                  start=True, stop=True).then_inc(g_mm, 1)

            pe.wait_ge(h2_lo, DC)
            pe.wait_ge(g_copied, 32 * TILES)

            def u_block(g, s, first=False):
                pe.wait_ge(u_ready, 2 * g + s + 1)
                if not first:
                    pe.wait_ge(act_ready, 2 * g + s - 1)
                for h in range(2):
                    tok = slice(h * HALF, (h + 1) * HALF)
                    for k in range(DC):
                        o = ps[:, 2 * s + h, :]
                        pe.matmul(o, uhi[:, s, k], h2hi[:, k, tok], start=(k == 0), stop=False)
                        pe.matmul(o, uhi[:, s, k], h2lo[:, k, tok], start=False, stop=False)
                        mm = pe.matmul(o, ulo[:, s, k], h2hi[:, k, tok], start=False, stop=(k == DC - 1))
                mm.then_inc(u_mm, 1)

            def v_group(g, par, first=False):
                pe.wait_ge(wlo_ready, 2 * g + 2)
                pe.wait_ge(v_ready, 2 * g + 2)
                for b in range(16):
                    c, h = b // 2, b % 2
                    tok = slice(h * HALF, (h + 1) * HALF)
                    if not (first and b < 4):
                        pe.wait_ge(flushed, 16 * g + b - 3)
                    o = ps[:, 4 + b % 4, :]
                    for s in range(2):
                        vh, vl = vhi[:, s, c * P:(c + 1) * P], vlo[:, s, c * P:(c + 1) * P]
                        pe.matmul(o, vh, whi[:, par, s, tok], start=(s == 0), stop=False)
                        pe.matmul(o, vh, wlo[:, par, s, tok], start=False, stop=False)
                        mm = pe.matmul(o, vl, whi[:, par, s, tok], start=False, stop=(s == 1))
                    mm.then_inc(v_mm, 1)

            u_block(0, 0, True)
            u_block(0, 1, True)
            u_block(1, 0)
            u_block(1, 1)
            v_group(0, 0, True)
            with pe.Fori(1, GROUPS // 2) as i:
                for par in range(2):
                    g = 2 * i + par
                    u_block(g, 0)
                    u_block(g, 1)
                    v_group(g - 1, 1 - par)
            v_group(GROUPS - 1, 1)
            norm_sum(2, esq)

        @block.scalar
        def _(act):
            act.wait_ge(const_in, 48)
            act.activation(silc[:], C_, ACT.Silu).then_inc(silc_ready, 1)

            def norm_root(n, x, sqb, rt, ready=None):
                for c in range(DC):
                    if c >= 2:
                        act.wait_ge(nmm[n], c - 1)
                    if ready is not None:
                        act.wait_ge(ready, c + 1)
                    act.activation(sqb[:, c % 2], x[:, c], ACT.Square).then_inc(nsq[n], 1)
                act.wait_ge(nmm[n], DC)
                act.activation(rt[:, 0], halves(ps, 6), ACT.Sqrt, scale=1.0 / D, bias=EPS).then_inc(nrt[n], 1)

            act.wait_ge(x_in, 16)
            norm_root(0, xT, sq, rstd)

            act.wait_ge(pads_zero, 1)
            with act.Fori(0, 4) as i:
                for s in range(3):
                    act.wait_ge(in_mm, 3 * i + s + 1)
                    act.wait_ge(conv_done, 3 * i)
                    act.activation(pre[:, s, 3:3 + T], halves(ps, 2 * s), ACT.Copy).then_inc(in_copied, 1)
                for s in range(3):
                    act.wait_ge(conv_done, 3 * i + s + 1)
                    act.activation(qkv[:, bass.ds(3 * i + s, 1), :].rearrange("p o t -> p (o t)"), cacc[:, s], ACT.Silu).then_inc(qkv_ready, 1)
            with act.Fori(0, 2) as i:
                for s in range(3):
                    act.wait_ge(in_mm, 12 + 3 * i + s + 1)
                    act.activation(zq[:, bass.ds(3 * i + s, 1), :].rearrange("p o t -> p (o t)"), halves(ps, 2 * s), ACT.Copy).then_inc(in_copied, 1)
            for s in range(3):
                act.wait_ge(in_mm, 18 + s + 1)
                dst = zq[:, 6 + s] if s < 2 else swk[:, P:P + T]
                act.activation(dst, halves(ps, 2 * s), ACT.Copy).then_inc(in_copied, 1)
            act.wait_ge(conv_done, 12)
            act.wait_ge(qkv_ready, 12)
            with act.Fori(0, 4) as i:
                for s in range(2):
                    act.wait_ge(l2_mm, 2 * i)
                    act.activation(sq[:, s], qkv[:, bass.ds(2 * i + s, 1), :].rearrange("p o t -> p (o t)"), ACT.Square).then_inc(l2_sq, 1)
                for s in range(2):
                    act.wait_ge(l2_mm, 2 * i + s + 1)
                    act.wait_ge(l2_inv, 2 * i)
                    act.activation(rstd[:, s], halves(ps, 2 * s), ACT.Sqrt, bias=EPS).then_inc(l2_root, 1)

            act.wait_ge(gate_vec, 1)
            act.activation(aab, adt, ACT.Abs).then_inc(gate_act, 1)
            act.wait_ge(gate_act, 1)
            act.activation(lns, aab, ACT.Exp, scale=-1.0).then_inc(gate_act, 1)
            act.wait_ge(gate_act, 2)
            act.activation(lns, lns, ACT.Ln, bias=1.0).then_inc(gate_act, 1)
            act.activation(nea[:, 0:H], rows[:, H:2 * H], ACT.Exp).then_inc(gate_act, 1)
            act.activation(beta.rearrange("p (t h) -> p t h", h=H), ab[:, :, H:2 * H], ACT.Sigmoid).then_inc(gate_act, 1)
            act.wait_ge(gate_vec, 7)
            act.activation(eg, gcol, ACT.Exp).then_inc(gate_act, 1)
            act.activation(ekd, dlt, ACT.Exp).then_inc(gate_act, 1)

            act.wait_ge(gate_vec, 9)
            with act.Fori(0, TILES) as i:
                v0, m0 = DNV * i, DNM * i
                act.wait_ge(dn_vec, v0 + 6)
                act.activation(egrow[:].rearrange("p h n -> p (h n)"), ps[:, 0, :], ACT.Exp).then_inc(dn_act, 1)
                for h in range(H):
                    act.activation(gam[:, h], gm[:, h], ACT.Exp, bias=ngcol[:, bass.ds(H * i + h, 1)]).then_inc(dn_act, 1)
                for s in range(6):
                    act.wait_ge(dn_mm, m0 + 7 + 2 * s)
                    act.activation(t1[:].rearrange("p h n -> p (h n)"), ps[:, 0, :], ACT.Copy).then_inc(dn_act, 1)
                act.wait_ge(dn_mm, m0 + 19)
                act.activation(u[:].rearrange("p h n -> p (h n)"), ps[:, 3, :], ACT.Copy).then_inc(dn_act, 1)
                act.activation(wT[:].rearrange("p h n -> p (h n)"), ps[:, 4, :], ACT.Copy).then_inc(dn_act, 1)
                for c in range(2):
                    act.wait_ge(dn_mm, m0 + 21 + 2 * c)
                    act.activation(qkv[:, 0:H, bass.ds(i * P + c * CHUNK, CHUNK)],
                                   ps[:, 6, 0:H * CHUNK].rearrange("p (h n) -> p h n", h=H), ACT.Copy).then_inc(dn_act, 1)

            with act.Fori(0, TILES) as i:
                v0, m0 = SWV * i, SWM * i
                act.wait_ge(sw_vec, v0 + 7)
                act.activation(prob[:], prob2[:], ACT.Exp).then_inc(sw_act, 1)
                act.activation(stat[:, 3], stat[:, 2], ACT.Exp).then_inc(sw_act, 1)
                act.wait_ge(sw_mm, m0 + 2)
                act.activation(probT[:].rearrange("p h b n -> p (h b n)"), ps[:, 4:8, :].rearrange("p b n -> p (b n)"), ACT.Copy).then_inc(sw_act, 1)
                act.wait_ge(sw_mm, m0 + 3)
                for r in range(2):
                    rr = slice(r * HD, (r + 1) * HD)
                    act.activation(zq[rr, 4:8, bass.ds(i * P, P)], ps[rr, r, :].rearrange("p (h n) -> p h n", h=4), ACT.Copy).then_inc(sw_act, 1)

            act.wait_ge(sw_mm, SWM * TILES)
            act.wait_ge(sw_vec, SWV * TILES)
            for c in range(H):
                act.activation(zq[:, c], zq[:, c], ACT.Silu).then_inc(z_silu, 1)
            for c in range(H):
                if c >= 2:
                    act.wait_ge(gn_mm, c - 1)
                act.activation(sq[:, c % 2], qkv[:, c], ACT.Square).then_inc(gn_sq, 1)
                act.wait_ge(gn_mm, c + 1)
                if c >= 2:
                    act.wait_ge(gn_vec, 3 * (c - 1))
                act.activation(rstd[:, c % 2], halves(ps, 2 * (c % 2)), ACT.Sqrt, scale=1.0 / P, bias=EPS).then_inc(gn_root, 1)

            act.wait_ge(gn_vec, 3 * H)
            with act.Fori(0, DC // 2) as i:
                for s in range(2):
                    for h in range(2):
                        n = 2 * (2 * i + s) + h
                        act.wait_ge(up_mm, n + 1)
                        act.wait_ge(up_done, 4 * i) if s == 0 else act.wait_ge(up_done, 4 * i + 1 + h)
                        for b in range(2):
                            act.activation(sig[:, h, b], ps[:, 4 * h + b, :], ACT.Sigmoid).then_inc(up_sig, 1)

            act.wait_ge(up_done, 2 * DC)
            norm_root(1, xT, sq, rstd, x2_done)

            with act.Fori(0, 8) as i:
                for s in range(2):
                    act.wait_ge(q_mm, 2 * i + s + 1)
                    act.activation(qT[:, bass.ds(2 * i + s, 1), :].rearrange("p o t -> p (o t)"), halves(ps, 2 * s), ACT.Copy).then_inc(q_copied, 1)

            with act.Fori(0, TILES) as i:
                act.wait_ge(sc_mm, i + 1)
                act.wait_ge(rt_vec, RTV * i)
                act.activation(sc[:].rearrange("p j n -> p (j n)"), ps[:, 0:4, :].rearrange("p b n -> p (b n)"), ACT.Copy).then_inc(sc_copied, 1)
                act.wait_ge(rt_vec, RTV * i + RTV - 4)
                act.activation(cv[:], cv[:], ACT.Exp).then_inc(rt_exp, 1)
                act.wait_ge(g_out, 16 * i)
                with act.Fori(0, P // 16) as j:
                    for b in range(4):
                        act.wait_ge(g_mm, 16 * (8 * i + j) + 4 * b + 4)
                        act.activation(Gsb[:, :, bass.ds(16 * j + 4 * b, 4)].rearrange("p e t -> p t e"),
                                       ps[:, 4 + b, :].rearrange("p (t e) -> p t e", t=4), ACT.Copy).then_inc(g_copied, 1)

            act.wait_ge(g_copied, 32 * TILES)
            for c in range(DC):
                act.activation(h2hi[:, c], hT[:, c], ACT.Copy).then_inc(h2_hi, 1)

            def u_high(g, s, first=False):
                act.wait_ge(ust_in[s], 16 * g + 16)
                if not first:
                    act.wait_ge(u_mm, 2 * g + s - 1)
                act.activation(uhi[:, s].rearrange("p k m -> p (k m)"), ust[:, s].rearrange("p k m -> p (k m)"), ACT.Copy).then_inc(uhi_ready, 1)

            def gelu(g, s, first=False):
                act.wait_ge(u_mm, 2 * g + s + 1)
                if not first:
                    act.wait_ge(w_ready, 2 * g + s - 1)
                act.activation(actb[:, s], halves(ps, 2 * s), ACT.Gelu).then_inc(act_ready, 1)

            def w_high(g, s, par, first=False):
                act.wait_ge(w_ready, 2 * g + s + 1)
                if not first:
                    act.wait_ge(v_mm, 16 * (g - 1))
                act.activation(whi[:, par, s], wbuf[:, s], ACT.Copy).then_inc(whi_ready, 1)

            def v_high(g, s, first=False):
                act.wait_ge(vst_in[s], 16 * g + 16)
                if not first:
                    act.wait_ge(v_mm, 16 * g)
                act.activation(vhi[:, s], vst[:, s], ACT.Copy).then_inc(vhi_ready, 1)

            def step(g, par, first=False, second=False, last=False):
                for s in range(2):
                    gelu(g, s, first)
                    if not last:
                        u_high(g + 1, s)
                    w_high(g, s, par, first or second)
                for s in range(2):
                    v_high(g, s, first)

            act.wait_ge(q_copied, 16)
            for s in range(2):
                u_high(0, s, True)
            step(0, 0, first=True)
            step(1, 1, second=True)
            with act.Fori(1, GROUPS // 2 - 1) as i:
                for par in range(2):
                    step(2 * i + par, par)
            step(GROUPS - 2, 0)
            step(GROUPS - 1, 1, last=True)

            norm_root(2, acc, esq, erstd, x3_done)

        @block.vector
        def _(dve):
            class Chain:

                def __init__(self, first=0):
                    self.first, self.n = first, 0

                def up(self):
                    self.n += 1
                    return 1

                def now(self):
                    return self.first + self.n

            dve.wait_ge(const_in, 48)
            with dve.Fori(0, 6) as i:
                for s in range(2):
                    dve.wait_ge(ada_mm, 2 * i + s + 1)
                    dve.tensor_tensor(mod[:, bass.ds(8 * i + 4 * s, 4)], ps[:, s, 0:4], ADAB[:, bass.ds(8 * i + 4 * s, 4)],
                                      ALU.add).then_inc(ada_add, 1)
            dve.wait_ge(ada_add, 12)
            dve.scalar_tensor_tensor(amp1[:], mod[:, 8:16], 1.0, G1, ALU.add, ALU.mult).then_inc(mod_ready, 1)
            dve.scalar_tensor_tensor(amp2[:], mod[:, 32:40], 1.0, G2, ALU.add, ALU.mult).then_inc(mod_ready, 1)
            dve.wait_ge(mod_ready, 2)

            def norm_apply(n, x, rt, dst, amp, shift):
                dve.wait_ge(nrt[n], 1)
                dve.reciprocal(rt[:, 1], rt[:, 0]).then_inc(nsc[n], 1)
                dve.wait_ge(nsc[n], 1)
                for c in range(DC):
                    r = dve.scalar_tensor_tensor(dst[:, c], x[:, c], amp[:, c:c + 1], rt[:, 1], ALU.mult, ALU.mult)
                    if shift is None:
                        r.then_inc(nout[n], 1)
                        continue
                    r.then_inc(nsc[n], 1)
                    if c:
                        dve.wait_ge(nsc[n], c + 1)
                        dve.tensor_scalar(dst[:, c - 1], dst[:, c - 1], shift[:, c - 1:c], None, ALU.add).then_inc(nout[n], 1)
                if shift is not None:
                    dve.wait_ge(nsc[n], DC + 1)
                    dve.tensor_scalar(dst[:, DC - 1], dst[:, DC - 1], shift[:, DC - 1:DC], None, ALU.add).then_inc(nout[n], 1)

            norm_apply(0, xT, rstd, hT, amp1, mod[:, 0:8])

            dve.wait_ge(nout[0], DC)
            dve.memset(swk[:, 0:P], 0.0)
            dve.memset(vtok[:, 0], 0.0)
            dve.memset(pre[:, :, 0:3], 0.0).then_inc(pads_zero, 1)
            with dve.Fori(0, 4) as i:
                for s in range(3):
                    dve.wait_ge(in_copied, 3 * i + s + 1)
                    dve.wait_ge(qkv_ready, 3 * i)
                    tap = [CONV[:, bass.ds(12 * i + 4 * s + j, 1)] for j in range(4)]
                    dve.tensor_scalar(cacc[:, s], pre[:, s, 0:T], tap[0], None, ALU.mult).then_inc(conv_step, 1)
                    for j in range(1, 4):
                        dve.wait_ge(conv_step, 9 * i + 3 * s + j)
                        r = dve.scalar_tensor_tensor(cacc[:, s], pre[:, s, j:j + T], tap[j], cacc[:, s], ALU.mult, ALU.add)
                        r.then_inc(conv_step if j < 3 else conv_done, 1)
            for t in range(TILES):
                dve.wait_ge(sm_mm, t + 1)
                dve.tensor_copy(ab[:, t], ps[:, 6 + t % 2, 0:8]).then_inc(sm_copied, 1)
                dve.tensor_copy(vtok[:, 1 + t], ps[:, 6 + t % 2, 8:SMALL]).then_inc(sm_copied, 1)
            with dve.Fori(0, 4) as i:
                for s in range(2):
                    dve.wait_ge(l2_root, 2 * i + s + 1)
                    dve.reciprocal(rstd[:, s], rstd[:, s]).then_inc(l2_done, 1)
                    dve.wait_ge(l2_done, 2 * i + s + 1)
                    row = qkv[:, bass.ds(2 * i + s, 1), :].rearrange("p o t -> p (o t)")
                    dve.tensor_tensor(row, row, rstd[:, s], ALU.mult).then_inc(l2_inv, 1)

            def th(x):
                return x.rearrange("p (t h) -> p t h", h=H)
            dve.wait_ge(sm_copied, 2 * TILES)
            dve.tensor_tensor(th(adt), ab[:, :, 0:H], rows[:, 0:H].unsqueeze(1).to_broadcast([P, TILES, H]), ALU.add).then_inc(gate_vec, 1)
            dve.wait_ge(gate_vec, 1)
            dve.wait_ge(gate_act, 4)
            dve.tensor_scalar(adt, adt, 0.0, None, ALU.max).then_inc(gate_vec, 1)
            dve.wait_ge(gate_vec, 2)
            dve.tensor_tensor(adt, adt, lns, ALU.add).then_inc(gate_vec, 1)
            dve.wait_ge(gate_vec, 3)
            dve.scalar_tensor_tensor(th(ld), th(adt), -1.0, nea[:, 0:H].unsqueeze(1).to_broadcast([P, TILES, H]),
                                     ALU.mult, ALU.mult).then_inc(gate_vec, 1)
            dve.wait_ge(gate_mm, 1)
            dve.tensor_copy(gcol, ps[:, 0, 0:32]).then_inc(gate_vec, 1)
            dve.tensor_scalar(ngcol, ps[:, 0, 0:32], -1.0, None, ALU.mult).then_inc(gate_vec, 1)
            dve.wait_ge(gate_vec, 6)
            dve.tensor_tensor(dlt, ps[:, 0, 32:64], gcol, ALU.subtract).then_inc(gate_vec, 1)
            dve.wait_ge(gate_act, 7)
            dve.tensor_tensor(beg, beta, eg, ALU.mult).then_inc(gate_vec, 1)
            dve.memset(St[:], 0.0).then_inc(gate_vec, 1)
            dve.wait_ge(gate_vec, 9)

            def flat(x):
                return x[:].rearrange("p h n -> p (h n)")

            def over_n(col, i):
                return col[:, bass.ds(H * i, H)].unsqueeze(2).to_broadcast([P, H, P])

            def over_h(m):
                return m.unsqueeze(1).to_broadcast([P, H, P])

            with dve.Fori(0, TILES) as i:
                c_, m0, a0 = Chain(DNV * i), DNM * i, DNA * i
                tok = bass.ds(i * P, P)
                dve.wait_ge(dn_mm, m0)
                dve.tensor_copy(kn[:], qkv[:, H:2 * H, tok]).then_inc(dn_vec, c_.up())
                dve.tensor_scalar(qn[:], qkv[:, 0:H, tok], float(P) ** -0.5, None, ALU.mult).then_inc(dn_vec, c_.up())
                dve.tensor_copy(vv[:], qkv[:, 2 * H:3 * H, tok]).then_inc(dn_vec, c_.up())
                dve.tensor_copy(ldb[:], over_n(ld, i)).then_inc(dn_vec, c_.up())
                dve.tensor_copy(btb[:], over_n(beta, i)).then_inc(dn_vec, c_.up())
                dve.wait_ge(dn_mm, m0 + 1)
                dve.tensor_tensor(gm[:], ps[:, 0, :].rearrange("p (h n) -> p h n", h=H), over_h(neg), ALU.add).then_inc(dn_vec, c_.up())
                dve.wait_ge(dn_mm, m0 + 6)
                dve.wait_ge(dn_act, a0 + 5)
                bank = [ps[:, b, :].rearrange("p (h n) -> p h n", h=H) for b in range(8)]
                dve.tensor_tensor(LT[:], bank[2], gam[:], ALU.mult).then_inc(dn_vec, c_.up())
                dve.tensor_tensor(AT[:], bank[3], gam[:], ALU.mult).then_inc(dn_vec, c_.up())
                dve.tensor_tensor(vb[:], bank[5], over_n(beta, i), ALU.mult).then_inc(dn_vec, c_.up())
                dve.tensor_tensor(kbe[:], bank[4], over_n(beg, i), ALU.mult).then_inc(dn_vec, c_.up())
                dve.tensor_tensor(kd[:], bank[4], over_n(ekd, i), ALU.mult).then_inc(dn_vec, c_.up())
                dve.tensor_tensor(qdec[:], qn[:], egrow[:], ALU.mult).then_inc(dn_vec, c_.up())
                dve.tensor_copy(X[:], over_h(ident)).then_inc(dn_vec, c_.up())
                dve.tensor_copy(XT[:], over_h(ident)).then_inc(dn_vec, c_.up())
                dve.wait_ge(dn_vec, c_.now())
                dve.tensor_tensor(LT[:], LT[:], bank[1], ALU.mult).then_inc(dn_vec, c_.up())
                dve.memset(vz[:], 0.0).then_inc(dn_vec, c_.up())
                assert c_.n == 16
                for s in range(6):
                    dve.wait_ge(dn_vec, c_.now())
                    dve.tensor_tensor(bt[:], LT[:], over_h(level[s]), ALU.mult).then_inc(dn_vec, c_.up())
                    dve.wait_ge(dn_mm, m0 + 8 + 2 * s)
                    if s < 5:
                        dve.tensor_tensor(X[:], X[:], bank[1], ALU.subtract).then_inc(dn_vec, c_.up())
                    dve.tensor_tensor(XT[:], XT[:], bank[2], ALU.subtract).then_inc(dn_vec, c_.up())
                assert c_.n == 33
                for c in range(2):
                    lo = c * CHUNK
                    dve.wait_ge(dn_mm, m0 + 20 + 2 * c)
                    dve.tensor_tensor(vz[lo:lo + CHUNK, c], u[lo:lo + CHUNK], bank[5][lo:lo + CHUNK], ALU.subtract).then_inc(dn_vec, c_.up())
                    dve.wait_ge(dn_mm, m0 + 21 + 2 * c)
                    for h in range(H):
                        dve.scalar_tensor_tensor(St[:, h], St[:, h], egrow[:, h, lo + CHUNK - 1:lo + CHUNK], bank[7][:, h],
                                                 ALU.mult, ALU.add).then_inc(dn_vec, c_.up())
                assert c_.n == DNV, c_.n

            dve.wait_ge(dn_act, DNA * TILES)
            dve.wait_ge(dn_vec, DNV * TILES)
            dve.memset(qz[:], 0.0)
            dve.tensor_copy(mbuf[:], wmask0).then_inc(gate_vec, 1)
            dve.wait_ge(gate_vec, 10)
            with dve.Fori(0, TILES) as i:
                c_, m0, a0 = Chain(SWV * i), SWM * i, SWA_ * i
                dve.wait_ge(sw_mm, m0)
                dve.wait_ge(sw_vec, SWV * i)
                for r in range(2):
                    rr = slice(r * HD, (r + 1) * HD)
                    dve.tensor_scalar(qz[rr, 4 * r:4 * r + 4], zq[rr, 4:8, bass.ds(i * P, P)], float(HD) ** -0.5, None,
                                      ALU.mult).then_inc(sw_vec, c_.up())
                dve.tensor_copy(vbuf[:].rearrange("p b n -> p (b n)"),
                                vtok[:].rearrange("p b n -> p (b n)")[:, bass.ds(i * P, 2 * P)]).then_inc(sw_vec, c_.up())
                dve.wait_ge(sw_mm, m0 + 1)
                scores = ps[:, 0:4, :].rearrange("p b (h n) -> p (b h) n", h=2)
                dve.tensor_tensor(prob[:], scores, mbuf[:].unsqueeze(1).to_broadcast([P, QH, 2 * P]), ALU.add).then_inc(sw_vec, c_.up())
                dve.wait_ge(sw_vec, c_.now())
                dve.tensor_reduce(stat[:, 0], prob[:], AX.X, ALU.max).then_inc(sw_vec, c_.up())
                dve.wait_ge(sw_vec, c_.now())
                sinks = rows[:, 8:16]
                dve.tensor_tensor(stat[:, 1], stat[:, 0], sinks, ALU.max).then_inc(sw_vec, c_.up())
                dve.wait_ge(sw_vec, c_.now())
                dve.tensor_tensor(stat[:, 2], sinks, stat[:, 1], ALU.subtract)
                dve.tensor_tensor(prob2[:], prob[:], stat[:, 1].unsqueeze(2).to_broadcast([P, QH, 2 * P]), ALU.subtract).then_inc(sw_vec, c_.up())
                dve.wait_ge(sw_act, a0 + 2)
                dve.tensor_reduce(stat[:, 4], prob[:], AX.X, ALU.add).then_inc(sw_vec, c_.up())
                dve.wait_ge(sw_vec, c_.now())
                dve.tensor_tensor(stat[:, 5], stat[:, 4], stat[:, 3], ALU.add).then_inc(sw_vec, c_.up())
                dve.wait_ge(sw_vec, c_.now())
                dve.reciprocal(stat[:, 4], stat[:, 5]).then_inc(sw_vec, c_.up())
                dve.wait_ge(sw_vec, c_.now())
                dve.tensor_tensor(prob2[:], prob[:], stat[:, 4].unsqueeze(2).to_broadcast([P, QH, 2 * P]), ALU.mult).then_inc(sw_vec, c_.up())
                dve.tensor_copy(mbuf[:], wmask).then_inc(sw_vec, c_.up())
                assert c_.n == SWV, c_.n

            for c in range(H):
                dve.wait_ge(gn_root, c + 1)
                dve.reciprocal(rstd[:, c % 2], rstd[:, c % 2]).then_inc(gn_vec, 1)
                dve.wait_ge(gn_vec, 3 * c + 1)
                dve.scalar_tensor_tensor(qkv[:, c], qkv[:, c], OGAIN, rstd[:, c % 2], ALU.mult, ALU.mult).then_inc(gn_vec, 1)
                dve.wait_ge(gn_vec, 3 * c + 2)
                dve.wait_ge(z_silu, c + 1)
                dve.tensor_tensor(qkv[:, c], qkv[:, c], zq[:, c], ALU.mult).then_inc(gn_vec, 1)

            with dve.Fori(0, DC // 2) as i:
                for s in range(2):
                    for h in range(2):
                        n = 2 * (2 * i + s) + h
                        dve.wait_ge(up_sig, 2 * n + 2)
                        for b in range(2):
                            dve.tensor_tensor(mtmp[:, h, b], sig[:, h, b], ps[:, 4 * h + 2 + b, :], ALU.mult).then_inc(up_vec, 1)
                        dve.wait_ge(up_vec, 2 * n + 2)
                        dst = merged[:, bass.ds(2 * i + s, 1), h * HALF:(h + 1) * HALF].rearrange("p o t -> p (o t)")
                        dve.tensor_tensor(dst, mtmp[:, h, 0], mtmp[:, h, 1], ALU.add).then_inc(up_done, 1)
            dve.wait_ge(up_done, 2 * DC)
            with dve.Fori(0, DC // 2) as i:
                for s in range(2):
                    dve.wait_ge(wo_mm, 2 * i + s + 1)
                    row = xT[:, bass.ds(2 * i + s, 1), :].rearrange("p o t -> p (o t)")
                    dve.scalar_tensor_tensor(row, halves(ps, 2 * s), mod[:, bass.ds(16 + 2 * i + s, 1)], row, ALU.mult, ALU.add).then_inc(x2_done, 1)
            dve.wait_ge(x2_done, DC)
            norm_apply(1, xT, rstd, hT, amp2, mod[:, 24:32])

            with dve.Fori(0, TILES) as i:
                c_ = Chain(RTV * i)

                def top16(n, vals, idx, src, tmp):
                    def each(f):
                        dve.wait_ge(rt_vec, c_.now())
                        dve.memset(carrier[:], 0.0)
                        for j in range(n):
                            r = f(j)
                        r.then_inc(rt_vec, c_.up())
                    each(lambda j: dve.max(vals[:, j, 0:8], src[:, j]))
                    each(lambda j: dve.max_index(idx[:, j, 0:8], vals[:, j, 0:8], src[:, j]))
                    each(lambda j: dve.match_replace(tmp[:, j], vals[:, j, 0:8], src[:, j], LOWEST))
                    each(lambda j: dve.max(vals[:, j, 8:16], tmp[:, j]))
                    each(lambda j: dve.max_index(idx[:, j, 8:16], vals[:, j, 8:16], tmp[:, j]))

                dve.wait_ge(g_mm, P * i)
                dve.wait_ge(sc_copied, i + 1)
                top16(16, sv, si, sc, sc2)
                dve.wait_ge(rt_vec, c_.now())
                dve.tensor_copy(sif[:], si[:]).then_inc(rt_vec, c_.up())
                sv4 = sv[:].rearrange("p (h two) k -> p h two k", two=2)
                shape = [P, PH, TOPK, TOPK]
                cand = sc[:].rearrange("p (h two) n -> p h (two n)", two=2)
                cand2 = sc2[:].rearrange("p (h two) n -> p h (two n)", two=2)
                dve.tensor_tensor(cand.rearrange("p h (a b) -> p h a b", b=TOPK), sv4[:, :, 0, :].unsqueeze(3).to_broadcast(shape),
                                  sv4[:, :, 1, :].unsqueeze(2).to_broadcast(shape), ALU.add).then_inc(rt_vec, c_.up())
                top16(PH, cv, ci, cand, cand2)
                dve.wait_ge(rt_vec, c_.now())
                flat_ci = ci[:].rearrange("p h k -> p (h k)")
                dve.tensor_scalar(cab[:, 0], flat_ci, 4, None, ALU.logical_shift_right)
                dve.tensor_scalar(cab[:, 1], flat_ci, 15, None, ALU.bitwise_and).then_inc(rt_vec, c_.up())
                dve.wait_ge(rt_vec, c_.now())
                dve.tensor_copy(cabf[:], cab[:]).then_inc(rt_vec, c_.up())
                sif4 = sif[:].rearrange("p (h two) k -> p h two k", two=2)
                eq = qbuf[:].rearrange("p j n -> p (j n)").rearrange("p (h k a) -> p h k a", h=PH, k=TOPK)
                for r in range(2):
                    dve.wait_ge(rt_vec, c_.now())
                    dve.tensor_tensor(eq, cabf[:, r].rearrange("p (h k) -> p h k", h=PH).unsqueeze(3).to_broadcast(shape),
                                      iota[:, 0:TOPK].unsqueeze(1).unsqueeze(1).to_broadcast(shape), ALU.is_equal).then_inc(rt_vec, c_.up())
                    dve.wait_ge(rt_vec, c_.now())
                    dve.tensor_tensor(eq, eq, sif4[:, :, r, :].unsqueeze(2).to_broadcast(shape), ALU.mult).then_inc(rt_vec, c_.up())
                    dve.wait_ge(rt_vec, c_.now())
                    dve.tensor_reduce(pick[:, r].rearrange("p (h k) -> p h k", h=PH), eq, AX.X, ALU.add).then_inc(rt_vec, c_.up())
                dve.tensor_copy(gsum[:, 0], cv[:, :, 0]).then_inc(rt_vec, c_.up())
                dve.wait_ge(rt_vec, c_.now())
                top = gsum[:, 0].unsqueeze(2).to_broadcast([P, PH, TOPK])
                dve.tensor_tensor(cv[:], cv[:], top, ALU.subtract).then_inc(rt_vec, c_.up())
                assert c_.n == RTV - 4, c_.n
                dve.wait_ge(rt_exp, i + 1)
                dve.tensor_reduce(gsum[:, 1], cv[:], AX.X, ALU.add).then_inc(rt_vec, c_.up())
                dve.wait_ge(rt_vec, c_.now())
                dve.reciprocal(gsum[:, 0], gsum[:, 1]).then_inc(rt_vec, c_.up())
                dve.wait_ge(rt_vec, c_.now())
                dve.tensor_tensor(pick[:, 2].rearrange("p (h k) -> p h k", h=PH), cv[:],
                                  gsum[:, 0].unsqueeze(2).to_broadcast([P, PH, TOPK]), ALU.mult).then_inc(rt_vec, c_.up())
                dve.wait_ge(rt_mm, i + 1)
                dve.tensor_copy(rT[:].rearrange("p r n -> p (r n)"), ps[:, 0, 0:3 * P]).then_inc(rt_vec, c_.up())
                assert c_.n == RTV, c_.n
                dve.wait_ge(rt_vec, c_.now())
                dve.memset(carrier[:], 0.0)
                with dve.Fori(0, P // 16) as j:
                    n0 = 16 * (8 * i + j)
                    for t in range(16):
                        col = [rT[:, r, bass.ds(16 * j + t, 1)] for r in range(3)]
                        if t < 8:
                            if t == 0:
                                dve.wait_ge(g_mm, n0)
                        else:
                            dve.wait_ge(g_mm, n0 + t - 7)
                        dve.tensor_scalar(oneL[:, t % 8], iota, col[0], None, ALU.is_equal)
                        dve.tensor_scalar(oneR[:, t % 8], iota, col[1], col[2], ALU.is_equal, ALU.mult).then_inc(one_ready, 1)

            for c in range(DC):
                dve.wait_ge(h2_hi, c + 1)
                dve.tensor_tensor(h2lo[:, c], hT[:, c], h2hi[:, c].bitcast(F32), ALU.subtract).then_inc(h2_lo, 1)

            def fl(x):
                return x.rearrange("p k m -> p (k m)")

            def u_low(g, s):
                dve.wait_ge(uhi_ready, 2 * g + s + 1)
                dve.tensor_tensor(fl(ulo[:, s]), fl(ust[:, s]), fl(uhi[:, s]).bitcast(F32), ALU.subtract).then_inc(u_ready, 1)

            def v_low(g, s):
                dve.wait_ge(vhi_ready, 2 * g + s + 1)
                dve.tensor_tensor(vlo[:, s], vst[:, s], vhi[:, s].bitcast(F32), ALU.subtract).then_inc(v_ready, 1)

            def weigh(g, s, first=False):
                dve.wait_ge(act_ready, 2 * g + s + 1)
                dve.wait_ge(gst_in[s], 16 * g + 16)
                if not first:
                    dve.wait_ge(wlo_ready, 2 * g + s - 1)
                dve.tensor_tensor(wbuf[:, s], gst[:, s], actb[:, s], ALU.mult).then_inc(w_ready, 1)

            def w_low(g, s, par):
                dve.wait_ge(whi_ready, 2 * g + s + 1)
                dve.tensor_tensor(wlo[:, par, s], wbuf[:, s], whi[:, par, s].bitcast(F32), ALU.subtract).then_inc(wlo_ready, 1)

            def flush(g):
                for b in range(16):
                    dve.wait_ge(v_mm, 16 * g + b + 1)
                    o = acc[:, b // 2, (b % 2) * HALF:(b % 2 + 1) * HALF]
                    dve.tensor_tensor(o, o, ps[:, 4 + b % 4, :], ALU.add).then_inc(flushed, 1)

            def step(g, par, first=False, last=False):
                for s in range(2):
                    weigh(g, s, first)
                    if not last:
                        u_low(g + 1, s)
                    w_low(g, s, par)
                if not first:
                    flush(g - 1)
                for s in range(2):
                    v_low(g, s)

            for s in range(2):
                u_low(0, s)
            step(0, 0, first=True)
            dve.wait_ge(acc_zero, 1)
            step(1, 1)
            with dve.Fori(1, GROUPS // 2 - 1) as i:
                for par in range(2):
                    step(2 * i + par, par)
            step(GROUPS - 2, 0)
            step(GROUPS - 1, 1, last=True)
            flush(GROUPS - 1)

            dve.wait_ge(flushed, 16 * GROUPS)
            dve.wait_ge(x2_in, 16)
            for c in range(DC):
                dve.scalar_tensor_tensor(acc[:, c], acc[:, c], mod[:, 40 + c:41 + c], x2[:, c], ALU.mult, ALU.add).then_inc(x3_done, 1)
            dve.wait_ge(x3_done, DC)
            norm_apply(2, acc, erstd, oT, GF, None)


def constants():
    i = np.arange(P)
    f = np.float32
    keep = np.concatenate([np.eye(P), np.tile(i, (P, 1)), np.ones((P, P))], 1).astype(f)
    same = (i[:, None] // CHUNK) == (i[None, :] // CHUNK)
    tri = same & (i[:, None] <= i[None, :])
    parts = [tri, same, np.where(tri, 0.0, -BIG)]
    for s in range(6):
        w = 1 << s
        parts.append(((i[:, None] // (2 * w)) == (i[None, :] // (2 * w))) & ((i[:, None] // w) % 2 == 0) & ((i[None, :] // w) % 2 == 1))
    j = np.arange(2 * P)
    own = i[:, None] // CHUNK + 2
    kc = j[None, :] // CHUNK
    ok = (kc == own) | (kc == own - 1)
    parts.append(np.where(ok, 0.0, -BIG))
    parts.append(np.where(ok & (j[None, :] >= P), 0.0, -BIG))
    return keep, np.concatenate([np.asarray(x, f) for x in parts], 1)


def lay_out(x, c, ada_w, ada_b, norm1_gain, w_in, conv_w, dn_a_log, dn_dt_bias, dn_out_gain, swa_sinks, w_dn_up,
            w_swa_up, w_out, norm2_gain, peer_w_q, peer_sub_keys, peer_u, peer_v, final_gain):
    keep, masks = constants()

    def col(v):
        return v.reshape(-1, P).T

    def blocks(w):
        k, n = w.shape
        return w.reshape(k // P, P, n // P, P).transpose(2, 1, 0, 3)

    w = w_in[0]
    q0 = 1536 + 8 + 512
    heads = [slice(q0 + h * HD, q0 + (h + 1) * HD) for g in range(4) for h in (g, g + 4)]
    k0 = q0 + 512
    g0 = k0 + 256
    front = np.concatenate([w[:, 0:1536], w[:, 1544:1544 + 512]] + [w[:, s] for s in heads] + [w[:, k0:k0 + P]], 1)
    small = np.concatenate([w[:, 1536:1544], w[:, k0 + P:k0 + 2 * P]], 1)
    up_rows = np.concatenate([w_swa_up[0][h * HD:(h + 1) * HD] for g in range(4) for h in (g, g + 4)], 0)
    up = np.concatenate([blocks(w[:, g0:g0 + D]), blocks(w[:, g0 + D:g0 + 2 * D]), blocks(w_dn_up[0]), blocks(up_rows)], 2)
    conv = conv_w[0].reshape(12, P, 4).transpose(1, 0, 2).reshape(P, 48)
    row = np.broadcast_to(np.concatenate([dn_dt_bias[0], dn_a_log[0], swa_sinks[0]])[None, :], (P, 16))
    cols = np.concatenate([col(c[0]), col(ada_b[0]), col(norm1_gain[0]), col(norm2_gain[0]), col(final_gain), conv,
                           dn_out_gain[0].reshape(P, 1), row], 1)
    return {
        "c_keep": keep, "c_masks": masks, "p_cols": cols,
        "xT": x[0].T, "ada_w": ada_w[0],
        "w_in": blocks(front), "w_small": small.reshape(DC, P, SMALL).transpose(1, 0, 2),
        "w_up": up, "w_out": blocks(w_out[0]), "w_q": blocks(peer_w_q[0]),
        "sub_k": peer_sub_keys[0].reshape(16, NK, P).transpose(2, 0, 1),
        "u": peer_u[0].reshape(NK, NK, DC, P).transpose(1, 3, 2, 0),
        "v": peer_v[0].reshape(NK, NK, D).transpose(1, 0, 2),
    }


def kernel(**inputs):
    import concourse.bacc as _bacc
    from concourse.bass_utils import run_bass_kernel_spmd as _run

    data = {k: np.ascontiguousarray(v) for k, v in lay_out(**{k: np.asarray(v) for k, v in inputs.items()}).items()}
    nc = _bacc.Bacc("TRN2", target_bir_lowering=False, num_devices=1)
    arrays, args = {}, {}
    for name, v in data.items():
        arrays[f"in_{name}"] = v
        args[name] = nc.dram_tensor(f"in_{name}", list(v.shape), mybir.dt.from_np(v.dtype), kind="ExternalInput").ap()
    out = nc.dram_tensor("out_T", [D, T], F32, kind="ExternalOutput").ap()
    block_kernel(nc, args, out)
    r = _run(nc, [arrays], core_ids=[0])
    return np.ascontiguousarray(r.results[0]["out_T"].T).reshape(1, T, D)
```

```python
from contextlib import ExitStack

import numpy as np
import concourse.bass as bass
from concourse import mybir

P = 128
D = 1024
T = 1024
HALF = 512
DC = D // P
TILES = T // P
CHUNK = 64
EPS = 1e-6
H = 4
QH = 8
HD = 64
IN_JOBS = 21
SMALL = 8 + P
PH = 8
NK = 128
TOPK = 16
GROUP = 2
GROUPS = NK // GROUP
EARLY = 32
PER_TILE = EARLY // TILES
LEAD = EARLY // GROUP
FULL = GROUPS - LEAD
ADA_SLABS = 12
ADA_FIRST = 4
BIG = 1.0e30
LOWEST = -3.0e38

F32 = mybir.dt.float32
F32R = mybir.dt.float32r
U32 = mybir.dt.uint32
ALU = mybir.AluOpType
ACT = mybir.ActivationFunctionType
AX = mybir.AxisListType

CONSTS = ["c_keep", "c_masks"]
PARAMS = ["p_cols", "p_rows"]


def block_kernel(nc, a, out):
    KB = 1024
    base = 16512
    limit = 229368

    def at(name, shape, kb, dtype=F32):
        size = 4 * int(np.prod(shape[1:]))
        off = base + int(kb * KB)
        assert off + size <= limit, (name, off + size - limit)
        return nc.alloc_sbuf_tensor_at(name, list(shape), dtype, offset=off)

    ctx = ExitStack()
    with ctx:
        def sem(name):
            return ctx.enter_context(nc.semaphore(name))

        ps = ctx.enter_context(nc.psum_tensor("ps", [P, 8, 512], F32))

        keep = at("keep", [P, 3 * P], 0)
        ident, iota, ones = keep[:, 0:P], keep[:, P:2 * P], keep[:, 2 * P:3 * P]
        cols = at("cols", [P, 145], 1.5)
        C_, ADAB, G1, G2, GF, CONV, OGAIN = (cols[:, 0:8], cols[:, 8:56], cols[:, 56:64], cols[:, 64:72],
                                             cols[:, 72:80], cols[:, 80:128], cols[:, 128:129])
        rows = cols[:, 129:145]
        mod = at("mod", [P, 48], 2.25)
        silc = at("silc", [P, 8], 2.5)
        amp1 = at("amp1", [P, 8], 2.5625)
        amp2 = at("amp2", [P, 8], 2.625)
        O = 4

        xT = at("xT", [P, DC, T], O + 0)
        hT = at("hT", [P, DC, T], O + 32)
        qkv = at("qkv", [P, 12, T], O + 64)
        zq = at("zq", [P, 8, T], O + 112)
        swk = at("swk", [P, P + T], O + 144)
        vtok = at("vtok", [P, 1 + TILES, P], O + 148.5)
        masks = at("masks", [P, 4 * P + 6 * P + 4 * P], O + 153)
        tri, blk, neg = masks[:, 0:P], masks[:, P:2 * P], masks[:, 2 * P:3 * P]
        level = [masks[:, (3 + s) * P:(4 + s) * P] for s in range(6)]
        wmask = masks[:, 9 * P:11 * P]
        wmask0 = masks[:, 11 * P:13 * P]
        slab = [at("slab_a", [P, 2, DC, 512], O + 64), at("slab_b", [P, 2, DC, 512], O + 0)]
        arow = at("arow", [P, 2, 512], O + 189)
        wjob = at("wjob", [P, 3, DC, P], O + 161)
        sq = at("sq", [P, 2, T], O + 173)
        rstd = at("rstd", [P, 2, T], O + 181)
        pre = at("pre", [P, 3, 3 + T], O + 173)
        cacc = at("cacc", [P, 3, T], O + 185.25)
        wsmall = at("wsmall", [P, DC, SMALL], O + 197.25)
        ab = at("ab", [P, TILES, 8], O + 203)

        def dn(name, k, shape=(P, H, P)):
            return at(name, shape, O + 161 + 2 * k)
        ldb, btb, kn, qn, vv, gm, gam = [dn(n, k) for k, n in enumerate(["ldb", "btb", "kn", "qn", "vv", "gm", "gam"])]
        egrow, qdec, LT, AT, X, XT, t1 = [dn(n, 7 + k) for k, n in enumerate(["egrow", "qdec", "LT", "AT", "X", "XT", "t1"])]
        vb, kbe, kd, u, wT, St = [dn(n, 14 + k) for k, n in enumerate(["vb", "kbe", "kd", "u", "wT", "St"])]
        bt = gm
        vz = at("vz", [P, 2, H, P], O + 161 + 2 * 0)
        small = at("small", [P, 12, 32], O + 201.5)
        (adt, aab, lns, ld, beta, gcol, ngcol, dlt, eg, ekd, beg, nea) = [small[:, k, :] for k in range(12)]

        qz = at("qz", [P, QH, P], O + 161)
        vbuf = at("vbuf", [P, 2, P], O + 165)
        mbuf = at("mbuf", [P, 2 * P], O + 166)
        prob = at("prob", [P, QH, 2 * P], O + 167)
        probT = at("probT", [P, QH, 2, P], O + 175)
        prob2 = at("prob2", [P, QH, 2 * P], O + 183)
        stat = at("stat", [P, 6, QH], O + 191)

        wup = at("wup", [P, 2, 24, P], O + 161)
        sig = at("sig", [P, 2, 2, HALF], O + 185)
        mtmp = at("mtmp", [P, 2, 2, HALF], O + 193)
        merged = at("merged", [P, DC, T], O + 80)

        qs_hi = at("qs_hi", [P, 2, DC, P], O + 128, F32R)
        qs_lo = at("qs_lo", [P, 2, DC, P], O + 136, F32R)
        qj = at("qj", [P, 2, T], O + 144)
        sj = at("sj", [P, 2, TILES, P], O + 152)
        subk = at("subk", [P, 16, P], O + 192)

        sc = at("sc", [P, 16, P], O + 0)
        sc2 = at("sc2", [P, 16, P], O + 8)
        eqa = at("eqa", [P, PH, TOPK, TOPK], O + 16)
        oneL = at("oneL", [P, 8, P], O + 24)
        oneR = at("oneR", [P, 8, P], O + 28)
        Gsb = at("Gsb", [P, NK, P], O + 128)
        sv = at("sv", [P, 16, TOPK], O + 192)
        si = at("si", [P, 16, TOPK], O + 193, U32)
        sif = at("sif", [P, 16, TOPK], O + 194)
        cv = at("cv", [P, PH, TOPK], O + 195)
        ci = at("ci", [P, PH, TOPK], O + 195.5, U32)
        cab = at("cab", [P, 2, PH * TOPK], O + 196, U32)
        cabf = at("cabf", [P, 2, PH * TOPK], O + 197)
        pick = at("pick", [P, 3, PH * TOPK], O + 198)
        rT = at("rT", [P, 3, P], O + 199.5)
        gsum = at("gsum", [P, 2, PH], O + 201)
        carrier = at("carrier", [P, 2], O + 202)

        acc = at("acc", [P, DC, T], O + 0)
        ust = at("ust", [P, 2, DC, P], O + 32)
        uhi = at("uhi", [P, 2, DC, P], O + 40, F32R)
        ulo = at("ulo", [P, 2, DC, P], O + 48, F32R)
        actb = at("actb", [P, 2, T], O + 56)
        h2hi = at("h2hi", [P, DC, T], O + 64, F32R)
        h2lo = at("h2lo", [P, DC, T], O + 96, F32R)
        vst = at("vst", [P, 2, D], O + 128)
        gst = at("gst", [P, 2, T], O + 136)
        vhi = at("vhi", [P, 2, D], O + 144, F32R)
        vlo = at("vlo", [P, 2, D], O + 152, F32R)
        whi = at("whi", [P, 2, 2, T], O + 160, F32R)
        wlo = at("wlo", [P, 2, 2, T], O + 176, F32R)
        wbuf = at("wbuf", [P, 2, T], O + 192)

        x2 = at("x2", [P, DC, T], O + 64)
        oT = at("oT", [P, DC, T], O + 96)
        esq = at("esq", [P, 2, T], O + 128)
        erstd = at("erstd", [P, 2, T], O + 136)

        x2_dram = nc.dram_tensor("x2_scratch", [D, T], F32, kind="Internal").ap()
        s_dram = nc.dram_tensor("score_scratch", [TILES, P, 16, NK], F32, kind="Internal").ap()
        a_dram = nc.dram_tensor("act_scratch", [EARLY, P, T], F32, kind="Internal").ap()
        g_dram = nc.dram_tensor("gate_scratch", [NK, NK, T], F32, kind="Internal").ap()

        const_in, x_in, small_in, subk_in = sem("const_in"), sem("x_in"), sem("small_in"), sem("subk_in")
        slab_in = [sem(f"slab_in{s}") for s in range(2)]
        score_in, x_back = sem("score_in"), sem("x_back")
        score_out = [sem(f"score_out{s}") for s in range(2)]
        act_out = [sem(f"act_out{s}") for s in range(2)]
        act_in = [sem(f"act_in{s}") for s in range(2)]
        wjob_in = [sem(f"wjob_in{s}") for s in range(3)]
        wup_in = [sem(f"wup_in{s}") for s in range(2)]
        wout_in = [sem(f"wout_in{s}") for s in range(2)]
        wq_in = [sem(f"wq_in{s}") for s in range(2)]
        ust_in = [sem(f"ust_in{s}") for s in range(2)]
        vst_in = [sem(f"vst_in{s}") for s in range(2)]
        gst_in = [sem(f"gst_in{s}") for s in range(2)]
        x2_out, x2_in, g_out, y_out = sem("x2_out"), sem("x2_in"), sem("g_out"), sem("y_out")
        silc_ready, ada_mm, ada_row, ada_col, ada_add, mod_ready = (sem("silc_ready"), sem("ada_mm"), sem("ada_row"),
                                                                    sem("ada_col"), sem("ada_add"), sem("mod_ready"))
        nsq = [sem(f"norm{k}_squared") for k in range(3)]
        nmm = [sem(f"norm{k}_summed") for k in range(3)]
        nrt = [sem(f"norm{k}_root") for k in range(3)]
        nsc = [sem(f"norm{k}_scaled") for k in range(3)]
        nout = [sem(f"norm{k}_out") for k in range(3)]
        in_mm, in_copied, conv_step, conv_done, qkv_ready = (sem("in_mm"), sem("in_copied"), sem("conv_step"),
                                                             sem("conv_done"), sem("qkv_ready"))
        pads_zero, sm_mm, sm_copied = sem("pads_zero"), sem("sm_mm"), sem("sm_copied")
        l2_sq, l2_mm, l2_root, l2_inv, l2_done = sem("l2_sq"), sem("l2_mm"), sem("l2_root"), sem("l2_inv"), sem("l2_done")
        gate_vec, gate_act, gate_mm = sem("gate_vec"), sem("gate_act"), sem("gate_mm")
        dn_vec, dn_act, dn_mm = sem("dn_vec"), sem("dn_act"), sem("dn_mm")
        sw_vec, sw_act, sw_mm = sem("sw_vec"), sem("sw_act"), sem("sw_mm")
        gn_sq, gn_mm, gn_root, gn_vec, z_silu = sem("gn_sq"), sem("gn_mm"), sem("gn_root"), sem("gn_vec"), sem("z_silu")
        up_mm, up_sig, up_vec, up_done = sem("up_mm"), sem("up_sig"), sem("up_vec"), sem("up_done")
        wo_mm, x2_done = sem("wo_mm"), sem("x2_done")
        q_hi, q_lo, q_mm, q_copied, s_mm, s_copied = (sem("q_hi"), sem("q_lo"), sem("q_mm"), sem("q_copied"),
                                                      sem("s_mm"), sem("s_copied"))
        rt_vec, rt_pool, rt_exp, rt_mm = sem("rt_vec"), sem("rt_pool"), sem("rt_exp"), sem("rt_mm")
        left_ready, right_ready, g_mm, g_copied = sem("left_ready"), sem("right_ready"), sem("g_mm"), sem("g_copied")
        h2_hi, h2_lo, acc_zero = sem("h2_hi"), sem("h2_lo"), sem("acc_zero")
        uhi_ready, u_ready, u_mm, act_ready, w_ready, whi_ready, wlo_ready = (
            sem("uhi_ready"), sem("u_ready"), sem("u_mm"), sem("act_ready"), sem("w_ready"), sem("whi_ready"), sem("wlo_ready"))
        vhi_ready, v_ready, v_mm, flushed = sem("vhi_ready"), sem("v_ready"), sem("v_mm"), sem("flushed")
        x3_done = sem("x3_done")

        block = ctx.enter_context(nc.Block())

        DNV, DNA, DNM = 43, 15, 23
        SWV, SWA_, SWM = 12, 5, 3
        RTV = 25
        G_PER_TILE = P

        def halves(ap3, bank):
            return ps[:, bank:bank + 2, :].rearrange("p b n -> p (b n)")

        @block.sync
        def _(sp):
            sp.dma_start(keep[:], a["c_keep"]).then_inc(const_in, 16)
            sp.dma_start(cols[:], a["p_cols"]).then_inc(const_in, 16)
            sp.dma_start(masks[:, 0:13 * P], a["c_masks"]).then_inc(const_in, 16)
            sp.dma_start(xT[:], a["xT"].rearrange("(c p) t -> p c t", p=P)).then_inc(x_in, 16)
            ada = a["ada_w"].rearrange("(k p) n -> p k n", p=P)

            def load_slab(n):
                if n >= 2:
                    sp.wait_ge(ada_mm, n - 1)
                sp.dma_start(slab[n >= ADA_FIRST][:, n % 2], ada[:, :, n * 512:(n + 1) * 512]).then_inc(slab_in[n % 2], 16)
            for n in range(ADA_FIRST):
                load_slab(n)
            sp.dma_start(wsmall[:], a["w_small"]).then_inc(small_in, 16)
            with sp.Fori(0, IN_JOBS // 3) as i:
                for s in range(3):
                    sp.wait_ge(in_mm, 1 + 3 * i)
                    sp.dma_start(wjob[:, s], a["w_in"][bass.ds(3 * i + s, 1)].rearrange("o p k m -> p (o k) m")).then_inc(wjob_in[s], 16)
            sp.wait_ge(nout[0], DC)
            for n in range(ADA_FIRST, ADA_SLABS):
                load_slab(n)
            sp.wait_ge(ada_mm, ADA_SLABS)
            sp.dma_start(xT[:], a["xT"].rearrange("(c p) t -> p c t", p=P)).then_inc(x_back, 16)
            sp.wait_ge(gn_vec, 2 * H)
            with sp.Fori(0, DC // 2) as i:
                for s in range(2):
                    sp.wait_ge(up_mm, 1 + 4 * i)
                    sp.dma_start(wup[:, s], a["w_up"][bass.ds(2 * i + s, 1)].rearrange("o p k m -> p (o k) m")).then_inc(wup_in[s], 16)
            sp.wait_ge(up_mm, 1 + 2 * DC)
            with sp.Fori(0, DC // 2) as i:
                for s in range(2):
                    sp.wait_ge(wo_mm, 1 + 2 * i)
                    sp.dma_start(wjob[:, s], a["w_out"][bass.ds(2 * i + s, 1)].rearrange("o p k m -> p (o k) m")).then_inc(wout_in[s], 16)
            sp.wait_ge(x2_done, 1 + DC)
            sp.dma_start(subk[:], a["sub_k"]).then_inc(subk_in, 16)
            sp.dma_start(x2_dram.rearrange("(c p) t -> p c t", p=P), xT[:]).then_inc(x2_out, 16)
            def load_q(i, s):
                sp.dma_start(wjob[:, s], a["w_q"][bass.ds(2 * i + s, 1)].rearrange("o p k m -> p (o k) m")).then_inc(wq_in[s], 16)

            def store_scores(i):
                for s in range(2):
                    sp.wait_ge(s_copied, 1 + 2 * i + s + 1)
                    sp.dma_start(s_dram[:, :, bass.ds(2 * i + s, 1), :].rearrange("t p o n -> p t (o n)"), sj[:, s]).then_inc(score_out[s], 16)
            for s in range(2):
                load_q(0, s)
            with sp.Fori(0, 7) as i:
                for s in range(2):
                    sp.wait_ge(q_lo, 2 * i + s + 1)
                    load_q(i + 1, s)
                store_scores(i)
            store_scores(7)
            sp.wait_ge(x2_out, 16)
            for s in range(2):
                sp.wait_ge(score_out[s], 16 + 16 * 8)

            def load_u(n, s, first=False):
                if not first:
                    sp.wait_ge(uhi_ready, n - 1)
                    sp.wait_ge(u_ready, n - 1)
                sp.dma_start(ust[:, s], a["u"][bass.ds(n, 1)].rearrange("o p k m -> p (o k) m")).then_inc(ust_in[s], 16)

            def load_gate(j, g, s, first=False):
                if not first:
                    sp.wait_ge(w_ready, 2 * j + s - 1)
                sp.dma_start(gst[:, s], g_dram[bass.ds(2 * g + s, 1)].rearrange("o i t -> (o i) t")).then_inc(gst_in[s], 16)

            def load_v(j, g, s, first=False):
                if not first:
                    sp.wait_ge(vhi_ready, 2 * j + s - 1)
                    sp.wait_ge(v_ready, 2 * j + s - 1)
                sp.dma_start(vst[:, s], a["v"][bass.ds(2 * g + s, 1)].rearrange("o p n -> (o p) n")).then_inc(vst_in[s], 16)

            sp.wait_ge(h2_lo, DC)
            load_u(0, 0, True)
            load_u(1, 1, True)
            sp.dma_start(sc[:], s_dram[0]).then_inc(score_in, 16)
            with sp.Fori(0, TILES) as i:
                for k in range(PER_TILE):
                    n, s = PER_TILE * i + k, k % 2
                    load_u(n + 2, s)
                    sp.wait_ge(act_ready, n + 3)
                    sp.dma_start(a_dram[bass.ds(n, 1)].rearrange("o p t -> (o p) t"), actb[:, s]).then_inc(act_out[s], 16)
                sp.wait_ge(rt_vec, 1 + RTV * i + 12)
                sp.dma_start(sc[:], s_dram[bass.ds((i + 1) % TILES, 1)].rearrange("o p j n -> (o p) j n")).then_inc(score_in, 16)
            sp.wait_ge(score_in, 16 * (TILES + 1))
            for s in range(2):
                sp.wait_ge(act_out[s], 16 + 16 * EARLY // 2)
            sp.wait_ge(g_out, 16 + 16 * TILES)
            for s in range(2):
                load_gate(0, LEAD, s, True)
            for s in range(2):
                load_v(0, LEAD, s, True)
            with sp.Fori(1, FULL) as j:
                for s in range(2):
                    load_u(2 * (LEAD + j) + s, s)
                    load_gate(j, LEAD + j, s)
                for s in range(2):
                    load_v(j, LEAD + j, s)
            with sp.Fori(FULL, GROUPS) as j:
                for s in range(2):
                    sp.wait_ge(w_ready, 2 * j + s - 1)
                    sp.dma_start(actb[:, s], a_dram[bass.ds(2 * (j - FULL) + s, 1)].rearrange("o p t -> (o p) t")).then_inc(act_in[s], 16)
                    load_gate(j, j - FULL, s)
                for s in range(2):
                    load_v(j, j - FULL, s)
            sp.wait_ge(v_mm, 16 * GROUPS)
            sp.dma_start(x2[:], x2_dram.rearrange("(c p) t -> p c t", p=P)).then_inc(x2_in, 16)
            sp.wait_ge(nout[2], DC)
            sp.dma_start(out.rearrange("(c p) t -> p c t", p=P), oT[:]).then_inc(y_out, 16)
            sp.wait_ge(y_out, 16)

        @block.gpsimd
        def _(pool):
            for q in (in_mm, up_mm, wo_mm, q_mm, in_copied, l2_root, l2_done, dn_act, dn_vec, sw_act, sw_mm, sw_vec, up_done, x2_done, q_copied, rt_vec, conv_done, qkv_ready, l2_mm, l2_inv, dn_mm, s_copied, s_mm):
                pool.nop().then_inc(q, 1)
            for q in (g_out, *act_out, *score_out):
                pool.nop().then_inc(q, 16)
            with pool.Fori(0, TILES) as i:
                shape = [P, PH, TOPK, TOPK]
                pool.wait_ge(rt_vec, 1 + RTV * i + 17)
                sif4 = sif[:].rearrange("p (h two) k -> p h two k", two=2)
                pool.tensor_tensor(eqa[:], eqa[:], sif4[:, :, 0, :].unsqueeze(2).to_broadcast(shape), ALU.mult).then_inc(rt_pool, 1)
            pool.wait_ge(g_mm, 8 + T)
            pool.wait_ge(score_in, 16 * (TILES + 1))
            pool.memset(acc[:], 0.0).then_inc(acc_zero, 1)

        @block.tensor
        def _(pe):
            pe.nop().then_inc(g_mm, 8)

            def ada_slab(n, bank):
                pe.wait_ge(slab_in[n % 2], 16 * (n // 2) + 16)
                if n >= 2:
                    pe.wait_ge(ada_row, n - 1)
                for k in range(DC):
                    mm = pe.matmul(ps[0:1, bank + n % 2, :], silc[:, k:k + 1], slab[n >= ADA_FIRST][:, n % 2, k, :],
                                   start=(k == 0), stop=(k == DC - 1))
                mm.then_inc(ada_mm, 1)

            def ada_turn(n, bank):
                pe.wait_ge(ada_row, n + 1)
                if n >= 2:
                    pe.wait_ge(ada_add, n - 1)
                for m in range(4):
                    mm = pe.matmul(ps[:, bank + n % 2, m:m + 1], arow[0:1, n % 2, m * P:(m + 1) * P], ones[0:1, 0:1],
                                   start=True, stop=True)
                mm.then_inc(ada_col, 1)

            def ada(n0, n1, bank_a, bank_b):
                for n in range(n0, n1):
                    ada_slab(n, bank_a)
                    if n > n0:
                        ada_turn(n - 1, bank_b)
                ada_turn(n1 - 1, bank_b)

            def norm_sum(n, src):
                for c in range(DC):
                    pe.wait_ge(nsq[n], c + 1)
                    for h in range(2):
                        mm = pe.matmul(ps[:, 6 + h, :], ones, src[:, c % 2, h * HALF:(h + 1) * HALF],
                                       start=(c == 0), stop=(c == DC - 1))
                    mm.then_inc(nmm[n], 1)

            norm_sum(0, sq)
            pe.wait_ge(silc_ready, 1)
            ada(0, ADA_FIRST, 0, 2)

            pe.wait_ge(nout[0], DC)
            with pe.Fori(0, IN_JOBS // 3) as i:
                for s in range(3):
                    pe.wait_ge(wjob_in[s], 16 * i + 16)
                    pe.wait_ge(in_copied, 1 + 3 * i)
                    for h in range(2):
                        for k in range(DC):
                            mm = pe.matmul(ps[:, 2 * s + h, :], wjob[:, s, k, :], hT[:, k, h * HALF:(h + 1) * HALF],
                                           start=(k == 0), stop=(k == DC - 1))
                    mm.then_inc(in_mm, 1)
            pe.wait_ge(small_in, 16)
            for t in range(TILES):
                if t >= 2:
                    pe.wait_ge(sm_copied, 2 * (t - 1))
                else:
                    pe.wait_ge(nrt[0], 1)
                for k in range(DC):
                    mm = pe.matmul(ps[:, 6 + t % 2, 0:SMALL], hT[:, k, t * P:(t + 1) * P], wsmall[:, k, :],
                                   start=(k == 0), stop=(k == DC - 1))
                mm.then_inc(sm_mm, 1)
            pe.wait_ge(in_copied, 1 + IN_JOBS)
            ada(ADA_FIRST, ADA_SLABS, 0, 2)
            pe.wait_ge(ada_add, ADA_SLABS)
            with pe.Fori(0, 4) as i:
                for s in range(2):
                    pe.wait_ge(l2_sq, 2 * i + s + 1)
                    pe.wait_ge(l2_root, 1 + 2 * i)
                    for h in range(2):
                        mm = pe.matmul(ps[:, 2 * s + h, :], ones, sq[:, s, h * HALF:(h + 1) * HALF], start=True, stop=True)
                    mm.then_inc(l2_mm, 1)
            pe.wait_ge(gate_vec, 4)
            pe.wait_ge(l2_root, 1 + 8)
            pe.matmul(ps[:, 0, 0:32], tri, ld, start=True, stop=True)
            pe.matmul(ps[:, 0, 32:64], blk, ld, start=True, stop=True).then_inc(gate_mm, 1)

            pe.wait_ge(gate_vec, 9)
            with pe.Fori(0, TILES) as i:
                v0, a0 = DNV * i, DNA * i

                def heads(bank, f, width=P):
                    for h in range(H):
                        m = f(h, ps[:, bank, h * width:(h + 1) * width])
                    return m
                pe.wait_ge(dn_act, 1 + a0)
                pe.wait_ge(dn_vec, 1 + v0 + 5)
                heads(0, lambda h, o: pe.matmul(o, ldb[:, h], tri, start=True, stop=True)).then_inc(dn_mm, 1)
                heads(1, lambda h, o: pe.matmul(o, btb[:, h], ident, start=True, stop=True)).then_inc(dn_mm, 1)
                heads(2, lambda h, o: pe.matmul(o, kn[:, h], kn[:, h], start=True, stop=True)).then_inc(dn_mm, 1)
                heads(3, lambda h, o: pe.matmul(o, kn[:, h], qn[:, h], start=True, stop=True)).then_inc(dn_mm, 1)
                heads(4, lambda h, o: pe.transpose(o, kn[:, h], ident)).then_inc(dn_mm, 1)
                heads(5, lambda h, o: pe.transpose(o, vv[:, h], ident)).then_inc(dn_mm, 1)
                for s in range(6):
                    pe.wait_ge(dn_vec, 1 + v0 + 17 + 3 * s)
                    heads(0, lambda h, o: pe.matmul(o, bt[:, h], X[:, h], start=True, stop=True)).then_inc(dn_mm, 1)
                    pe.wait_ge(dn_act, 1 + a0 + 6 + s)
                    if s < 5:
                        heads(1, lambda h, o: pe.matmul(o, XT[:, h], t1[:, h], start=True, stop=True))
                    heads(2, lambda h, o: pe.matmul(o, t1[:, h], XT[:, h], start=True, stop=True)).then_inc(dn_mm, 1)
                pe.wait_ge(dn_vec, 1 + v0 + 33)
                heads(3, lambda h, o: pe.matmul(o, XT[:, h], vb[:, h], start=True, stop=True))
                heads(4, lambda h, o: pe.matmul(o, kbe[:, h], XT[:, h], start=True, stop=True)).then_inc(dn_mm, 1)
                pe.wait_ge(dn_act, 1 + a0 + 13)
                for c in range(2):
                    lo = c * CHUNK
                    if c:
                        pe.wait_ge(dn_vec, 1 + v0 + 38)
                        pe.wait_ge(dn_act, 1 + a0 + 14)
                    heads(5, lambda h, o: pe.matmul(o, wT[:, h], St[:, h], start=True, stop=True)).then_inc(dn_mm, 1)
                    pe.wait_ge(dn_vec, 1 + v0 + 34 + 5 * c)
                    for h in range(H):
                        o = ps[:, 6, h * CHUNK:(h + 1) * CHUNK]
                        pe.matmul(o, St[:, h], qdec[:, h, lo:lo + CHUNK], start=True, stop=False)
                        pe.matmul(o, vz[:, c, h], AT[:, h, lo:lo + CHUNK], start=False, stop=True)
                    heads(7, lambda h, o: pe.matmul(o, kd[:, h], vz[:, c, h], start=True, stop=True)).then_inc(dn_mm, 1)

            pe.wait_ge(dn_act, 1 + DNA * TILES)
            pe.wait_ge(dn_vec, 1 + DNV * TILES)
            with pe.Fori(0, TILES) as i:
                v0, a0 = SWV * i, SWA_ * i
                pe.wait_ge(sw_act, 1 + a0)
                pe.wait_ge(sw_vec, 1 + v0 + 3)
                for h in range(QH):
                    mm = pe.matmul(ps[:, h // 2, (h % 2) * 256:(h % 2) * 256 + 256], qz[:, h], swk[:, bass.ds(i * P, 2 * P)],
                                   start=True, stop=True)
                mm.then_inc(sw_mm, 1)
                pe.wait_ge(sw_vec, 1 + v0 + 11)
                for h in range(QH):
                    for b in range(2):
                        j = 2 * h + b
                        mm = pe.transpose(ps[:, 4 + j // 4, (j % 4) * P:(j % 4 + 1) * P], prob2[:, h, b * P:(b + 1) * P], ident)
                mm.then_inc(sw_mm, 1)
                pe.wait_ge(sw_act, 1 + a0 + 3)
                for h in range(QH):
                    for b in range(2):
                        mm = pe.matmul(ps[:, h // 4, (h % 4) * P:(h % 4 + 1) * P], vbuf[:, b], probT[:, h, b],
                                       start=(b == 0), stop=(b == 1))
                mm.then_inc(sw_mm, 1)

            pe.wait_ge(sw_act, 1 + SWA_ * TILES)
            for c in range(H):
                pe.wait_ge(gn_sq, c + 1)
                if c >= 2:
                    pe.wait_ge(gn_root, 2 * (c - 1))
                for h in range(2):
                    mm = pe.matmul(ps[:, 2 * (c % 2) + h, :], ones, sq[:, c % 2, h * HALF:(h + 1) * HALF], start=True, stop=True)
                mm.then_inc(gn_mm, 1)

            pe.wait_ge(gn_vec, 2 * H)
            with pe.Fori(0, DC // 2) as i:
                for s in range(2):
                    pe.wait_ge(wup_in[s], 16 * i + 16)
                    for h in range(2):
                        if s == 0:
                            pe.wait_ge(up_done, 1 + 4 * i)
                        else:
                            pe.wait_ge(up_done, 1 + 4 * i + 1 + h)
                        tok = slice(h * HALF, (h + 1) * HALF)
                        for bank, w0, n, src in ((0, 0, DC, hT), (1, 8, DC, hT), (2, 16, H, qkv), (3, 20, H, zq)):
                            for k in range(n):
                                x = src[:, 4 + k, tok] if src is zq else src[:, k, tok]
                                mm = pe.matmul(ps[:, 4 * h + bank, :], wup[:, s, w0 + k, :], x, start=(k == 0), stop=(k == n - 1))
                        mm.then_inc(up_mm, 1)

            def project(n, w_in_sem, done, read, x, step):
                with pe.Fori(0, n) as i:
                    for s in range(2):
                        pe.wait_ge(w_in_sem[s], 16 * i + 16)
                        pe.wait_ge(read, 1 + 2 * i)
                        for h in range(2):
                            for k in range(DC):
                                mm = pe.matmul(ps[:, 2 * s + h, :], wjob[:, s, k, :], x[:, k, h * HALF:(h + 1) * HALF],
                                               start=(k == 0), stop=(k == DC - 1))
                        mm.then_inc(done, 1)

            pe.wait_ge(up_done, 1 + 2 * DC)
            project(DC // 2, wout_in, wo_mm, x2_done, merged, 2)
            norm_sum(1, sq)
            pe.wait_ge(nout[1], DC)

            pe.wait_ge(subk_in, 16)
            pe.wait_ge(h2_lo, DC)
            with pe.Fori(0, 8) as i:
                for s in range(2):
                    n = 2 * i + s
                    pe.wait_ge(q_lo, n + 1)
                    pe.wait_ge(q_copied, 1 + 2 * i)
                    for h in range(2):
                        tok = slice(h * HALF, (h + 1) * HALF)
                        for k in range(DC):
                            o = ps[:, 2 * s + h, :]
                            pe.matmul(o, qs_hi[:, s, k], h2hi[:, k, tok], start=(k == 0), stop=False)
                            pe.matmul(o, qs_hi[:, s, k], h2lo[:, k, tok], start=False, stop=False)
                            mm = pe.matmul(o, qs_lo[:, s, k], h2hi[:, k, tok], start=False, stop=(k == DC - 1))
                    mm.then_inc(q_mm, 1)
                for s in range(2):
                    n = 2 * i + s
                    pe.wait_ge(q_copied, 1 + n + 1)
                    pe.wait_ge(s_copied, 1 + 2 * i)
                    for t in range(TILES):
                        mm = pe.matmul(ps[:, 4 + 2 * s + t // 4, (t % 4) * P:(t % 4 + 1) * P], qj[:, s, t * P:(t + 1) * P],
                                       subk[:, bass.ds(n, 1), :].rearrange("p o n -> p (o n)"), start=True, stop=True)
                    mm.then_inc(s_mm, 1)

            def u_block(n, s, first=False):
                pe.wait_ge(u_ready, n + 1)
                if not first:
                    pe.wait_ge(act_ready, n + 1)
                for h in range(2):
                    tok = slice(h * HALF, (h + 1) * HALF)
                    for k in range(DC):
                        o = ps[:, 2 * s + h, :]
                        pe.matmul(o, uhi[:, s, k], h2hi[:, k, tok], start=(k == 0), stop=False)
                        pe.matmul(o, uhi[:, s, k], h2lo[:, k, tok], start=False, stop=False)
                        mm = pe.matmul(o, ulo[:, s, k], h2hi[:, k, tok], start=False, stop=(k == DC - 1))
                mm.then_inc(u_mm, 1)

            def v_group(j, par, hi, lo, first=False):
                pe.wait_ge(wlo_ready, 2 * j + 2)
                pe.wait_ge(v_ready, 2 * j + 2)
                for b in range(16):
                    c, h = b // 2, b % 2
                    tok = slice(h * HALF, (h + 1) * HALF)
                    if not (first and b < 4):
                        pe.wait_ge(flushed, 16 * j + b - 3)
                    o = ps[:, 4 + b % 4, :]
                    for s in range(2):
                        vh, vl = hi(s)[:, c * P:(c + 1) * P], lo(s)[:, c * P:(c + 1) * P]
                        pe.matmul(o, vh, whi[:, par, s, tok], start=(s == 0), stop=False)
                        pe.matmul(o, vh, wlo[:, par, s, tok], start=False, stop=False)
                        mm = pe.matmul(o, vl, whi[:, par, s, tok], start=False, stop=(s == 1))
                    mm.then_inc(v_mm, 1)

            pe.wait_ge(s_copied, 1 + 16)
            with pe.Fori(0, TILES) as i:
                for k in range(PER_TILE):
                    n = PER_TILE * i + k
                    pe.wait_ge(u_ready, n + 1)
                    pe.wait_ge(act_ready, n + 1)
                    for h in range(2):
                        tok = slice(h * HALF, (h + 1) * HALF)
                        for kk in range(DC):
                            o = ps[:, 2 * (k % 2) + h, :]
                            pe.matmul(o, uhi[:, k % 2, kk], h2hi[:, kk, tok], start=(kk == 0), stop=False)
                            pe.matmul(o, uhi[:, k % 2, kk], h2lo[:, kk, tok], start=False, stop=False)
                            mm = pe.matmul(o, ulo[:, k % 2, kk], h2hi[:, kk, tok], start=False, stop=(kk == DC - 1))
                    mm.then_inc(u_mm, 1)
                pe.wait_ge(rt_vec, 1 + RTV * i + RTV - 1)
                pe.wait_ge(g_copied, 32 * i + 4)
                for j in range(3):
                    mm = pe.transpose(ps[:, 4, j * P:(j + 1) * P], pick[:, j, :], ident)
                mm.then_inc(rt_mm, 1)
                with pe.Fori(0, P // 16) as j:
                    n0 = 16 * (8 * i + j)
                    for t in range(16):
                        if t % 4 == 0:
                            pe.wait_ge(left_ready, n0 + t + 4)
                            pe.wait_ge(g_copied, 4 * (8 * i + j) + t // 4 + 1)
                        pe.wait_ge(right_ready, n0 + t + 1)
                        pe.matmul(ps[:, 4 + t // 4, (t % 4) * P:(t % 4 + 1) * P], oneL[:, t % 8], oneR[:, t % 8],
                                  start=True, stop=True).then_inc(g_mm, 1)

            def v_now(s):
                return vhi[:, s]

            def v_now_lo(s):
                return vlo[:, s]

            def v_alt(s):
                return uhi[:, s].rearrange("p k m -> p (k m)")

            def v_alt_lo(s):
                return ulo[:, s].rearrange("p k m -> p (k m)")

            def u_pair(j):
                for s in range(2):
                    u_block(2 * (LEAD + j) + s, s)

            u_pair(0)
            u_pair(1)
            v_group(0, 0, v_now, v_now_lo, True)
            with pe.Fori(1, FULL // 2) as i:
                for par in range(2):
                    j = 2 * i + par
                    u_pair(j)
                    v_group(j - 1, 1 - par, v_now, v_now_lo)
            v_group(FULL - 1, 1, v_now, v_now_lo)
            with pe.Fori(FULL // 2, GROUPS // 2) as i:
                v_group(2 * i, 0, v_alt, v_alt_lo)
                v_group(2 * i + 1, 1, v_now, v_now_lo)
            norm_sum(2, esq)

        @block.scalar
        def _(act):
            act.wait_ge(const_in, 48)
            act.activation(silc[:], C_, ACT.Silu).then_inc(silc_ready, 1)

            def norm_root(n, x, sqb, rt, ready=None, first=0):
                for c in range(DC):
                    if c >= 2:
                        act.wait_ge(nmm[n], c - 1)
                    if ready is not None:
                        act.wait_ge(ready, first + c + 1)
                    act.activation(sqb[:, c % 2], x[:, c], ACT.Square).then_inc(nsq[n], 1)
                act.wait_ge(nmm[n], DC)
                act.activation(rt[:, 0], halves(ps, 6), ACT.Ln, scale=1.0 / D, bias=EPS).then_inc(nrt[n], 1)
                act.wait_ge(nrt[n], 1)
                act.activation(rt[:, 1], rt[:, 0], ACT.Exp, scale=-0.5).then_inc(nrt[n], 1)

            act.nop().then_inc(act_ready, 2)
            act.nop().then_inc(g_copied, 4)
            act.wait_ge(x_in, 16)
            norm_root(0, xT, sq, rstd)

            def ada_rows(n0, n1, bank):
                for n in range(n0, n1):
                    act.wait_ge(ada_mm, n + 1)
                    if n >= 2:
                        act.wait_ge(ada_col, n - 1)
                    act.activation(arow[0:1, n % 2], ps[0:1, bank + n % 2, :], ACT.Copy).then_inc(ada_row, 1)
            ada_rows(0, ADA_FIRST, 0)

            act.wait_ge(pads_zero, 1)
            with act.Fori(0, 4) as i:
                for s in range(3):
                    act.wait_ge(in_mm, 1 + 3 * i + s + 1)
                    act.wait_ge(conv_done, 1 + 3 * i)
                    act.activation(pre[:, s, 3:3 + T], halves(ps, 2 * s), ACT.Copy).then_inc(in_copied, 1)
                for s in range(3):
                    act.wait_ge(conv_done, 1 + 3 * i + s + 1)
                    act.activation(qkv[:, bass.ds(3 * i + s, 1), :].rearrange("p o t -> p (o t)"), cacc[:, s], ACT.Silu).then_inc(qkv_ready, 1)
            with act.Fori(0, 2) as i:
                for s in range(3):
                    act.wait_ge(in_mm, 1 + 12 + 3 * i + s + 1)
                    act.activation(zq[:, bass.ds(3 * i + s, 1), :].rearrange("p o t -> p (o t)"), halves(ps, 2 * s), ACT.Copy).then_inc(in_copied, 1)
            for s in range(3):
                act.wait_ge(in_mm, 1 + 18 + s + 1)
                dst = zq[:, 6 + s] if s < 2 else swk[:, P:P + T]
                act.activation(dst, halves(ps, 2 * s), ACT.Copy).then_inc(in_copied, 1)
            act.wait_ge(conv_done, 1 + 12)
            ada_rows(ADA_FIRST, ADA_SLABS, 0)
            act.wait_ge(qkv_ready, 1 + 12)
            with act.Fori(0, 4) as i:
                for s in range(2):
                    act.wait_ge(l2_mm, 1 + 2 * i)
                    act.wait_ge(l2_done, 1 + 2 * i)
                    act.activation(sq[:, s], qkv[:, bass.ds(2 * i + s, 1), :].rearrange("p o t -> p (o t)"), ACT.Square).then_inc(l2_sq, 1)
                for s in range(2):
                    act.wait_ge(l2_mm, 1 + 2 * i + s + 1)
                    act.wait_ge(l2_inv, 1 + 2 * i)
                    act.activation(sq[:, s], halves(ps, 2 * s), ACT.Ln, bias=EPS).then_inc(l2_root, 1)
                for s in range(2):
                    act.wait_ge(l2_root, 1 + 2 * i + s + 1)
                    act.activation(rstd[:, s], sq[:, s], ACT.Exp, scale=-0.5).then_inc(l2_done, 1)

            act.wait_ge(gate_vec, 1)
            act.activation(aab, adt, ACT.Abs).then_inc(gate_act, 1)
            act.wait_ge(gate_act, 1)
            act.activation(lns, aab, ACT.Exp, scale=-1.0).then_inc(gate_act, 1)
            act.wait_ge(gate_act, 2)
            act.activation(lns, lns, ACT.Ln, bias=1.0).then_inc(gate_act, 1)
            act.activation(nea[:, 0:H], rows[:, H:2 * H], ACT.Exp).then_inc(gate_act, 1)
            act.activation(beta.rearrange("p (t h) -> p t h", h=H), ab[:, :, H:2 * H], ACT.Sigmoid).then_inc(gate_act, 1)
            act.wait_ge(gate_vec, 7)
            act.activation(eg, gcol, ACT.Exp).then_inc(gate_act, 1)
            act.activation(ekd, dlt, ACT.Exp).then_inc(gate_act, 1)

            act.wait_ge(gate_vec, 9)
            with act.Fori(0, TILES) as i:
                v0, m0 = DNV * i, DNM * i
                act.wait_ge(dn_vec, 1 + v0 + 6)
                act.activation(egrow[:].rearrange("p h n -> p (h n)"), ps[:, 0, :], ACT.Exp).then_inc(dn_act, 1)
                for h in range(H):
                    act.activation(gam[:, h], gm[:, h], ACT.Exp, bias=ngcol[:, bass.ds(H * i + h, 1)]).then_inc(dn_act, 1)
                for s in range(6):
                    act.wait_ge(dn_mm, 1 + m0 + 7 + 2 * s)
                    act.activation(t1[:].rearrange("p h n -> p (h n)"), ps[:, 0, :], ACT.Copy).then_inc(dn_act, 1)
                act.wait_ge(dn_mm, 1 + m0 + 19)
                act.activation(u[:].rearrange("p h n -> p (h n)"), ps[:, 3, :], ACT.Copy).then_inc(dn_act, 1)
                act.activation(wT[:].rearrange("p h n -> p (h n)"), ps[:, 4, :], ACT.Copy).then_inc(dn_act, 1)
                for c in range(2):
                    act.wait_ge(dn_mm, 1 + m0 + 21 + 2 * c)
                    act.activation(qkv[:, 0:H, bass.ds(i * P + c * CHUNK, CHUNK)],
                                   ps[:, 6, 0:H * CHUNK].rearrange("p (h n) -> p h n", h=H), ACT.Copy).then_inc(dn_act, 1)

            with act.Fori(0, TILES) as i:
                v0, m0 = SWV * i, SWM * i
                act.wait_ge(sw_vec, 1 + v0 + 7)
                act.activation(prob[:], prob2[:], ACT.Exp).then_inc(sw_act, 1)
                act.activation(stat[:, 3], stat[:, 2], ACT.Exp).then_inc(sw_act, 1)
                act.wait_ge(sw_mm, 1 + m0 + 2)
                act.activation(probT[:].rearrange("p h b n -> p (h b n)"), ps[:, 4:8, :].rearrange("p b n -> p (b n)"), ACT.Copy).then_inc(sw_act, 1)
                act.wait_ge(sw_mm, 1 + m0 + 3)
                for r in range(2):
                    rr = slice(r * HD, (r + 1) * HD)
                    act.activation(zq[rr, 4:8, bass.ds(i * P, P)], ps[rr, r, :].rearrange("p (h n) -> p h n", h=4), ACT.Copy).then_inc(sw_act, 1)

            act.wait_ge(sw_mm, 1 + SWM * TILES)
            act.wait_ge(sw_vec, 1 + SWV * TILES)
            for c in range(H):
                act.activation(zq[:, c], zq[:, c], ACT.Silu).then_inc(z_silu, 1)
            for c in range(H):
                if c >= 2:
                    act.wait_ge(gn_mm, c - 1)
                act.activation(sq[:, c % 2], qkv[:, c], ACT.Square).then_inc(gn_sq, 1)
                act.wait_ge(gn_mm, c + 1)
                if c >= 2:
                    act.wait_ge(gn_vec, 2 * (c - 1))
                act.activation(rstd[:, c % 2], halves(ps, 2 * (c % 2)), ACT.Ln, scale=1.0 / P, bias=EPS).then_inc(gn_root, 1)
                act.wait_ge(gn_root, 2 * c + 1)
                act.activation(rstd[:, c % 2], rstd[:, c % 2], ACT.Exp, scale=-0.5).then_inc(gn_root, 1)

            act.wait_ge(gn_vec, 2 * H)
            with act.Fori(0, DC // 2) as i:
                for s in range(2):
                    for h in range(2):
                        n = 2 * (2 * i + s) + h
                        act.wait_ge(up_mm, 1 + n + 1)
                        act.wait_ge(up_done, 1 + 4 * i) if s == 0 else act.wait_ge(up_done, 1 + 4 * i + 1 + h)
                        for b in range(2):
                            act.activation(sig[:, h, b], ps[:, 4 * h + b, :], ACT.Sigmoid).then_inc(up_sig, 1)

            act.wait_ge(up_done, 1 + 2 * DC)
            norm_root(1, xT, sq, rstd, x2_done, 1)

            for c in range(DC):
                act.wait_ge(nout[1], c + 1)
                act.activation(h2hi[:, c], hT[:, c], ACT.Copy).then_inc(h2_hi, 1)
            with act.Fori(0, 8) as i:
                for s in range(2):
                    act.wait_ge(wq_in[s], 16 * i + 16)
                    act.wait_ge(q_mm, 1 + 2 * i)
                    act.activation(qs_hi[:, s].rearrange("p k m -> p (k m)"), wjob[:, s].rearrange("p k m -> p (k m)"), ACT.Copy).then_inc(q_hi, 1)
                for s in range(2):
                    act.wait_ge(q_mm, 1 + 2 * i + s + 1)
                    act.wait_ge(s_mm, 1 + 2 * i)
                    act.activation(qj[:, s], halves(ps, 2 * s), ACT.Copy).then_inc(q_copied, 1)

            def u_high(n, s, landed, first=False):
                act.wait_ge(ust_in[s], landed)
                if not first:
                    act.wait_ge(u_mm, n - 1)
                act.activation(uhi[:, s].rearrange("p k m -> p (k m)"), ust[:, s].rearrange("p k m -> p (k m)"), ACT.Copy).then_inc(uhi_ready, 1)

            def gelu(n, s):
                act.wait_ge(u_mm, n + 1)
                act.activation(actb[:, s], halves(ps, 2 * s), ACT.Gelu).then_inc(act_ready, 1)

            act.wait_ge(q_copied, 1 + 16)
            for s in range(2):
                u_high(s, s, 16, True)
            with act.Fori(0, TILES) as i:
                n = PER_TILE * i
                for k in range(PER_TILE):
                    if k == 3:
                        act.wait_ge(rt_vec, 1 + RTV * i + 16)
                        act.activation(cv[:], cv[:], ACT.Exp).then_inc(rt_exp, 1)
                    act.wait_ge(act_out[k % 2], 16 + 16 * (2 * i + k // 2))
                    gelu(n + k, k % 2)
                    if k < 3:
                        u_high(n + k + 2, k % 2, 16 * (2 * i + (k + 2) // 2 + 1))
                act.wait_ge(g_out, 16 + 16 * i)
                with act.Fori(0, P // 16) as j:
                    for b in range(4):
                        act.wait_ge(g_mm, 8 + 16 * (8 * i + j) + 4 * b + 4)
                        act.activation(Gsb[:, :, bass.ds(16 * j + 4 * b, 4)].rearrange("p e t -> p t e"),
                                       ps[:, 4 + b, :].rearrange("p (t e) -> p t e", t=4), ACT.Copy).then_inc(g_copied, 1)
                act.wait_ge(g_copied, 4 + 32 * (i + 1))
                act.dma_start(g_dram[:, :, bass.ds(i * P, P)].rearrange("j i t -> i j t"), Gsb[:]).then_inc(g_out, 16)
                u_high(n + 5, 1, 16 * (2 * i + 3))

            def w_high(j, s, par, first=False):
                act.wait_ge(w_ready, 2 * j + s + 1)
                if not first:
                    act.wait_ge(v_mm, 16 * (j - 1))
                act.activation(whi[:, par, s], wbuf[:, s], ACT.Copy).then_inc(whi_ready, 1)

            def v_high(j, s, dst, free):
                act.wait_ge(vst_in[s], 16 * j + 16)
                if free is not None:
                    act.wait_ge(v_mm, free)
                act.activation(dst, vst[:, s], ACT.Copy).then_inc(vhi_ready, 1)

            def step(j, par, first=False, second=False, last=False):
                for s in range(2):
                    n = 2 * (LEAD + j) + s
                    if first:
                        act.wait_ge(act_out[s], 16 + 16 * (EARLY // 2))
                    else:
                        act.wait_ge(w_ready, 2 * j + s - 1)
                    gelu(n, s)
                    if not last:
                        u_high(n + 2, s, 16 * (LEAD + j + 2))
                    w_high(j, s, par, first or second)
                for s in range(2):
                    v_high(j, s, vhi[:, s], None if first else 16 * j)

            act.wait_ge(g_out, 16 + 16 * TILES)
            step(0, 0, first=True)
            step(1, 1, second=True)
            with act.Fori(1, FULL // 2 - 1) as i:
                for par in range(2):
                    step(2 * i + par, par)
            step(FULL - 2, 0)
            step(FULL - 1, 1, last=True)
            with act.Fori(FULL // 2, GROUPS // 2) as i:
                for par in range(2):
                    j = 2 * i + par
                    for s in range(2):
                        w_high(j, s, par)
                        dst = vhi[:, s] if par else uhi[:, s].rearrange("p k m -> p (k m)")
                        v_high(j, s, dst, 16 * (j - 1))

            norm_root(2, acc, esq, erstd, x3_done)

        @block.vector
        def _(dve):
            class Chain:

                def __init__(self, first=0):
                    self.first, self.n = first, 0

                def up(self):
                    self.n += 1
                    return 1

                def now(self):
                    return self.first + self.n

            dve.wait_ge(const_in, 48)

            def ada_bias(n0, n1, bank):
                for n in range(n0, n1):
                    dve.wait_ge(ada_col, n + 1)
                    dve.tensor_tensor(mod[:, 4 * n:4 * n + 4], ps[:, bank + n % 2, 0:4], ADAB[:, 4 * n:4 * n + 4],
                                      ALU.add).then_inc(ada_add, 1)
                dve.wait_ge(ada_add, n1)

            ada_bias(0, ADA_FIRST, 2)
            dve.scalar_tensor_tensor(amp1[:], mod[:, 8:16], 1.0, G1, ALU.add, ALU.mult).then_inc(mod_ready, 1)
            dve.wait_ge(mod_ready, 1)

            def norm_apply(n, x, rt, dst, amp, shift):
                dve.wait_ge(nrt[n], 2)
                for c in range(DC):
                    r = dve.scalar_tensor_tensor(dst[:, c], x[:, c], amp[:, c:c + 1], rt[:, 1], ALU.mult, ALU.mult)
                    if shift is None:
                        r.then_inc(nout[n], 1)
                        continue
                    r.then_inc(nsc[n], 1)
                    if c:
                        dve.wait_ge(nsc[n], c)
                        dve.tensor_scalar(dst[:, c - 1], dst[:, c - 1], shift[:, c - 1:c], None, ALU.add).then_inc(nout[n], 1)
                if shift is not None:
                    dve.wait_ge(nsc[n], DC)
                    dve.tensor_scalar(dst[:, DC - 1], dst[:, DC - 1], shift[:, DC - 1:DC], None, ALU.add).then_inc(nout[n], 1)

            norm_apply(0, xT, rstd, hT, amp1, mod[:, 0:8])

            dve.wait_ge(nout[0], DC)
            dve.memset(swk[:, 0:P], 0.0)
            dve.memset(vtok[:, 0], 0.0)
            dve.memset(pre[:, :, 0:3], 0.0).then_inc(pads_zero, 1)
            with dve.Fori(0, 4) as i:
                for s in range(3):
                    dve.wait_ge(in_copied, 1 + 3 * i + s + 1)
                    dve.wait_ge(qkv_ready, 1 + 3 * i)
                    tap = [CONV[:, bass.ds(12 * i + 4 * s + j, 1)] for j in range(4)]
                    dve.tensor_scalar(cacc[:, s], pre[:, s, 0:T], tap[0], None, ALU.mult).then_inc(conv_step, 1)
                    for j in range(1, 4):
                        dve.wait_ge(conv_step, 9 * i + 3 * s + j)
                        r = dve.scalar_tensor_tensor(cacc[:, s], pre[:, s, j:j + T], tap[j], cacc[:, s], ALU.mult, ALU.add)
                        r.then_inc(conv_step if j < 3 else conv_done, 1)
            for t in range(TILES):
                dve.wait_ge(sm_mm, t + 1)
                dve.tensor_copy(ab[:, t], ps[:, 6 + t % 2, 0:8]).then_inc(sm_copied, 1)
                dve.tensor_copy(vtok[:, 1 + t], ps[:, 6 + t % 2, 8:SMALL]).then_inc(sm_copied, 1)
            ada_bias(ADA_FIRST, ADA_SLABS, 2)
            dve.scalar_tensor_tensor(amp2[:], mod[:, 32:40], 1.0, G2, ALU.add, ALU.mult).then_inc(mod_ready, 1)
            dve.wait_ge(mod_ready, 2)
            with dve.Fori(0, 4) as i:
                for s in range(2):
                    dve.wait_ge(l2_done, 1 + 2 * i + s + 1)
                    row = qkv[:, bass.ds(2 * i + s, 1), :].rearrange("p o t -> p (o t)")
                    dve.tensor_tensor(row, row, rstd[:, s], ALU.mult).then_inc(l2_inv, 1)

            def th(x):
                return x.rearrange("p (t h) -> p t h", h=H)
            dve.wait_ge(sm_copied, 2 * TILES)
            dve.tensor_tensor(th(adt), ab[:, :, 0:H], rows[:, 0:H].unsqueeze(1).to_broadcast([P, TILES, H]), ALU.add).then_inc(gate_vec, 1)
            dve.wait_ge(gate_vec, 1)
            dve.wait_ge(gate_act, 4)
            dve.tensor_scalar(adt, adt, 0.0, None, ALU.max).then_inc(gate_vec, 1)
            dve.wait_ge(gate_vec, 2)
            dve.tensor_tensor(adt, adt, lns, ALU.add).then_inc(gate_vec, 1)
            dve.wait_ge(gate_vec, 3)
            dve.scalar_tensor_tensor(th(ld), th(adt), -1.0, nea[:, 0:H].unsqueeze(1).to_broadcast([P, TILES, H]),
                                     ALU.mult, ALU.mult).then_inc(gate_vec, 1)
            dve.wait_ge(gate_mm, 1)
            dve.tensor_copy(gcol, ps[:, 0, 0:32]).then_inc(gate_vec, 1)
            dve.tensor_scalar(ngcol, ps[:, 0, 0:32], -1.0, None, ALU.mult).then_inc(gate_vec, 1)
            dve.wait_ge(gate_vec, 6)
            dve.tensor_tensor(dlt, ps[:, 0, 32:64], gcol, ALU.subtract).then_inc(gate_vec, 1)
            dve.wait_ge(gate_act, 7)
            dve.tensor_tensor(beg, beta, eg, ALU.mult).then_inc(gate_vec, 1)
            dve.memset(St[:], 0.0).then_inc(gate_vec, 1)
            dve.wait_ge(gate_vec, 9)

            def flat(x):
                return x[:].rearrange("p h n -> p (h n)")

            def over_n(col, i):
                return col[:, bass.ds(H * i, H)].unsqueeze(2).to_broadcast([P, H, P])

            def over_h(m):
                return m.unsqueeze(1).to_broadcast([P, H, P])

            with dve.Fori(0, TILES) as i:
                c_, m0, a0 = Chain(DNV * i), DNM * i, DNA * i
                tok = bass.ds(i * P, P)
                dve.wait_ge(dn_mm, 1 + m0)
                dve.tensor_copy(kn[:], qkv[:, H:2 * H, tok]).then_inc(dn_vec, c_.up())
                dve.tensor_scalar(qn[:], qkv[:, 0:H, tok], float(P) ** -0.5, None, ALU.mult).then_inc(dn_vec, c_.up())
                dve.tensor_copy(vv[:], qkv[:, 2 * H:3 * H, tok]).then_inc(dn_vec, c_.up())
                dve.tensor_copy(ldb[:], over_n(ld, i)).then_inc(dn_vec, c_.up())
                dve.tensor_copy(btb[:], over_n(beta, i)).then_inc(dn_vec, c_.up())
                dve.wait_ge(dn_mm, 1 + m0 + 1)
                dve.tensor_tensor(gm[:], ps[:, 0, :].rearrange("p (h n) -> p h n", h=H), over_h(neg), ALU.add).then_inc(dn_vec, c_.up())
                dve.wait_ge(dn_mm, 1 + m0 + 6)
                dve.wait_ge(dn_act, 1 + a0 + 5)
                bank = [ps[:, b, :].rearrange("p (h n) -> p h n", h=H) for b in range(8)]
                dve.tensor_tensor(LT[:], bank[2], gam[:], ALU.mult).then_inc(dn_vec, c_.up())
                dve.tensor_tensor(AT[:], bank[3], gam[:], ALU.mult).then_inc(dn_vec, c_.up())
                dve.tensor_tensor(vb[:], bank[5], over_n(beta, i), ALU.mult).then_inc(dn_vec, c_.up())
                dve.tensor_tensor(kbe[:], bank[4], over_n(beg, i), ALU.mult).then_inc(dn_vec, c_.up())
                dve.tensor_tensor(kd[:], bank[4], over_n(ekd, i), ALU.mult).then_inc(dn_vec, c_.up())
                dve.tensor_tensor(qdec[:], qn[:], egrow[:], ALU.mult).then_inc(dn_vec, c_.up())
                dve.tensor_copy(X[:], over_h(ident)).then_inc(dn_vec, c_.up())
                dve.tensor_copy(XT[:], over_h(ident)).then_inc(dn_vec, c_.up())
                dve.wait_ge(dn_vec, 1 + c_.now())
                dve.tensor_tensor(LT[:], LT[:], bank[1], ALU.mult).then_inc(dn_vec, c_.up())
                dve.memset(vz[:], 0.0).then_inc(dn_vec, c_.up())
                assert c_.n == 16
                for s in range(6):
                    dve.wait_ge(dn_vec, 1 + c_.now())
                    dve.tensor_tensor(bt[:], LT[:], over_h(level[s]), ALU.mult).then_inc(dn_vec, c_.up())
                    dve.wait_ge(dn_mm, 1 + m0 + 8 + 2 * s)
                    if s < 5:
                        dve.tensor_tensor(X[:], X[:], bank[1], ALU.subtract).then_inc(dn_vec, c_.up())
                    dve.tensor_tensor(XT[:], XT[:], bank[2], ALU.subtract).then_inc(dn_vec, c_.up())
                assert c_.n == 33
                for c in range(2):
                    lo = c * CHUNK
                    dve.wait_ge(dn_mm, 1 + m0 + 20 + 2 * c)
                    dve.tensor_tensor(vz[lo:lo + CHUNK, c], u[lo:lo + CHUNK], bank[5][lo:lo + CHUNK], ALU.subtract).then_inc(dn_vec, c_.up())
                    dve.wait_ge(dn_mm, 1 + m0 + 21 + 2 * c)
                    for h in range(H):
                        dve.scalar_tensor_tensor(St[:, h], St[:, h], egrow[:, h, lo + CHUNK - 1:lo + CHUNK], bank[7][:, h],
                                                 ALU.mult, ALU.add).then_inc(dn_vec, c_.up())
                assert c_.n == DNV, c_.n

            dve.wait_ge(dn_act, 1 + DNA * TILES)
            dve.wait_ge(dn_vec, 1 + DNV * TILES)
            dve.memset(qz[:], 0.0)
            dve.tensor_copy(mbuf[:], wmask0).then_inc(gate_vec, 1)
            dve.wait_ge(gate_vec, 10)
            with dve.Fori(0, TILES) as i:
                c_, m0, a0 = Chain(SWV * i), SWM * i, SWA_ * i
                dve.wait_ge(sw_mm, 1 + m0)
                dve.wait_ge(sw_vec, 1 + SWV * i)
                for r in range(2):
                    rr = slice(r * HD, (r + 1) * HD)
                    dve.tensor_scalar(qz[rr, 4 * r:4 * r + 4], zq[rr, 4:8, bass.ds(i * P, P)], float(HD) ** -0.5, None,
                                      ALU.mult).then_inc(sw_vec, c_.up())
                dve.tensor_copy(vbuf[:].rearrange("p b n -> p (b n)"),
                                vtok[:].rearrange("p b n -> p (b n)")[:, bass.ds(i * P, 2 * P)]).then_inc(sw_vec, c_.up())
                dve.wait_ge(sw_mm, 1 + m0 + 1)
                scores = ps[:, 0:4, :].rearrange("p b (h n) -> p (b h) n", h=2)
                dve.tensor_tensor(prob[:], scores, mbuf[:].unsqueeze(1).to_broadcast([P, QH, 2 * P]), ALU.add).then_inc(sw_vec, c_.up())
                dve.wait_ge(sw_vec, 1 + c_.now())
                dve.tensor_reduce(stat[:, 0], prob[:], AX.X, ALU.max).then_inc(sw_vec, c_.up())
                dve.wait_ge(sw_vec, 1 + c_.now())
                sinks = rows[:, 8:16]
                dve.tensor_tensor(stat[:, 1], stat[:, 0], sinks, ALU.max).then_inc(sw_vec, c_.up())
                dve.wait_ge(sw_vec, 1 + c_.now())
                dve.tensor_tensor(stat[:, 2], sinks, stat[:, 1], ALU.subtract)
                dve.tensor_tensor(prob2[:], prob[:], stat[:, 1].unsqueeze(2).to_broadcast([P, QH, 2 * P]), ALU.subtract).then_inc(sw_vec, c_.up())
                dve.wait_ge(sw_act, 1 + a0 + 2)
                dve.tensor_reduce(stat[:, 4], prob[:], AX.X, ALU.add).then_inc(sw_vec, c_.up())
                dve.wait_ge(sw_vec, 1 + c_.now())
                dve.tensor_tensor(stat[:, 5], stat[:, 4], stat[:, 3], ALU.add).then_inc(sw_vec, c_.up())
                dve.wait_ge(sw_vec, 1 + c_.now())
                dve.reciprocal(stat[:, 4], stat[:, 5]).then_inc(sw_vec, c_.up())
                dve.wait_ge(sw_vec, 1 + c_.now())
                dve.tensor_tensor(prob2[:], prob[:], stat[:, 4].unsqueeze(2).to_broadcast([P, QH, 2 * P]), ALU.mult).then_inc(sw_vec, c_.up())
                dve.tensor_copy(mbuf[:], wmask).then_inc(sw_vec, c_.up())
                assert c_.n == SWV, c_.n

            for c in range(H):
                dve.wait_ge(gn_root, 2 * c + 2)
                dve.scalar_tensor_tensor(qkv[:, c], qkv[:, c], OGAIN, rstd[:, c % 2], ALU.mult, ALU.mult).then_inc(gn_vec, 1)
                dve.wait_ge(gn_vec, 2 * c + 1)
                dve.wait_ge(z_silu, c + 1)
                dve.tensor_tensor(qkv[:, c], qkv[:, c], zq[:, c], ALU.mult).then_inc(gn_vec, 1)

            with dve.Fori(0, DC // 2) as i:
                for s in range(2):
                    for h in range(2):
                        n = 2 * (2 * i + s) + h
                        dve.wait_ge(up_sig, 2 * n + 2)
                        for b in range(2):
                            dve.tensor_tensor(mtmp[:, h, b], sig[:, h, b], ps[:, 4 * h + 2 + b, :], ALU.mult).then_inc(up_vec, 1)
                        dve.wait_ge(up_vec, 2 * n + 2)
                        dst = merged[:, bass.ds(2 * i + s, 1), h * HALF:(h + 1) * HALF].rearrange("p o t -> p (o t)")
                        dve.tensor_tensor(dst, mtmp[:, h, 0], mtmp[:, h, 1], ALU.add).then_inc(up_done, 1)
            dve.wait_ge(x_back, 16)
            dve.wait_ge(up_done, 1 + 2 * DC)
            with dve.Fori(0, DC // 2) as i:
                for s in range(2):
                    dve.wait_ge(wo_mm, 1 + 2 * i + s + 1)
                    row = xT[:, bass.ds(2 * i + s, 1), :].rearrange("p o t -> p (o t)")
                    dve.scalar_tensor_tensor(row, halves(ps, 2 * s), mod[:, bass.ds(16 + 2 * i + s, 1)], row, ALU.mult, ALU.add).then_inc(x2_done, 1)
            dve.wait_ge(x2_done, 1 + DC)
            norm_apply(1, xT, rstd, hT, amp2, mod[:, 24:32])

            def fl(x):
                return x.rearrange("p k m -> p (k m)")

            for c in range(DC):
                dve.wait_ge(h2_hi, c + 1)
                dve.tensor_tensor(h2lo[:, c], hT[:, c], h2hi[:, c].bitcast(F32), ALU.subtract).then_inc(h2_lo, 1)
            with dve.Fori(0, 8) as i:
                for s in range(2):
                    dve.wait_ge(q_hi, 2 * i + s + 1)
                    dve.tensor_tensor(fl(qs_lo[:, s]), fl(wjob[:, s]), fl(qs_hi[:, s]).bitcast(F32), ALU.subtract).then_inc(q_lo, 1)
                for s in range(2):
                    dve.wait_ge(s_mm, 1 + 2 * i + s + 1)
                    dve.wait_ge(score_out[s], 16 + 16 * i)
                    dve.tensor_copy(fl(sj[:, s]), halves(ps, 4 + 2 * s)).then_inc(s_copied, 1)

            def u_low(n, s):
                dve.wait_ge(uhi_ready, n + 1)
                dve.tensor_tensor(fl(ulo[:, s]), fl(ust[:, s]), fl(uhi[:, s]).bitcast(F32), ALU.subtract).then_inc(u_ready, 1)

            for s in range(2):
                u_low(s, s)
            with dve.Fori(0, TILES) as i:
                c_ = Chain(RTV * i)
                n = PER_TILE * i

                def top16(m, vals, idx, src, tmp):
                    def each(f):
                        dve.wait_ge(rt_vec, 1 + c_.now())
                        dve.memset(carrier[:, 0:1], 0.0)
                        for j in range(m):
                            op = f(j)
                        op.then_inc(rt_vec, c_.up())
                    each(lambda j: dve.max(vals[:, j, 0:8], src[:, j]))
                    each(lambda j: dve.max_index(idx[:, j, 0:8], vals[:, j, 0:8], src[:, j]))
                    each(lambda j: dve.match_replace(tmp[:, j], vals[:, j, 0:8], src[:, j], LOWEST))
                    each(lambda j: dve.max(vals[:, j, 8:16], tmp[:, j]))
                    each(lambda j: dve.max_index(idx[:, j, 8:16], vals[:, j, 8:16], tmp[:, j]))

                dve.wait_ge(score_in, 16 * i + 16)
                top16(16, sv, si, sc, sc2)
                u_low(n + 2, 0)
                dve.wait_ge(rt_vec, 1 + c_.now())
                dve.tensor_copy(sif[:], si[:]).then_inc(rt_vec, c_.up())
                sv4 = sv[:].rearrange("p (h two) k -> p h two k", two=2)
                shape = [P, PH, TOPK, TOPK]
                cand = sc[:].rearrange("p (h two) n -> p h (two n)", two=2)
                cand2 = sc2[:].rearrange("p (h two) n -> p h (two n)", two=2)
                dve.tensor_tensor(cand.rearrange("p h (a b) -> p h a b", b=TOPK), sv4[:, :, 0, :].unsqueeze(3).to_broadcast(shape),
                                  sv4[:, :, 1, :].unsqueeze(2).to_broadcast(shape), ALU.add).then_inc(rt_vec, c_.up())
                top16(PH, cv, ci, cand, cand2)
                assert c_.n == 12
                dve.wait_ge(rt_vec, 1 + c_.now())
                flat_ci = ci[:].rearrange("p h k -> p (h k)")
                dve.tensor_scalar(cab[:, 0], flat_ci, 4, None, ALU.logical_shift_right)
                dve.tensor_scalar(cab[:, 1], flat_ci, 15, None, ALU.bitwise_and).then_inc(rt_vec, c_.up())
                dve.wait_ge(rt_vec, 1 + c_.now())
                dve.tensor_copy(cabf[:], cab[:]).then_inc(rt_vec, c_.up())
                assert c_.n == 14
                dve.tensor_copy(gsum[:, 0], cv[:, :, 0]).then_inc(rt_vec, c_.up())
                dve.wait_ge(rt_vec, 1 + c_.now())
                top = gsum[:, 0].unsqueeze(2).to_broadcast([P, PH, TOPK])
                dve.tensor_tensor(cv[:], cv[:], top, ALU.subtract).then_inc(rt_vec, c_.up())
                assert c_.n == 16
                dve.tensor_tensor(eqa[:], cabf[:, 0].rearrange("p (h k) -> p h k", h=PH).unsqueeze(3).to_broadcast(shape),
                                  iota[:, 0:TOPK].unsqueeze(1).unsqueeze(1).to_broadcast(shape), ALU.is_equal).then_inc(rt_vec, c_.up())
                u_low(n + 3, 1)
                sif4 = sif[:].rearrange("p (h two) k -> p h two k", two=2)
                eq = cand2.rearrange("p h (k a) -> p h k a", k=TOPK)
                dve.tensor_tensor(eq, cabf[:, 1].rearrange("p (h k) -> p h k", h=PH).unsqueeze(3).to_broadcast(shape),
                                  iota[:, 0:TOPK].unsqueeze(1).unsqueeze(1).to_broadcast(shape), ALU.is_equal).then_inc(rt_vec, c_.up())
                dve.wait_ge(rt_vec, 1 + c_.now())
                dve.tensor_tensor(eq, eq, sif4[:, :, 1, :].unsqueeze(2).to_broadcast(shape), ALU.mult).then_inc(rt_vec, c_.up())
                dve.wait_ge(rt_vec, 1 + c_.now())
                dve.tensor_reduce(pick[:, 1].rearrange("p (h k) -> p h k", h=PH), eq, AX.X, ALU.add).then_inc(rt_vec, c_.up())
                dve.wait_ge(rt_exp, i + 1)
                dve.tensor_reduce(gsum[:, 1], cv[:], AX.X, ALU.add).then_inc(rt_vec, c_.up())
                dve.wait_ge(rt_vec, 1 + c_.now())
                dve.reciprocal(gsum[:, 0], gsum[:, 1]).then_inc(rt_vec, c_.up())
                dve.wait_ge(rt_vec, 1 + c_.now())
                dve.tensor_tensor(pick[:, 2].rearrange("p (h k) -> p h k", h=PH), cv[:],
                                  gsum[:, 0].unsqueeze(2).to_broadcast([P, PH, TOPK]), ALU.mult).then_inc(rt_vec, c_.up())
                dve.wait_ge(rt_pool, i + 1)
                dve.tensor_reduce(pick[:, 0].rearrange("p (h k) -> p h k", h=PH), eqa[:], AX.X, ALU.add).then_inc(rt_vec, c_.up())
                assert c_.n == RTV - 1, c_.n
                dve.wait_ge(rt_mm, i + 1)
                dve.tensor_copy(rT[:].rearrange("p r n -> p (r n)"), ps[:, 4, 0:3 * P]).then_inc(rt_vec, c_.up())
                u_low(n + 4, 0)
                dve.wait_ge(rt_vec, 1 + c_.now())
                dve.memset(carrier[:, 0:1], 0.0)
                with dve.Fori(0, P // 16) as j:
                    n0 = 16 * (8 * i + j)
                    for t in range(16):
                        if t % 4 == 0:
                            dve.wait_ge(g_mm, n0 + t + 4)
                            dve.tensor_tensor(oneL[:, t % 8:t % 8 + 4], iota.unsqueeze(1).to_broadcast([P, 4, P]),
                                              rT[:, 0, bass.ds(16 * j + t, 4)].unsqueeze(2).to_broadcast([P, 4, P]),
                                              ALU.is_equal).then_inc(left_ready, 4)
                        col = [rT[:, m, bass.ds(16 * j + t, 1)] for m in (1, 2)]
                        dve.wait_ge(g_mm, n0 + t + 1)
                        dve.tensor_scalar(oneR[:, t % 8], iota, col[0], col[1], ALU.is_equal, ALU.mult).then_inc(right_ready, 1)
                u_low(n + 5, 1)

            def weigh(j, s, first=False, landed=None):
                if landed is None:
                    dve.wait_ge(act_ready, 2 * (LEAD + j) + s + 3)
                else:
                    dve.wait_ge(act_in[s], landed)
                dve.wait_ge(gst_in[s], 16 * j + 16)
                if not first:
                    dve.wait_ge(wlo_ready, 2 * j + s - 1)
                dve.tensor_tensor(wbuf[:, s], gst[:, s], actb[:, s], ALU.mult).then_inc(w_ready, 1)

            def w_low(j, s, par):
                dve.wait_ge(whi_ready, 2 * j + s + 1)
                dve.tensor_tensor(wlo[:, par, s], wbuf[:, s], whi[:, par, s].bitcast(F32), ALU.subtract).then_inc(wlo_ready, 1)

            def v_low(j, s, hi, lo):
                dve.wait_ge(vhi_ready, 2 * j + s + 1)
                dve.tensor_tensor(lo, vst[:, s], hi.bitcast(F32), ALU.subtract).then_inc(v_ready, 1)

            def flush(j, b0=0, b1=16):
                for b in range(b0, b1):
                    dve.wait_ge(v_mm, 16 * j + b + 1)
                    o = acc[:, b // 2, (b % 2) * HALF:(b % 2 + 1) * HALF]
                    dve.tensor_tensor(o, o, ps[:, 4 + b % 4, :], ALU.add).then_inc(flushed, 1)

            def step(j, par, first=False, last=False):
                for s in range(2):
                    weigh(j, s, first)
                    if not last:
                        u_low(2 * (LEAD + j + 1) + s, s)
                    w_low(j, s, par)
                if not first:
                    flush(j - 1)
                for s in range(2):
                    v_low(j, s, vhi[:, s], vlo[:, s])

            step(0, 0, first=True)
            dve.wait_ge(acc_zero, 1)
            step(1, 1)
            with dve.Fori(1, FULL // 2 - 1) as i:
                for par in range(2):
                    step(2 * i + par, par)
            step(FULL - 2, 0)
            step(FULL - 1, 1, last=True)
            with dve.Fori(FULL // 2, GROUPS // 2) as i:
                for par in range(2):
                    j = 2 * i + par
                    hi, lo = (vhi, vlo) if par else (uhi, ulo)
                    for s in range(2):
                        weigh(j, s, landed=16 * (j - FULL) + 16)
                        w_low(j, s, par)
                        flush(j - 1, 4 * s, 4 * s + 4)
                    for s in range(2):
                        v_low(j, s, hi[:, s] if par else fl(hi[:, s]), lo[:, s] if par else fl(lo[:, s]))
                        flush(j - 1, 8 + 4 * s, 12 + 4 * s)
            flush(GROUPS - 1)

            dve.wait_ge(flushed, 16 * GROUPS)
            dve.wait_ge(x2_in, 16)
            for c in range(DC):
                dve.scalar_tensor_tensor(acc[:, c], acc[:, c], mod[:, 40 + c:41 + c], x2[:, c], ALU.mult, ALU.add).then_inc(x3_done, 1)
            dve.wait_ge(x3_done, DC)
            norm_apply(2, acc, erstd, oT, GF, None)


def constants():
    i = np.arange(P)
    f = np.float32
    keep = np.concatenate([np.eye(P), np.tile(i, (P, 1)), np.ones((P, P))], 1).astype(f)
    same = (i[:, None] // CHUNK) == (i[None, :] // CHUNK)
    tri = same & (i[:, None] <= i[None, :])
    parts = [tri, same, np.where(tri, 0.0, -BIG)]
    for s in range(6):
        w = 1 << s
        parts.append(((i[:, None] // (2 * w)) == (i[None, :] // (2 * w))) & ((i[:, None] // w) % 2 == 0) & ((i[None, :] // w) % 2 == 1))
    j = np.arange(2 * P)
    own = i[:, None] // CHUNK + 2
    kc = j[None, :] // CHUNK
    ok = (kc == own) | (kc == own - 1)
    parts.append(np.where(ok, 0.0, -BIG))
    parts.append(np.where(ok & (j[None, :] >= P), 0.0, -BIG))
    return keep, np.concatenate([np.asarray(x, f) for x in parts], 1)


def lay_out(x, c, ada_w, ada_b, norm1_gain, w_in, conv_w, dn_a_log, dn_dt_bias, dn_out_gain, swa_sinks, w_dn_up,
            w_swa_up, w_out, norm2_gain, peer_w_q, peer_sub_keys, peer_u, peer_v, final_gain):
    keep, masks = constants()

    def col(v):
        return v.reshape(-1, P).T

    def blocks(w):
        k, n = w.shape
        return w.reshape(k // P, P, n // P, P).transpose(2, 1, 0, 3)

    w = w_in[0]
    q0 = 1536 + 8 + 512
    heads = [slice(q0 + h * HD, q0 + (h + 1) * HD) for g in range(4) for h in (g, g + 4)]
    k0 = q0 + 512
    g0 = k0 + 256
    front = np.concatenate([w[:, 0:1536], w[:, 1544:1544 + 512]] + [w[:, s] for s in heads] + [w[:, k0:k0 + P]], 1)
    small = np.concatenate([w[:, 1536:1544], w[:, k0 + P:k0 + 2 * P]], 1)
    up_rows = np.concatenate([w_swa_up[0][h * HD:(h + 1) * HD] for g in range(4) for h in (g, g + 4)], 0)
    up = np.concatenate([blocks(w[:, g0:g0 + D]), blocks(w[:, g0 + D:g0 + 2 * D]), blocks(w_dn_up[0]), blocks(up_rows)], 2)
    conv = conv_w[0].reshape(12, P, 4).transpose(1, 0, 2).reshape(P, 48)
    row = np.broadcast_to(np.concatenate([dn_dt_bias[0], dn_a_log[0], swa_sinks[0]])[None, :], (P, 16))
    cols = np.concatenate([col(c[0]), col(ada_b[0]), col(norm1_gain[0]), col(norm2_gain[0]), col(final_gain), conv,
                           dn_out_gain[0].reshape(P, 1), row], 1)
    return {
        "c_keep": keep, "c_masks": masks, "p_cols": cols,
        "xT": x[0].T, "ada_w": ada_w[0],
        "w_in": blocks(front), "w_small": small.reshape(DC, P, SMALL).transpose(1, 0, 2),
        "w_up": up, "w_out": blocks(w_out[0]), "w_q": blocks(peer_w_q[0]),
        "sub_k": peer_sub_keys[0].reshape(16, NK, P).transpose(2, 0, 1),
        "u": peer_u[0].reshape(NK, NK, DC, P).transpose(1, 3, 2, 0),
        "v": peer_v[0].reshape(NK, NK, D).transpose(1, 0, 2),
    }


def kernel(**inputs):
    import concourse.bacc as _bacc
    from concourse.bass_utils import run_bass_kernel_spmd as _run

    data = {k: np.ascontiguousarray(v) for k, v in lay_out(**{k: np.asarray(v) for k, v in inputs.items()}).items()}
    nc = _bacc.Bacc("TRN2", target_bir_lowering=False, num_devices=1)
    arrays, args = {}, {}
    for name, v in data.items():
        arrays[f"in_{name}"] = v
        args[name] = nc.dram_tensor(f"in_{name}", list(v.shape), mybir.dt.from_np(v.dtype), kind="ExternalInput").ap()
    out = nc.dram_tensor("out_T", [D, T], F32, kind="ExternalOutput").ap()
    block_kernel(nc, args, out)
    r = _run(nc, [arrays], core_ids=[0])
    return np.ascontiguousarray(r.results[0]["out_T"].T).reshape(1, T, D)
```

```python
from contextlib import ExitStack

import numpy as np
import concourse.bass as bass
from concourse import mybir

P = 128
D = 1024
T = 1024
HALF = 512
DC = D // P
TILES = T // P
CHUNK = 64
EPS = 1e-6
H = 4
QH = 8
HD = 64
IN_JOBS = 21
SMALL = 8 + P
PH = 8
NK = 128
TOPK = 16
GROUP = 2
GROUPS = NK // GROUP
EARLY = 32
PER_TILE = EARLY // TILES
LEAD = EARLY // GROUP
FULL = GROUPS - LEAD
ADA_SLABS = 12
ADA_FIRST = 4
BIG = 1.0e30
LOWEST = -3.0e38

F32 = mybir.dt.float32
F32R = mybir.dt.float32r
U32 = mybir.dt.uint32
ALU = mybir.AluOpType
ACT = mybir.ActivationFunctionType
AX = mybir.AxisListType

CONSTS = ["c_keep", "c_masks"]
PARAMS = ["p_cols", "p_rows"]


def block_kernel(nc, a, out):
    KB = 1024
    base = 16512
    limit = 229368

    def at(name, shape, kb, dtype=F32):
        size = 4 * int(np.prod(shape[1:]))
        off = base + int(kb * KB)
        assert off + size <= limit, (name, off + size - limit)
        return nc.alloc_sbuf_tensor_at(name, list(shape), dtype, offset=off)

    ctx = ExitStack()
    with ctx:
        def sem(name):
            return ctx.enter_context(nc.semaphore(name))

        ps = ctx.enter_context(nc.psum_tensor("ps", [P, 8, 512], F32))

        keep = at("keep", [P, 3 * P], 0)
        ident, iota, ones = keep[:, 0:P], keep[:, P:2 * P], keep[:, 2 * P:3 * P]
        cols = at("cols", [P, 145], 1.5)
        C_, ADAB, G1, G2, GF, CONV, OGAIN = (cols[:, 0:8], cols[:, 8:56], cols[:, 56:64], cols[:, 64:72],
                                             cols[:, 72:80], cols[:, 80:128], cols[:, 128:129])
        rows = cols[:, 129:145]
        mod = at("mod", [P, 48], 2.25)
        silc = at("silc", [P, 8], 2.5)
        amp1 = at("amp1", [P, 8], 2.5625)
        amp2 = at("amp2", [P, 8], 2.625)
        O = 4

        xT = at("xT", [P, DC, T], O + 0)
        hT = at("hT", [P, DC, T], O + 32)
        qkv = at("qkv", [P, 12, T], O + 64)
        zq = at("zq", [P, 8, T], O + 112)
        swk = at("swk", [P, P + T], O + 144)
        vtok = at("vtok", [P, 1 + TILES, P], O + 148.5)
        masks = at("masks", [P, 4 * P + 6 * P + 4 * P], O + 153)
        tri, blk, neg = masks[:, 0:P], masks[:, P:2 * P], masks[:, 2 * P:3 * P]
        level = [masks[:, (3 + s) * P:(4 + s) * P] for s in range(6)]
        wmask = masks[:, 9 * P:11 * P]
        wmask0 = masks[:, 11 * P:13 * P]
        slab = [at("slab_a", [P, 2, DC, 512], O + 64), at("slab_b", [P, 2, DC, 512], O + 0)]
        arow = at("arow", [P, 2, 512], O + 189)
        wjob = at("wjob", [P, 3, DC, P], O + 161)
        sq = at("sq", [P, 2, T], O + 173)
        rstd = at("rstd", [P, 2, T], O + 181)
        pre = at("pre", [P, 3, 3 + T], O + 173)
        cacc = at("cacc", [P, 3, T], O + 185.25)
        wsmall = at("wsmall", [P, DC, SMALL], O + 197.25)
        ab = at("ab", [P, TILES, 8], O + 203)

        def dn(name, k, n=1):
            shape = (P, H, P) if n == 1 else (P, n, H, P)
            return [at(f"{name}{w}", shape, O + (161, 0)[w] + 2 * k) for w in range(2)]
        ldb, btb, kn, qn, vv, gm, gam = [dn(n, k) for k, n in enumerate(["ldb", "btb", "kn", "qn", "vv", "gm", "gam"])]
        egrow, LT, AT, X, XT, t1, vb, kbe = [dn(n, 7 + k) for k, n in enumerate(["egrow", "LT", "AT", "X", "XT", "t1", "vb", "kbe"])]
        vz = dn("vz", 0, 2)
        wT, qdec, kd, u = kn, qn, vv, gam
        lowT = [[gm[w], gam[w]] for w in range(2)]
        St = at("St", [P, H, P], O + 191)
        small = at("small", [P, 12, 32], O + 201.5)
        (adt, aab, lns, ld, beta, gcol, ngcol, dlt, eg, ekd, beg, nea) = [small[:, k, :] for k in range(12)]

        def sw(name, shape, k):
            return [at(f"{name}{w}", shape, O + (161, 0)[w] + k) for w in range(2)]
        qz, vbuf, prob = sw("qz", [P, QH, P], 0), sw("vbuf", [P, 2, P], 4), sw("prob", [P, QH, 2 * P], 6)
        probT, stat = sw("probT", [P, QH, 2, P], 14), sw("stat", [P, 6, QH], 30)
        prob2 = sw("prob2", [P, QH, 2 * P], 22)
        mbuf = at("mbuf", [P, 2 * P], O + 166)

        wup = at("wup", [P, 2, 24, P], O + 161)
        sig = at("sig", [P, 2, 2, HALF], O + 185)
        mtmp = at("mtmp", [P, 2, 2, HALF], O + 193)
        merged = at("merged", [P, DC, T], O + 80)

        qs_hi = at("qs_hi", [P, 2, DC, P], O + 128, F32R)
        qs_lo = at("qs_lo", [P, 2, DC, P], O + 136, F32R)
        qj = at("qj", [P, 2, T], O + 144)
        sj = at("sj", [P, 2, TILES, P], O + 152)
        subk = at("subk", [P, 16, P], O + 192)

        sc = at("sc", [P, 16, P], O + 0)
        sc2 = at("sc2", [P, 16, P], O + 8)
        eqa = at("eqa", [P, PH, TOPK, TOPK], O + 16)
        oneL = at("oneL", [P, 8, P], O + 24)
        oneR = at("oneR", [P, 8, P], O + 28)
        Gsb = at("Gsb", [P, NK, P], O + 128)
        sv = at("sv", [P, 16, TOPK], O + 192)
        si = at("si", [P, 16, TOPK], O + 193, U32)
        sif = at("sif", [P, 16, TOPK], O + 194)
        cv = at("cv", [P, PH, TOPK], O + 195)
        ci = at("ci", [P, PH, TOPK], O + 195.5, U32)
        cab = at("cab", [P, 2, PH * TOPK], O + 196, U32)
        cabf = at("cabf", [P, 2, PH * TOPK], O + 197)
        pick = at("pick", [P, 3, PH * TOPK], O + 198)
        rT = at("rT", [P, 3, P], O + 199.5)
        gsum = at("gsum", [P, 2, PH], O + 201)
        carrier = at("carrier", [P, 2], O + 202)

        acc = at("acc", [P, DC, T], O + 0)
        ust = at("ust", [P, 2, DC, P], O + 32)
        uhi = at("uhi", [P, 2, DC, P], O + 40, F32R)
        ulo = at("ulo", [P, 2, DC, P], O + 48, F32R)
        actb = at("actb", [P, 2, T], O + 56)
        h2hi = at("h2hi", [P, DC, T], O + 64, F32R)
        h2lo = at("h2lo", [P, DC, T], O + 96, F32R)
        vst = at("vst", [P, 2, D], O + 128)
        gst = at("gst", [P, 2, T], O + 136)
        vhi = at("vhi", [P, 2, D], O + 144, F32R)
        vlo = at("vlo", [P, 2, D], O + 152, F32R)
        whi = at("whi", [P, 2, 2, T], O + 160, F32R)
        wlo = at("wlo", [P, 2, 2, T], O + 176, F32R)
        wbuf = at("wbuf", [P, 2, T], O + 192)

        x2 = at("x2", [P, DC, T], O + 64)
        oT = at("oT", [P, DC, T], O + 96)
        esq = at("esq", [P, 2, T], O + 128)
        erstd = at("erstd", [P, 2, T], O + 136)

        x2_dram = nc.dram_tensor("x2_scratch", [D, T], F32, kind="Internal").ap()
        s_dram = nc.dram_tensor("score_scratch", [TILES, P, 16, NK], F32, kind="Internal").ap()
        a_dram = nc.dram_tensor("act_scratch", [EARLY, P, T], F32, kind="Internal").ap()
        g_dram = nc.dram_tensor("gate_scratch", [NK, NK, T], F32, kind="Internal").ap()

        const_in, x_in, small_in, subk_in = sem("const_in"), sem("x_in"), sem("small_in"), sem("subk_in")
        slab_in = [sem(f"slab_in{s}") for s in range(2)]
        score_in, x_back = sem("score_in"), sem("x_back")
        score_out = [sem(f"score_out{s}") for s in range(2)]
        act_out = [sem(f"act_out{s}") for s in range(2)]
        act_in = [sem(f"act_in{s}") for s in range(2)]
        wjob_in = [sem(f"wjob_in{s}") for s in range(3)]
        wup_in = [sem(f"wup_in{s}") for s in range(2)]
        wout_in = [sem(f"wout_in{s}") for s in range(2)]
        wq_in = [sem(f"wq_in{s}") for s in range(2)]
        ust_in = [sem(f"ust_in{s}") for s in range(2)]
        vst_in = [sem(f"vst_in{s}") for s in range(2)]
        gst_in = [sem(f"gst_in{s}") for s in range(2)]
        x2_out, x2_in, g_out, y_out = sem("x2_out"), sem("x2_in"), sem("g_out"), sem("y_out")
        silc_ready, ada_mm, ada_row, ada_col, ada_add, mod_ready = (sem("silc_ready"), sem("ada_mm"), sem("ada_row"),
                                                                    sem("ada_col"), sem("ada_add"), sem("mod_ready"))
        nsq = [sem(f"norm{k}_squared") for k in range(3)]
        nmm = [sem(f"norm{k}_summed") for k in range(3)]
        nrt = [sem(f"norm{k}_root") for k in range(3)]
        nsc = [sem(f"norm{k}_scaled") for k in range(3)]
        nout = [sem(f"norm{k}_out") for k in range(3)]
        in_mm, in_copied, conv_step, conv_done, qkv_ready = (sem("in_mm"), sem("in_copied"), sem("conv_step"),
                                                             sem("conv_done"), sem("qkv_ready"))
        pads_zero, sm_mm, sm_copied = sem("pads_zero"), sem("sm_mm"), sem("sm_copied")
        l2_sq, l2_mm, l2_root, l2_inv, l2_done = sem("l2_sq"), sem("l2_mm"), sem("l2_root"), sem("l2_inv"), sem("l2_done")
        gate_vec, gate_act, gate_mm = sem("gate_vec"), sem("gate_act"), sem("gate_mm")
        dn_vec, dn_act, dn_mm, dn_pool = [[sem(f"dn_{n}{w}") for w in range(2)] for n in ("vec", "act", "mm", "pool")]
        sw_vec, sw_act, sw_mm = [[sem(f"sw_{n}{w}") for w in range(2)] for n in ("vec", "act", "mm")]
        gn_sq, gn_mm, gn_root, gn_vec, z_silu = sem("gn_sq"), sem("gn_mm"), sem("gn_root"), sem("gn_vec"), sem("z_silu")
        up_mm, up_sig, up_vec, up_done = sem("up_mm"), sem("up_sig"), sem("up_vec"), sem("up_done")
        wo_mm, x2_done = sem("wo_mm"), sem("x2_done")
        q_hi, q_lo, q_mm, q_copied, s_mm, s_copied = (sem("q_hi"), sem("q_lo"), sem("q_mm"), sem("q_copied"),
                                                      sem("s_mm"), sem("s_copied"))
        rt_vec, rt_pool, rt_exp, rt_mm = sem("rt_vec"), sem("rt_pool"), sem("rt_exp"), sem("rt_mm")
        left_ready, right_ready, g_mm, g_copied = sem("left_ready"), sem("right_ready"), sem("g_mm"), sem("g_copied")
        h2_hi, h2_lo, acc_zero = sem("h2_hi"), sem("h2_lo"), sem("acc_zero")
        uhi_ready, u_ready, u_mm, act_ready, w_ready, whi_ready, wlo_ready = (
            sem("uhi_ready"), sem("u_ready"), sem("u_mm"), sem("act_ready"), sem("w_ready"), sem("whi_ready"), sem("wlo_ready"))
        vhi_ready, v_ready, v_mm, flushed = sem("vhi_ready"), sem("v_ready"), sem("v_mm"), sem("flushed")
        x3_done = sem("x3_done")

        block = ctx.enter_context(nc.Block())

        DNV, DNA, DNM, DNG = 30, 14, 24, 11
        SWV, SWA_, SWM = (12, 11), 5, 3
        RTV = 25
        G_PER_TILE = P

        def halves(ap3, bank):
            return ps[:, bank:bank + 2, :].rearrange("p b n -> p (b n)")

        @block.sync
        def _(sp):
            sp.dma_start(keep[:], a["c_keep"]).then_inc(const_in, 16)
            sp.dma_start(cols[:], a["p_cols"]).then_inc(const_in, 16)
            sp.dma_start(masks[:, 0:13 * P], a["c_masks"]).then_inc(const_in, 16)
            sp.dma_start(xT[:], a["xT"].rearrange("(c p) t -> p c t", p=P)).then_inc(x_in, 16)
            ada = a["ada_w"].rearrange("(k p) n -> p k n", p=P)

            def load_slab(n):
                if n >= 2:
                    sp.wait_ge(ada_mm, n - 1)
                sp.dma_start(slab[n >= ADA_FIRST][:, n % 2], ada[:, :, n * 512:(n + 1) * 512]).then_inc(slab_in[n % 2], 16)
            for n in range(ADA_FIRST):
                load_slab(n)
            sp.dma_start(wsmall[:], a["w_small"]).then_inc(small_in, 16)
            with sp.Fori(0, IN_JOBS // 3) as i:
                for s in range(3):
                    sp.wait_ge(in_mm, 1 + 3 * i)
                    sp.dma_start(wjob[:, s], a["w_in"][bass.ds(3 * i + s, 1)].rearrange("o p k m -> p (o k) m")).then_inc(wjob_in[s], 16)
            sp.wait_ge(nout[0], DC)
            for n in range(ADA_FIRST, ADA_SLABS):
                load_slab(n)
            sp.wait_ge(gn_vec, 2 * H)
            with sp.Fori(0, DC // 2) as i:
                for s in range(2):
                    sp.wait_ge(up_mm, 1 + 4 * i)
                    sp.dma_start(wup[:, s], a["w_up"][bass.ds(2 * i + s, 1)].rearrange("o p k m -> p (o k) m")).then_inc(wup_in[s], 16)
            sp.dma_start(xT[:], a["xT"].rearrange("(c p) t -> p c t", p=P)).then_inc(x_back, 16)
            sp.wait_ge(up_mm, 1 + 2 * DC)
            with sp.Fori(0, DC // 2) as i:
                for s in range(2):
                    sp.wait_ge(wo_mm, 1 + 2 * i)
                    sp.dma_start(wjob[:, s], a["w_out"][bass.ds(2 * i + s, 1)].rearrange("o p k m -> p (o k) m")).then_inc(wout_in[s], 16)
            sp.wait_ge(x2_done, 1 + DC)
            sp.dma_start(subk[:], a["sub_k"]).then_inc(subk_in, 16)
            sp.dma_start(x2_dram.rearrange("(c p) t -> p c t", p=P), xT[:]).then_inc(x2_out, 16)
            def load_q(i, s):
                sp.dma_start(wjob[:, s], a["w_q"][bass.ds(2 * i + s, 1)].rearrange("o p k m -> p (o k) m")).then_inc(wq_in[s], 16)

            def store_scores(i):
                for s in range(2):
                    sp.wait_ge(s_copied, 1 + 2 * i + s + 1)
                    sp.dma_start(s_dram[:, :, bass.ds(2 * i + s, 1), :].rearrange("t p o n -> p t (o n)"), sj[:, s]).then_inc(score_out[s], 16)
            for s in range(2):
                load_q(0, s)
            with sp.Fori(0, 7) as i:
                for s in range(2):
                    sp.wait_ge(q_lo, 2 * i + s + 1)
                    load_q(i + 1, s)
                store_scores(i)
            store_scores(7)
            sp.wait_ge(x2_out, 16)
            for s in range(2):
                sp.wait_ge(score_out[s], 16 + 16 * 8)

            def load_u(n, s, first=False):
                if not first:
                    sp.wait_ge(uhi_ready, n - 1)
                    sp.wait_ge(u_ready, n - 1)
                sp.dma_start(ust[:, s], a["u"][bass.ds(n, 1)].rearrange("o p k m -> p (o k) m")).then_inc(ust_in[s], 16)

            def load_gate(j, g, s, first=False):
                if not first:
                    sp.wait_ge(w_ready, 2 * j + s - 1)
                sp.dma_start(gst[:, s], g_dram[bass.ds(2 * g + s, 1)].rearrange("o i t -> (o i) t")).then_inc(gst_in[s], 16)

            def load_v(j, g, s, first=False):
                if not first:
                    sp.wait_ge(vhi_ready, 2 * j + s - 1)
                    sp.wait_ge(v_ready, 2 * j + s - 1)
                sp.dma_start(vst[:, s], a["v"][bass.ds(2 * g + s, 1)].rearrange("o p n -> (o p) n")).then_inc(vst_in[s], 16)

            sp.wait_ge(h2_lo, DC)
            load_u(0, 0, True)
            load_u(1, 1, True)
            sp.dma_start(sc[:], s_dram[0]).then_inc(score_in, 16)
            with sp.Fori(0, TILES) as i:
                for k in range(PER_TILE):
                    n, s = PER_TILE * i + k, k % 2
                    load_u(n + 2, s)
                    sp.wait_ge(act_ready, n + 3)
                    sp.dma_start(a_dram[bass.ds(n, 1)].rearrange("o p t -> (o p) t"), actb[:, s]).then_inc(act_out[s], 16)
                sp.wait_ge(rt_vec, 1 + RTV * i + 12)
                sp.dma_start(sc[:], s_dram[bass.ds((i + 1) % TILES, 1)].rearrange("o p j n -> (o p) j n")).then_inc(score_in, 16)
            sp.wait_ge(score_in, 16 * (TILES + 1))
            for s in range(2):
                sp.wait_ge(act_out[s], 16 + 16 * EARLY // 2)
            sp.wait_ge(g_out, 16 + 16 * TILES)
            for s in range(2):
                load_gate(0, LEAD, s, True)
            for s in range(2):
                load_v(0, LEAD, s, True)
            with sp.Fori(1, FULL) as j:
                for s in range(2):
                    load_u(2 * (LEAD + j) + s, s)
                    load_gate(j, LEAD + j, s)
                for s in range(2):
                    load_v(j, LEAD + j, s)
            with sp.Fori(FULL, GROUPS) as j:
                for s in range(2):
                    sp.wait_ge(w_ready, 2 * j + s - 1)
                    sp.dma_start(actb[:, s], a_dram[bass.ds(2 * (j - FULL) + s, 1)].rearrange("o p t -> (o p) t")).then_inc(act_in[s], 16)
                    load_gate(j, j - FULL, s)
                for s in range(2):
                    load_v(j, j - FULL, s)
            sp.wait_ge(v_mm, 16 * GROUPS)
            sp.dma_start(x2[:], x2_dram.rearrange("(c p) t -> p c t", p=P)).then_inc(x2_in, 16)
            sp.wait_ge(nout[2], DC)
            sp.dma_start(out.rearrange("(c p) t -> p c t", p=P), oT[:]).then_inc(y_out, 16)
            sp.wait_ge(y_out, 16)

        @block.gpsimd
        def _(pool):
            for q in (in_mm, up_mm, wo_mm, q_mm, in_copied, l2_root, l2_done, up_done, x2_done, q_copied, rt_vec,
                      conv_done, qkv_ready, l2_mm, l2_inv, s_copied, s_mm, *dn_act, *dn_vec, *dn_mm, *sw_act, *sw_mm, *sw_vec):
                pool.nop().then_inc(q, 1)
            for q in (g_out, *act_out, *score_out):
                pool.nop().then_inc(q, 16)
            pool.wait_ge(gate_vec, 9)
            with pool.Fori(0, TILES // 2) as i:
                g0, v0, m0 = DNG * i, DNV * i, DNM * i

                def over_n(col, t):
                    return col[:, bass.ds(H * t, H)].unsqueeze(2).to_broadcast([P, H, P])

                def level_mask(w, s):
                    if s == 0:
                        pool.wait_ge(dn_vec[w], 1 + v0 + 5)
                    elif s == 2:
                        pool.wait_ge(dn_vec[w], 1 + v0 + 11)
                    elif s > 2:
                        pool.wait_ge(dn_mm[w], 1 + m0 + 2 + 2 * s)
                    pool.tensor_tensor(lowT[w][s % 2][:], LT[w][:], level[s].unsqueeze(1).to_broadcast([P, H, P]),
                                       ALU.mult).then_inc(dn_pool[w], 1)
                for w in range(2):
                    t = 2 * i + w
                    tok = bass.ds(t * P, P)
                    pool.wait_ge(dn_mm[w], 1 + m0)
                    pool.tensor_copy(ldb[w][:], over_n(ld, t)).then_inc(dn_pool[w], 1)
                    pool.tensor_copy(btb[w][:], over_n(beta, t)).then_inc(dn_pool[w], 1)
                    pool.tensor_copy(kn[w][:], qkv[:, H:2 * H, tok]).then_inc(dn_pool[w], 1)
                    pool.tensor_copy(vv[w][:], qkv[:, 2 * H:3 * H, tok]).then_inc(dn_pool[w], 1)
                for s in range(2):
                    for w in range(2):
                        level_mask(w, s)
                for w in range(2):
                    pool.memset(vz[w][:], 0.0).then_inc(dn_pool[w], 1)
                for s in range(2, 6):
                    for w in range(2):
                        level_mask(w, s)
            with pool.Fori(0, TILES) as i:
                shape = [P, PH, TOPK, TOPK]
                pool.wait_ge(rt_vec, 1 + RTV * i + 17)
                sif4 = sif[:].rearrange("p (h two) k -> p h two k", two=2)
                pool.tensor_tensor(eqa[:], eqa[:], sif4[:, :, 0, :].unsqueeze(2).to_broadcast(shape), ALU.mult).then_inc(rt_pool, 1)
            pool.wait_ge(g_mm, 8 + T)
            pool.wait_ge(score_in, 16 * (TILES + 1))
            pool.memset(acc[:], 0.0).then_inc(acc_zero, 1)

        @block.tensor
        def _(pe):
            pe.nop().then_inc(g_mm, 8)

            def ada_slab(n, bank):
                pe.wait_ge(slab_in[n % 2], 16 * (n // 2) + 16)
                if n >= 2:
                    pe.wait_ge(ada_row, n - 1)
                for k in range(DC):
                    mm = pe.matmul(ps[0:1, bank + n % 2, :], silc[:, k:k + 1], slab[n >= ADA_FIRST][:, n % 2, k, :],
                                   start=(k == 0), stop=(k == DC - 1))
                mm.then_inc(ada_mm, 1)

            def ada_turn(n, bank):
                pe.wait_ge(ada_row, n + 1)
                if n >= 2:
                    pe.wait_ge(ada_add, n - 1)
                for m in range(4):
                    mm = pe.matmul(ps[:, bank + n % 2, m:m + 1], arow[0:1, n % 2, m * P:(m + 1) * P], ones[0:1, 0:1],
                                   start=True, stop=True)
                mm.then_inc(ada_col, 1)

            def ada(n0, n1, bank_a, bank_b):
                for n in range(n0, n1):
                    ada_slab(n, bank_a)
                    if n > n0:
                        ada_turn(n - 1, bank_b)
                ada_turn(n1 - 1, bank_b)

            def norm_sum(n, src):
                for c in range(DC):
                    pe.wait_ge(nsq[n], c + 1)
                    for h in range(2):
                        mm = pe.matmul(ps[:, 6 + h, :], ones, src[:, c % 2, h * HALF:(h + 1) * HALF],
                                       start=(c == 0), stop=(c == DC - 1))
                    mm.then_inc(nmm[n], 1)

            norm_sum(0, sq)
            pe.wait_ge(silc_ready, 1)
            ada(0, ADA_FIRST, 0, 2)

            pe.wait_ge(nout[0], DC)
            with pe.Fori(0, IN_JOBS // 3) as i:
                for s in range(3):
                    pe.wait_ge(wjob_in[s], 16 * i + 16)
                    pe.wait_ge(in_copied, 1 + 3 * i)
                    for h in range(2):
                        for k in range(DC):
                            mm = pe.matmul(ps[:, 2 * s + h, :], wjob[:, s, k, :], hT[:, k, h * HALF:(h + 1) * HALF],
                                           start=(k == 0), stop=(k == DC - 1))
                    mm.then_inc(in_mm, 1)
            pe.wait_ge(small_in, 16)
            for t in range(TILES):
                if t >= 2:
                    pe.wait_ge(sm_copied, 2 * (t - 1))
                else:
                    pe.wait_ge(nrt[0], 1)
                for k in range(DC):
                    mm = pe.matmul(ps[:, 6 + t % 2, 0:SMALL], hT[:, k, t * P:(t + 1) * P], wsmall[:, k, :],
                                   start=(k == 0), stop=(k == DC - 1))
                mm.then_inc(sm_mm, 1)
            pe.wait_ge(in_copied, 1 + IN_JOBS)
            ada(ADA_FIRST, ADA_SLABS, 0, 2)
            pe.wait_ge(ada_add, ADA_SLABS)
            with pe.Fori(0, 4) as i:
                for s in range(2):
                    pe.wait_ge(l2_sq, 2 * i + s + 1)
                    pe.wait_ge(l2_root, 1 + 2 * i)
                    for h in range(2):
                        mm = pe.matmul(ps[:, 2 * s + h, :], ones, sq[:, s, h * HALF:(h + 1) * HALF], start=True, stop=True)
                    mm.then_inc(l2_mm, 1)
            pe.wait_ge(gate_vec, 4)
            pe.wait_ge(l2_root, 1 + 8)
            pe.matmul(ps[:, 0, 0:32], tri, ld, start=True, stop=True)
            pe.matmul(ps[:, 0, 32:64], blk, ld, start=True, stop=True).then_inc(gate_mm, 1)

            pe.wait_ge(gate_vec, 9)

            def heads(bank, f):
                for h in range(H):
                    m = f(h, ps[:, bank, h * P:(h + 1) * P])
                return m

            with pe.Fori(0, TILES // 2) as i:
                v0, a0, m0, g0 = DNV * i, DNA * i, DNM * i, DNG * i
                for w in range(2):
                    b = 4 * w
                    pe.wait_ge(dn_act[w], 1 + a0)
                    pe.wait_ge(dn_vec[w], 1 + v0)
                    pe.wait_ge(dn_pool[w], g0 + 1)
                    heads(b, lambda h, o: pe.matmul(o, ldb[w][:, h], tri, start=True, stop=True)).then_inc(dn_mm[w], 1)
                    pe.wait_ge(dn_pool[w], g0 + 2)
                    heads(b + 1, lambda h, o: pe.matmul(o, btb[w][:, h], ident, start=True, stop=True)).then_inc(dn_mm[w], 1)
                    pe.wait_ge(dn_pool[w], g0 + 3)
                    heads(b + 2, lambda h, o: pe.matmul(o, kn[w][:, h], kn[w][:, h], start=True, stop=True)).then_inc(dn_mm[w], 1)
                    pe.wait_ge(dn_vec[w], 1 + v0 + 1)
                    heads(b + 3, lambda h, o: pe.matmul(o, kn[w][:, h], qn[w][:, h], start=True, stop=True)).then_inc(dn_mm[w], 1)
                for w in range(2):
                    pe.wait_ge(dn_act[w], 1 + a0 + 1)
                    pe.wait_ge(dn_vec[w], 1 + v0 + 2)
                    heads(4 * w, lambda h, o: pe.transpose(o, kn[w][:, h], ident)).then_inc(dn_mm[w], 1)
                for w in range(2):
                    pe.wait_ge(dn_pool[w], g0 + 4)
                    pe.wait_ge(dn_vec[w], 1 + v0 + 4)
                    heads(4 * w + 3, lambda h, o: pe.transpose(o, vv[w][:, h], ident)).then_inc(dn_mm[w], 1)
                for w in range(2):
                    pe.wait_ge(dn_pool[w], g0 + 5)
                    heads(4 * w + 1, lambda h, o: pe.transpose(o, lowT[w][0][:, h], ident)).then_inc(dn_mm[w], 1)
                for s in range(1, 6):
                    for w in range(2):
                        pe.wait_ge(dn_pool[w], g0 + (6 if s == 1 else 6 + s))
                        pe.wait_ge(dn_vec[w], 1 + v0 + 9 + 2 * s)
                        heads(4 * w + 1, lambda h, o: pe.matmul(o, lowT[w][s % 2][:, h], X[w][:, h], start=True, stop=True)).then_inc(dn_mm[w], 1)
                    for w in range(2):
                        pe.wait_ge(dn_act[w], 1 + a0 + 5 + s)
                        if s < 5:
                            heads(4 * w + 2, lambda h, o: pe.matmul(o, XT[w][:, h], t1[w][:, h], start=True, stop=True))
                        heads(4 * w + 3, lambda h, o: pe.matmul(o, t1[w][:, h], XT[w][:, h], start=True, stop=True)).then_inc(dn_mm[w], 1)
                for w in range(2):
                    pe.wait_ge(dn_vec[w], 1 + v0 + 20)
                    heads(4 * w, lambda h, o: pe.matmul(o, XT[w][:, h], vb[w][:, h], start=True, stop=True))
                    heads(4 * w + 1, lambda h, o: pe.matmul(o, kbe[w][:, h], XT[w][:, h], start=True, stop=True)).then_inc(dn_mm[w], 1)
                for w in range(2):
                    b = 4 * w
                    pe.wait_ge(dn_act[w], 1 + a0 + 12)
                    for c in range(2):
                        lo = c * CHUNK
                        if c:
                            pe.wait_ge(dn_vec[w], 1 + v0 + 25)
                            pe.wait_ge(dn_act[w], 1 + a0 + 13)
                        elif w:
                            pe.wait_ge(dn_vec[0], 1 + v0 + DNV)
                        else:
                            pe.wait_ge(dn_vec[1], 1 + v0)
                        heads(b + 2, lambda h, o: pe.matmul(o, wT[w][:, h], St[:, h], start=True, stop=True)).then_inc(dn_mm[w], 1)
                        pe.wait_ge(dn_vec[w], 1 + v0 + 21 + 5 * c)
                        for h in range(H):
                            o = ps[:, b + 3, h * CHUNK:(h + 1) * CHUNK]
                            pe.matmul(o, St[:, h], qdec[w][:, h, lo:lo + CHUNK], start=True, stop=False)
                            pe.matmul(o, vz[w][:, c, h], AT[w][:, h, lo:lo + CHUNK], start=False, stop=True)
                        heads(b, lambda h, o: pe.matmul(o, kd[w][:, h], vz[w][:, c, h], start=True, stop=True)).then_inc(dn_mm[w], 2)

            for w in range(2):
                pe.wait_ge(dn_act[w], 1 + DNA * TILES // 2)
                pe.wait_ge(dn_vec[w], 1 + DNV * TILES // 2)
            with pe.Fori(0, TILES // 2) as i:
                a0 = SWA_ * i
                for w in range(2):
                    pe.wait_ge(sw_act[w], 1 + a0)
                    pe.wait_ge(sw_vec[w], 1 + SWV[w] * i + 3)
                    for h in range(QH):
                        mm = pe.matmul(ps[:, 4 * w + h // 2, (h % 2) * 256:(h % 2) * 256 + 256], qz[w][:, h],
                                       swk[:, bass.ds((2 * i + w) * P, 2 * P)], start=True, stop=True)
                    mm.then_inc(sw_mm[w], 1)
                for w in range(2):
                    pe.wait_ge(sw_vec[w], 1 + SWV[w] * i + 11)
                    for h in range(QH):
                        for b in range(2):
                            j = 2 * h + b
                            mm = pe.transpose(ps[:, 4 * w + j // 4, (j % 4) * P:(j % 4 + 1) * P], prob2[w][:, h, b * P:(b + 1) * P], ident)
                    mm.then_inc(sw_mm[w], 1)
                for w in range(2):
                    pe.wait_ge(sw_act[w], 1 + a0 + 3)
                    for h in range(QH):
                        for b in range(2):
                            mm = pe.matmul(ps[:, 4 * w + h // 4, (h % 4) * P:(h % 4 + 1) * P], vbuf[w][:, b], probT[w][:, h, b],
                                           start=(b == 0), stop=(b == 1))
                    mm.then_inc(sw_mm[w], 1)

            for w in range(2):
                pe.wait_ge(sw_act[w], 1 + SWA_ * TILES // 2)
            for c in range(H):
                pe.wait_ge(gn_sq, c + 1)
                if c >= 2:
                    pe.wait_ge(gn_root, 2 * (c - 1))
                for h in range(2):
                    mm = pe.matmul(ps[:, 2 * (c % 2) + h, :], ones, sq[:, c % 2, h * HALF:(h + 1) * HALF], start=True, stop=True)
                mm.then_inc(gn_mm, 1)

            pe.wait_ge(gn_vec, 2 * H)
            with pe.Fori(0, DC // 2) as i:
                for s in range(2):
                    pe.wait_ge(wup_in[s], 16 * i + 16)
                    for h in range(2):
                        if s == 0:
                            pe.wait_ge(up_done, 1 + 4 * i)
                        else:
                            pe.wait_ge(up_done, 1 + 4 * i + 1 + h)
                        tok = slice(h * HALF, (h + 1) * HALF)
                        for bank, w0, n, src in ((0, 0, DC, hT), (1, 8, DC, hT), (2, 16, H, qkv), (3, 20, H, zq)):
                            for k in range(n):
                                x = src[:, 4 + k, tok] if src is zq else src[:, k, tok]
                                mm = pe.matmul(ps[:, 4 * h + bank, :], wup[:, s, w0 + k, :], x, start=(k == 0), stop=(k == n - 1))
                        mm.then_inc(up_mm, 1)

            def project(n, w_in_sem, done, read, x, step):
                with pe.Fori(0, n) as i:
                    for s in range(2):
                        pe.wait_ge(w_in_sem[s], 16 * i + 16)
                        pe.wait_ge(read, 1 + 2 * i)
                        for h in range(2):
                            for k in range(DC):
                                mm = pe.matmul(ps[:, 2 * s + h, :], wjob[:, s, k, :], x[:, k, h * HALF:(h + 1) * HALF],
                                               start=(k == 0), stop=(k == DC - 1))
                        mm.then_inc(done, 1)

            pe.wait_ge(up_done, 1 + 2 * DC)
            project(DC // 2, wout_in, wo_mm, x2_done, merged, 2)
            norm_sum(1, sq)
            pe.wait_ge(nout[1], DC)

            pe.wait_ge(subk_in, 16)
            pe.wait_ge(h2_lo, DC)
            with pe.Fori(0, 8) as i:
                for s in range(2):
                    n = 2 * i + s
                    pe.wait_ge(q_lo, n + 1)
                    pe.wait_ge(q_copied, 1 + 2 * i)
                    for h in range(2):
                        tok = slice(h * HALF, (h + 1) * HALF)
                        for k in range(DC):
                            o = ps[:, 2 * s + h, :]
                            pe.matmul(o, qs_hi[:, s, k], h2hi[:, k, tok], start=(k == 0), stop=False)
                            pe.matmul(o, qs_hi[:, s, k], h2lo[:, k, tok], start=False, stop=False)
                            mm = pe.matmul(o, qs_lo[:, s, k], h2hi[:, k, tok], start=False, stop=(k == DC - 1))
                    mm.then_inc(q_mm, 1)
                for s in range(2):
                    n = 2 * i + s
                    pe.wait_ge(q_copied, 1 + n + 1)
                    pe.wait_ge(s_copied, 1 + 2 * i)
                    for t in range(TILES):
                        mm = pe.matmul(ps[:, 4 + 2 * s + t // 4, (t % 4) * P:(t % 4 + 1) * P], qj[:, s, t * P:(t + 1) * P],
                                       subk[:, bass.ds(n, 1), :].rearrange("p o n -> p (o n)"), start=True, stop=True)
                    mm.then_inc(s_mm, 1)

            def u_block(n, s, first=False):
                pe.wait_ge(u_ready, n + 1)
                if not first:
                    pe.wait_ge(act_ready, n + 1)
                for h in range(2):
                    tok = slice(h * HALF, (h + 1) * HALF)
                    for k in range(DC):
                        o = ps[:, 2 * s + h, :]
                        pe.matmul(o, uhi[:, s, k], h2hi[:, k, tok], start=(k == 0), stop=False)
                        pe.matmul(o, uhi[:, s, k], h2lo[:, k, tok], start=False, stop=False)
                        mm = pe.matmul(o, ulo[:, s, k], h2hi[:, k, tok], start=False, stop=(k == DC - 1))
                mm.then_inc(u_mm, 1)

            def v_group(j, par, hi, lo, first=False):
                pe.wait_ge(wlo_ready, 2 * j + 2)
                pe.wait_ge(v_ready, 2 * j + 2)
                for b in range(16):
                    c, h = b // 2, b % 2
                    tok = slice(h * HALF, (h + 1) * HALF)
                    if not (first and b < 4):
                        pe.wait_ge(flushed, 16 * j + b - 3)
                    o = ps[:, 4 + b % 4, :]
                    for s in range(2):
                        vh, vl = hi(s)[:, c * P:(c + 1) * P], lo(s)[:, c * P:(c + 1) * P]
                        pe.matmul(o, vh, whi[:, par, s, tok], start=(s == 0), stop=False)
                        pe.matmul(o, vh, wlo[:, par, s, tok], start=False, stop=False)
                        mm = pe.matmul(o, vl, whi[:, par, s, tok], start=False, stop=(s == 1))
                    mm.then_inc(v_mm, 1)

            pe.wait_ge(s_copied, 1 + 16)
            with pe.Fori(0, TILES) as i:
                for k in range(PER_TILE):
                    n = PER_TILE * i + k
                    pe.wait_ge(u_ready, n + 1)
                    pe.wait_ge(act_ready, n + 1)
                    for h in range(2):
                        tok = slice(h * HALF, (h + 1) * HALF)
                        for kk in range(DC):
                            o = ps[:, 2 * (k % 2) + h, :]
                            pe.matmul(o, uhi[:, k % 2, kk], h2hi[:, kk, tok], start=(kk == 0), stop=False)
                            pe.matmul(o, uhi[:, k % 2, kk], h2lo[:, kk, tok], start=False, stop=False)
                            mm = pe.matmul(o, ulo[:, k % 2, kk], h2hi[:, kk, tok], start=False, stop=(kk == DC - 1))
                    mm.then_inc(u_mm, 1)
                pe.wait_ge(rt_vec, 1 + RTV * i + RTV - 1)
                pe.wait_ge(g_copied, 32 * i + 4)
                for j in range(3):
                    mm = pe.transpose(ps[:, 4, j * P:(j + 1) * P], pick[:, j, :], ident)
                mm.then_inc(rt_mm, 1)
                with pe.Fori(0, P // 16) as j:
                    n0 = 16 * (8 * i + j)
                    for t in range(16):
                        if t % 4 == 0:
                            pe.wait_ge(left_ready, n0 + t + 4)
                            pe.wait_ge(g_copied, 4 * (8 * i + j) + t // 4 + 1)
                        pe.wait_ge(right_ready, n0 + t + 1)
                        pe.matmul(ps[:, 4 + t // 4, (t % 4) * P:(t % 4 + 1) * P], oneL[:, t % 8], oneR[:, t % 8],
                                  start=True, stop=True).then_inc(g_mm, 1)

            def v_now(s):
                return vhi[:, s]

            def v_now_lo(s):
                return vlo[:, s]

            def v_alt(s):
                return uhi[:, s].rearrange("p k m -> p (k m)")

            def v_alt_lo(s):
                return ulo[:, s].rearrange("p k m -> p (k m)")

            def u_pair(j):
                for s in range(2):
                    u_block(2 * (LEAD + j) + s, s)

            u_pair(0)
            u_pair(1)
            v_group(0, 0, v_now, v_now_lo, True)
            with pe.Fori(1, FULL // 2) as i:
                for par in range(2):
                    j = 2 * i + par
                    u_pair(j)
                    v_group(j - 1, 1 - par, v_now, v_now_lo)
            v_group(FULL - 1, 1, v_now, v_now_lo)
            with pe.Fori(FULL // 2, GROUPS // 2) as i:
                v_group(2 * i, 0, v_alt, v_alt_lo)
                v_group(2 * i + 1, 1, v_now, v_now_lo)
            norm_sum(2, esq)

        @block.scalar
        def _(act):
            act.wait_ge(const_in, 48)
            act.activation(silc[:], C_, ACT.Silu).then_inc(silc_ready, 1)

            def norm_root(n, x, sqb, rt, ready=None, first=0):
                for c in range(DC):
                    if c >= 2:
                        act.wait_ge(nmm[n], c - 1)
                    if ready is not None:
                        act.wait_ge(ready, first + c + 1)
                    act.activation(sqb[:, c % 2], x[:, c], ACT.Square).then_inc(nsq[n], 1)
                act.wait_ge(nmm[n], DC)
                act.activation(rt[:, 0], halves(ps, 6), ACT.Ln, scale=1.0 / D, bias=EPS).then_inc(nrt[n], 1)
                act.wait_ge(nrt[n], 1)
                act.activation(rt[:, 1], rt[:, 0], ACT.Exp, scale=-0.5).then_inc(nrt[n], 1)

            act.nop().then_inc(act_ready, 2)
            act.nop().then_inc(g_copied, 4)
            act.wait_ge(x_in, 16)
            norm_root(0, xT, sq, rstd)

            def ada_rows(n0, n1, bank):
                for n in range(n0, n1):
                    act.wait_ge(ada_mm, n + 1)
                    if n >= 2:
                        act.wait_ge(ada_col, n - 1)
                    act.activation(arow[0:1, n % 2], ps[0:1, bank + n % 2, :], ACT.Copy).then_inc(ada_row, 1)
            ada_rows(0, ADA_FIRST, 0)

            act.wait_ge(pads_zero, 1)
            with act.Fori(0, 4) as i:
                for s in range(3):
                    act.wait_ge(in_mm, 1 + 3 * i + s + 1)
                    act.wait_ge(conv_done, 1 + 3 * i)
                    act.activation(pre[:, s, 3:3 + T], halves(ps, 2 * s), ACT.Copy).then_inc(in_copied, 1)
                for s in range(3):
                    act.wait_ge(conv_done, 1 + 3 * i + s + 1)
                    act.activation(qkv[:, bass.ds(3 * i + s, 1), :].rearrange("p o t -> p (o t)"), cacc[:, s], ACT.Silu).then_inc(qkv_ready, 1)
            with act.Fori(0, 2) as i:
                for s in range(3):
                    act.wait_ge(in_mm, 1 + 12 + 3 * i + s + 1)
                    act.activation(zq[:, bass.ds(3 * i + s, 1), :].rearrange("p o t -> p (o t)"), halves(ps, 2 * s), ACT.Copy).then_inc(in_copied, 1)
            for s in range(3):
                act.wait_ge(in_mm, 1 + 18 + s + 1)
                dst = zq[:, 6 + s] if s < 2 else swk[:, P:P + T]
                act.activation(dst, halves(ps, 2 * s), ACT.Copy).then_inc(in_copied, 1)
            act.wait_ge(conv_done, 1 + 12)
            ada_rows(ADA_FIRST, ADA_SLABS, 0)
            act.wait_ge(qkv_ready, 1 + 12)
            with act.Fori(0, 4) as i:
                for s in range(2):
                    act.wait_ge(l2_mm, 1 + 2 * i)
                    act.wait_ge(l2_done, 1 + 2 * i)
                    act.activation(sq[:, s], qkv[:, bass.ds(2 * i + s, 1), :].rearrange("p o t -> p (o t)"), ACT.Square).then_inc(l2_sq, 1)
                for s in range(2):
                    act.wait_ge(l2_mm, 1 + 2 * i + s + 1)
                    act.wait_ge(l2_inv, 1 + 2 * i)
                    act.activation(sq[:, s], halves(ps, 2 * s), ACT.Ln, bias=EPS).then_inc(l2_root, 1)
                for s in range(2):
                    act.wait_ge(l2_root, 1 + 2 * i + s + 1)
                    act.activation(rstd[:, s], sq[:, s], ACT.Exp, scale=-0.5).then_inc(l2_done, 1)

            act.wait_ge(gate_vec, 1)
            act.activation(aab, adt, ACT.Abs).then_inc(gate_act, 1)
            act.wait_ge(gate_act, 1)
            act.activation(lns, aab, ACT.Exp, scale=-1.0).then_inc(gate_act, 1)
            act.wait_ge(gate_act, 2)
            act.activation(lns, lns, ACT.Ln, bias=1.0).then_inc(gate_act, 1)
            act.activation(nea[:, 0:H], rows[:, H:2 * H], ACT.Exp).then_inc(gate_act, 1)
            act.activation(beta.rearrange("p (t h) -> p t h", h=H), ab[:, :, H:2 * H], ACT.Sigmoid).then_inc(gate_act, 1)
            act.wait_ge(gate_vec, 7)
            act.activation(eg, gcol, ACT.Exp).then_inc(gate_act, 1)
            act.activation(ekd, dlt, ACT.Exp).then_inc(gate_act, 1)

            act.wait_ge(gate_vec, 9)
            def fl3(x):
                return x[:].rearrange("p h n -> p (h n)")

            with act.Fori(0, TILES // 2) as i:
                v0, m0 = DNV * i, DNM * i
                for w in range(2):
                    act.wait_ge(dn_vec[w], 1 + v0 + 2)
                    act.activation(fl3(egrow[w]), ps[:, 4 * w, :], ACT.Exp).then_inc(dn_act[w], 1)
                    for h in range(H):
                        act.activation(gam[w][:, h], gm[w][:, h], ACT.Exp, bias=ngcol[:, bass.ds(H * (2 * i + w) + h, 1)]).then_inc(dn_act[w], 1)
                for s in range(1, 6):
                    for w in range(2):
                        act.wait_ge(dn_mm[w], 1 + m0 + 6 + 2 * s)
                        act.activation(fl3(t1[w]), ps[:, 4 * w + 1, :], ACT.Copy).then_inc(dn_act[w], 1)
                for w in range(2):
                    act.wait_ge(dn_mm[w], 1 + m0 + 18)
                    act.activation(fl3(u[w]), ps[:, 4 * w, :], ACT.Copy).then_inc(dn_act[w], 1)
                    act.activation(fl3(wT[w]), ps[:, 4 * w + 1, :], ACT.Copy).then_inc(dn_act[w], 1)
                for w in range(2):
                    for c in range(2):
                        act.wait_ge(dn_mm[w], 1 + m0 + 21 + 3 * c)
                        act.activation(qkv[:, 0:H, bass.ds((2 * i + w) * P + c * CHUNK, CHUNK)],
                                       ps[:, 4 * w + 3, 0:H * CHUNK].rearrange("p (h n) -> p h n", h=H), ACT.Copy).then_inc(dn_act[w], 1)

            with act.Fori(0, TILES // 2) as i:
                m0 = SWM * i
                for w in range(2):
                    act.wait_ge(sw_vec[w], 1 + SWV[w] * i + 7)
                    act.activation(prob[w][:], prob2[w][:], ACT.Exp).then_inc(sw_act[w], 1)
                    act.activation(stat[w][:, 3], stat[w][:, 2], ACT.Exp).then_inc(sw_act[w], 1)
                for w in range(2):
                    act.wait_ge(sw_mm[w], 1 + m0 + 2)
                    act.activation(probT[w][:].rearrange("p h b n -> p (h b n)"),
                                   ps[:, 4 * w:4 * w + 4, :].rearrange("p b n -> p (b n)"), ACT.Copy).then_inc(sw_act[w], 1)
                for w in range(2):
                    act.wait_ge(sw_mm[w], 1 + m0 + 3)
                    for r in range(2):
                        rr = slice(r * HD, (r + 1) * HD)
                        act.activation(zq[rr, 4:8, bass.ds((2 * i + w) * P, P)], ps[rr, 4 * w + r, :].rearrange("p (h n) -> p h n", h=4),
                                       ACT.Copy).then_inc(sw_act[w], 1)

            for w in range(2):
                act.wait_ge(sw_mm[w], 1 + SWM * TILES // 2)
                act.wait_ge(sw_vec[w], 1 + SWV[w] * TILES // 2)
            for c in range(H):
                act.activation(zq[:, c], zq[:, c], ACT.Silu).then_inc(z_silu, 1)
            for c in range(H):
                if c >= 2:
                    act.wait_ge(gn_mm, c - 1)
                act.activation(sq[:, c % 2], qkv[:, c], ACT.Square).then_inc(gn_sq, 1)
                act.wait_ge(gn_mm, c + 1)
                if c >= 2:
                    act.wait_ge(gn_vec, 2 * (c - 1))
                act.activation(rstd[:, c % 2], halves(ps, 2 * (c % 2)), ACT.Ln, scale=1.0 / P, bias=EPS).then_inc(gn_root, 1)
                act.wait_ge(gn_root, 2 * c + 1)
                act.activation(rstd[:, c % 2], rstd[:, c % 2], ACT.Exp, scale=-0.5).then_inc(gn_root, 1)

            act.wait_ge(gn_vec, 2 * H)
            with act.Fori(0, DC // 2) as i:
                for s in range(2):
                    for h in range(2):
                        n = 2 * (2 * i + s) + h
                        act.wait_ge(up_mm, 1 + n + 1)
                        act.wait_ge(up_done, 1 + 4 * i) if s == 0 else act.wait_ge(up_done, 1 + 4 * i + 1 + h)
                        for b in range(2):
                            act.activation(sig[:, h, b], ps[:, 4 * h + b, :], ACT.Sigmoid).then_inc(up_sig, 1)

            act.wait_ge(up_done, 1 + 2 * DC)
            norm_root(1, xT, sq, rstd, x2_done, 1)

            for c in range(DC):
                act.wait_ge(nout[1], c + 1)
                act.activation(h2hi[:, c], hT[:, c], ACT.Copy).then_inc(h2_hi, 1)
            with act.Fori(0, 8) as i:
                for s in range(2):
                    act.wait_ge(wq_in[s], 16 * i + 16)
                    act.wait_ge(q_mm, 1 + 2 * i)
                    act.activation(qs_hi[:, s].rearrange("p k m -> p (k m)"), wjob[:, s].rearrange("p k m -> p (k m)"), ACT.Copy).then_inc(q_hi, 1)
                for s in range(2):
                    act.wait_ge(q_mm, 1 + 2 * i + s + 1)
                    act.wait_ge(s_mm, 1 + 2 * i)
                    act.activation(qj[:, s], halves(ps, 2 * s), ACT.Copy).then_inc(q_copied, 1)

            def u_high(n, s, landed, first=False):
                act.wait_ge(ust_in[s], landed)
                if not first:
                    act.wait_ge(u_mm, n - 1)
                act.activation(uhi[:, s].rearrange("p k m -> p (k m)"), ust[:, s].rearrange("p k m -> p (k m)"), ACT.Copy).then_inc(uhi_ready, 1)

            def gelu(n, s):
                act.wait_ge(u_mm, n + 1)
                act.activation(actb[:, s], halves(ps, 2 * s), ACT.Gelu).then_inc(act_ready, 1)

            act.wait_ge(q_copied, 1 + 16)
            for s in range(2):
                u_high(s, s, 16, True)
            with act.Fori(0, TILES) as i:
                n = PER_TILE * i
                for k in range(PER_TILE):
                    if k == 3:
                        act.wait_ge(rt_vec, 1 + RTV * i + 16)
                        act.activation(cv[:], cv[:], ACT.Exp).then_inc(rt_exp, 1)
                    act.wait_ge(act_out[k % 2], 16 + 16 * (2 * i + k // 2))
                    gelu(n + k, k % 2)
                    if k < 3:
                        u_high(n + k + 2, k % 2, 16 * (2 * i + (k + 2) // 2 + 1))
                act.wait_ge(g_out, 16 + 16 * i)
                with act.Fori(0, P // 16) as j:
                    for b in range(4):
                        act.wait_ge(g_mm, 8 + 16 * (8 * i + j) + 4 * b + 4)
                        act.activation(Gsb[:, :, bass.ds(16 * j + 4 * b, 4)].rearrange("p e t -> p t e"),
                                       ps[:, 4 + b, :].rearrange("p (t e) -> p t e", t=4), ACT.Copy).then_inc(g_copied, 1)
                act.wait_ge(g_copied, 4 + 32 * (i + 1))
                act.dma_start(g_dram[:, :, bass.ds(i * P, P)].rearrange("j i t -> i j t"), Gsb[:]).then_inc(g_out, 16)
                u_high(n + 5, 1, 16 * (2 * i + 3))

            def w_high(j, s, par, first=False):
                act.wait_ge(w_ready, 2 * j + s + 1)
                if not first:
                    act.wait_ge(v_mm, 16 * (j - 1))
                act.activation(whi[:, par, s], wbuf[:, s], ACT.Copy).then_inc(whi_ready, 1)

            def v_high(j, s, dst, free):
                act.wait_ge(vst_in[s], 16 * j + 16)
                if free is not None:
                    act.wait_ge(v_mm, free)
                act.activation(dst, vst[:, s], ACT.Copy).then_inc(vhi_ready, 1)

            def step(j, par, first=False, second=False, last=False):
                for s in range(2):
                    n = 2 * (LEAD + j) + s
                    if first:
                        act.wait_ge(act_out[s], 16 + 16 * (EARLY // 2))
                    else:
                        act.wait_ge(w_ready, 2 * j + s - 1)
                    gelu(n, s)
                    if not last:
                        u_high(n + 2, s, 16 * (LEAD + j + 2))
                    w_high(j, s, par, first or second)
                for s in range(2):
                    v_high(j, s, vhi[:, s], None if first else 16 * j)

            act.wait_ge(g_out, 16 + 16 * TILES)
            step(0, 0, first=True)
            step(1, 1, second=True)
            with act.Fori(1, FULL // 2 - 1) as i:
                for par in range(2):
                    step(2 * i + par, par)
            step(FULL - 2, 0)
            step(FULL - 1, 1, last=True)
            with act.Fori(FULL // 2, GROUPS // 2) as i:
                for par in range(2):
                    j = 2 * i + par
                    for s in range(2):
                        w_high(j, s, par)
                        dst = vhi[:, s] if par else uhi[:, s].rearrange("p k m -> p (k m)")
                        v_high(j, s, dst, 16 * (j - 1))

            norm_root(2, acc, esq, erstd, x3_done)

        @block.vector
        def _(dve):
            class Chain:

                def __init__(self, first=0):
                    self.first, self.n = first, 0

                def up(self):
                    self.n += 1
                    return 1

                def now(self):
                    return self.first + self.n

            dve.wait_ge(const_in, 48)

            def ada_bias(n0, n1, bank):
                for n in range(n0, n1):
                    dve.wait_ge(ada_col, n + 1)
                    dve.tensor_tensor(mod[:, 4 * n:4 * n + 4], ps[:, bank + n % 2, 0:4], ADAB[:, 4 * n:4 * n + 4],
                                      ALU.add).then_inc(ada_add, 1)
                dve.wait_ge(ada_add, n1)

            ada_bias(0, ADA_FIRST, 2)
            dve.scalar_tensor_tensor(amp1[:], mod[:, 8:16], 1.0, G1, ALU.add, ALU.mult).then_inc(mod_ready, 1)
            dve.wait_ge(mod_ready, 1)

            def norm_apply(n, x, rt, dst, amp, shift):
                dve.wait_ge(nrt[n], 2)
                for c in range(DC):
                    r = dve.scalar_tensor_tensor(dst[:, c], x[:, c], amp[:, c:c + 1], rt[:, 1], ALU.mult, ALU.mult)
                    if shift is None:
                        r.then_inc(nout[n], 1)
                        continue
                    r.then_inc(nsc[n], 1)
                    if c:
                        dve.wait_ge(nsc[n], c)
                        dve.tensor_scalar(dst[:, c - 1], dst[:, c - 1], shift[:, c - 1:c], None, ALU.add).then_inc(nout[n], 1)
                if shift is not None:
                    dve.wait_ge(nsc[n], DC)
                    dve.tensor_scalar(dst[:, DC - 1], dst[:, DC - 1], shift[:, DC - 1:DC], None, ALU.add).then_inc(nout[n], 1)

            norm_apply(0, xT, rstd, hT, amp1, mod[:, 0:8])

            dve.wait_ge(nout[0], DC)
            dve.memset(swk[:, 0:P], 0.0)
            dve.memset(vtok[:, 0], 0.0)
            dve.memset(pre[:, :, 0:3], 0.0).then_inc(pads_zero, 1)
            with dve.Fori(0, 4) as i:
                for s in range(3):
                    dve.wait_ge(in_copied, 1 + 3 * i + s + 1)
                    dve.wait_ge(qkv_ready, 1 + 3 * i)
                    tap = [CONV[:, bass.ds(12 * i + 4 * s + j, 1)] for j in range(4)]
                    dve.tensor_scalar(cacc[:, s], pre[:, s, 0:T], tap[0], None, ALU.mult).then_inc(conv_step, 1)
                    for j in range(1, 4):
                        dve.wait_ge(conv_step, 9 * i + 3 * s + j)
                        r = dve.scalar_tensor_tensor(cacc[:, s], pre[:, s, j:j + T], tap[j], cacc[:, s], ALU.mult, ALU.add)
                        r.then_inc(conv_step if j < 3 else conv_done, 1)
            for t in range(TILES):
                dve.wait_ge(sm_mm, t + 1)
                dve.tensor_copy(ab[:, t], ps[:, 6 + t % 2, 0:8]).then_inc(sm_copied, 1)
                dve.tensor_copy(vtok[:, 1 + t], ps[:, 6 + t % 2, 8:SMALL]).then_inc(sm_copied, 1)
            ada_bias(ADA_FIRST, ADA_SLABS, 2)
            dve.scalar_tensor_tensor(amp2[:], mod[:, 32:40], 1.0, G2, ALU.add, ALU.mult).then_inc(mod_ready, 1)
            dve.wait_ge(mod_ready, 2)
            with dve.Fori(0, 4) as i:
                for s in range(2):
                    dve.wait_ge(l2_done, 1 + 2 * i + s + 1)
                    row = qkv[:, bass.ds(2 * i + s, 1), :].rearrange("p o t -> p (o t)")
                    dve.tensor_tensor(row, row, rstd[:, s], ALU.mult).then_inc(l2_inv, 1)

            def th(x):
                return x.rearrange("p (t h) -> p t h", h=H)
            dve.wait_ge(sm_copied, 2 * TILES)
            dve.tensor_tensor(th(adt), ab[:, :, 0:H], rows[:, 0:H].unsqueeze(1).to_broadcast([P, TILES, H]), ALU.add).then_inc(gate_vec, 1)
            dve.wait_ge(gate_vec, 1)
            dve.wait_ge(gate_act, 4)
            dve.tensor_scalar(adt, adt, 0.0, None, ALU.max).then_inc(gate_vec, 1)
            dve.wait_ge(gate_vec, 2)
            dve.tensor_tensor(adt, adt, lns, ALU.add).then_inc(gate_vec, 1)
            dve.wait_ge(gate_vec, 3)
            dve.scalar_tensor_tensor(th(ld), th(adt), -1.0, nea[:, 0:H].unsqueeze(1).to_broadcast([P, TILES, H]),
                                     ALU.mult, ALU.mult).then_inc(gate_vec, 1)
            dve.wait_ge(gate_mm, 1)
            dve.tensor_copy(gcol, ps[:, 0, 0:32]).then_inc(gate_vec, 1)
            dve.tensor_scalar(ngcol, ps[:, 0, 0:32], -1.0, None, ALU.mult).then_inc(gate_vec, 1)
            dve.wait_ge(gate_vec, 6)
            dve.tensor_tensor(dlt, ps[:, 0, 32:64], gcol, ALU.subtract).then_inc(gate_vec, 1)
            dve.wait_ge(gate_act, 7)
            dve.tensor_tensor(beg, beta, eg, ALU.mult).then_inc(gate_vec, 1)
            dve.memset(St[:], 0.0).then_inc(gate_vec, 1)
            dve.wait_ge(gate_vec, 9)

            def flat(x):
                return x[:].rearrange("p h n -> p (h n)")

            def over_n(col, i):
                return col[:, bass.ds(H * i, H)].unsqueeze(2).to_broadcast([P, H, P])

            def over_h(m):
                return m.unsqueeze(1).to_broadcast([P, H, P])

            with dve.Fori(0, TILES // 2) as i:
                m0, a0, g0 = DNM * i, DNA * i, DNG * i
                chain = [Chain(DNV * i) for w in range(2)]
                bank = [ps[:, b, :].rearrange("p (h n) -> p h n", h=H) for b in range(8)]

                def own(w):
                    dve.wait_ge(dn_vec[w], 1 + chain[w].now())
                for w in range(2):
                    dve.wait_ge(dn_mm[w], 1 + m0)
                    dve.tensor_scalar(qn[w][:], qkv[:, 0:H, bass.ds((2 * i + w) * P, P)], float(P) ** -0.5, None,
                                      ALU.mult).then_inc(dn_vec[w], chain[w].up())
                for w in range(2):
                    dve.wait_ge(dn_mm[w], 1 + m0 + 1)
                    dve.tensor_tensor(gm[w][:], bank[4 * w], over_h(neg), ALU.add).then_inc(dn_vec[w], chain[w].up())
                for w in range(2):
                    c_, t, b = chain[w], 2 * i + w, 4 * w
                    dve.wait_ge(dn_mm[w], 1 + m0 + 4)
                    dve.wait_ge(dn_act[w], 1 + a0 + 5)
                    dve.tensor_tensor(LT[w][:], bank[b + 2], gam[w][:], ALU.mult).then_inc(dn_vec[w], c_.up())
                    dve.tensor_tensor(AT[w][:], bank[b + 3], gam[w][:], ALU.mult).then_inc(dn_vec[w], c_.up())
                    own(w)
                    dve.tensor_tensor(LT[w][:], LT[w][:], bank[b + 1], ALU.mult).then_inc(dn_vec[w], c_.up())
                for w in range(2):
                    c_, t, b = chain[w], 2 * i + w, 4 * w
                    dve.wait_ge(dn_mm[w], 1 + m0 + 6)
                    dve.tensor_tensor(kbe[w][:], bank[b], over_n(beg, t), ALU.mult).then_inc(dn_vec[w], c_.up())
                    dve.tensor_tensor(vb[w][:], bank[b + 3], over_n(beta, t), ALU.mult).then_inc(dn_vec[w], c_.up())
                    dve.tensor_tensor(kd[w][:], bank[b], over_n(ekd, t), ALU.mult).then_inc(dn_vec[w], c_.up())
                    dve.tensor_tensor(qdec[w][:], qn[w][:], egrow[w][:], ALU.mult).then_inc(dn_vec[w], c_.up())
                for w in range(2):
                    c_ = chain[w]
                    dve.wait_ge(dn_pool[w], g0 + 5)
                    dve.tensor_tensor(XT[w][:], over_h(ident), lowT[w][0][:], ALU.subtract).then_inc(dn_vec[w], c_.up())
                    dve.wait_ge(dn_mm[w], 1 + m0 + 7)
                    dve.tensor_tensor(X[w][:], over_h(ident), bank[4 * w + 1], ALU.subtract).then_inc(dn_vec[w], c_.up())
                    assert c_.n == 11
                for s in range(1, 6):
                    for w in range(2):
                        c_ = chain[w]
                        own(w)
                        dve.wait_ge(dn_mm[w], 1 + m0 + 7 + 2 * s)
                        if s < 5:
                            dve.tensor_tensor(X[w][:], X[w][:], bank[4 * w + 2], ALU.subtract).then_inc(dn_vec[w], c_.up())
                        dve.tensor_tensor(XT[w][:], XT[w][:], bank[4 * w + 3], ALU.subtract).then_inc(dn_vec[w], c_.up())
                for w in range(2):
                    c_, b = chain[w], 4 * w
                    assert c_.n == 20
                    for c in range(2):
                        lo = c * CHUNK
                        dve.wait_ge(dn_mm[w], 1 + m0 + 19 + 3 * c)
                        dve.wait_ge(dn_act[w], 1 + a0 + 12)
                        dve.wait_ge(dn_pool[w], g0 + 7)
                        dve.tensor_tensor(vz[w][lo:lo + CHUNK, c], u[w][lo:lo + CHUNK], bank[b + 2][lo:lo + CHUNK],
                                          ALU.subtract).then_inc(dn_vec[w], c_.up())
                        dve.wait_ge(dn_mm[w], 1 + m0 + 21 + 3 * c)
                        for h in range(H):
                            dve.scalar_tensor_tensor(St[:, h], St[:, h], egrow[w][:, h, lo + CHUNK - 1:lo + CHUNK], bank[b][:, h],
                                                     ALU.mult, ALU.add).then_inc(dn_vec[w], c_.up())
                    assert c_.n == DNV, c_.n

            for w in range(2):
                dve.wait_ge(dn_act[w], 1 + DNA * TILES // 2)
                dve.wait_ge(dn_vec[w], 1 + DNV * TILES // 2)
                dve.memset(qz[w][:], 0.0)
            dve.tensor_copy(mbuf[:], wmask0).then_inc(gate_vec, 1)
            dve.wait_ge(gate_vec, 10)
            with dve.Fori(0, TILES // 2) as i:
                m0, a0 = SWM * i, SWA_ * i
                chain = [Chain(SWV[w] * i) for w in range(2)]

                def own(w):
                    dve.wait_ge(sw_vec[w], 1 + chain[w].now())
                for w in range(2):
                    c_, t = chain[w], 2 * i + w
                    dve.wait_ge(sw_mm[w], 1 + m0)
                    own(w)
                    for r in range(2):
                        rr = slice(r * HD, (r + 1) * HD)
                        dve.tensor_scalar(qz[w][rr, 4 * r:4 * r + 4], zq[rr, 4:8, bass.ds(t * P, P)], float(HD) ** -0.5, None,
                                          ALU.mult).then_inc(sw_vec[w], c_.up())
                    dve.tensor_copy(vbuf[w][:].rearrange("p b n -> p (b n)"),
                                    vtok[:].rearrange("p b n -> p (b n)")[:, bass.ds(t * P, 2 * P)]).then_inc(sw_vec[w], c_.up())
                for w in range(2):
                    c_, st = chain[w], stat[w]
                    dve.wait_ge(sw_mm[w], 1 + m0 + 1)
                    scores = ps[:, 4 * w:4 * w + 4, :].rearrange("p b (h n) -> p (b h) n", h=2)
                    mask = wmask if w else mbuf[:]
                    dve.tensor_tensor(prob[w][:], scores, mask.unsqueeze(1).to_broadcast([P, QH, 2 * P]), ALU.add).then_inc(sw_vec[w], c_.up())
                    own(w)
                    dve.tensor_reduce(st[:, 0], prob[w][:], AX.X, ALU.max).then_inc(sw_vec[w], c_.up())
                    own(w)
                    sinks = rows[:, 8:16]
                    dve.tensor_tensor(st[:, 1], st[:, 0], sinks, ALU.max).then_inc(sw_vec[w], c_.up())
                    own(w)
                    dve.tensor_tensor(st[:, 2], sinks, st[:, 1], ALU.subtract)
                    dve.tensor_tensor(prob2[w][:], prob[w][:], st[:, 1].unsqueeze(2).to_broadcast([P, QH, 2 * P]), ALU.subtract).then_inc(sw_vec[w], c_.up())
                for w in range(2):
                    c_, st = chain[w], stat[w]
                    dve.wait_ge(sw_act[w], 1 + a0 + 2)
                    dve.tensor_reduce(st[:, 4], prob[w][:], AX.X, ALU.add).then_inc(sw_vec[w], c_.up())
                    own(w)
                    dve.tensor_tensor(st[:, 5], st[:, 4], st[:, 3], ALU.add).then_inc(sw_vec[w], c_.up())
                    own(w)
                    dve.reciprocal(st[:, 4], st[:, 5]).then_inc(sw_vec[w], c_.up())
                    own(w)
                    dve.tensor_tensor(prob2[w][:], prob[w][:], st[:, 4].unsqueeze(2).to_broadcast([P, QH, 2 * P]), ALU.mult).then_inc(sw_vec[w], c_.up())
                    if w == 0:
                        dve.tensor_copy(mbuf[:], wmask).then_inc(sw_vec[w], c_.up())
                    assert c_.n == SWV[w], c_.n

            for c in range(H):
                dve.wait_ge(gn_root, 2 * c + 2)
                dve.scalar_tensor_tensor(qkv[:, c], qkv[:, c], OGAIN, rstd[:, c % 2], ALU.mult, ALU.mult).then_inc(gn_vec, 1)
                dve.wait_ge(gn_vec, 2 * c + 1)
                dve.wait_ge(z_silu, c + 1)
                dve.tensor_tensor(qkv[:, c], qkv[:, c], zq[:, c], ALU.mult).then_inc(gn_vec, 1)

            with dve.Fori(0, DC // 2) as i:
                for s in range(2):
                    for h in range(2):
                        n = 2 * (2 * i + s) + h
                        dve.wait_ge(up_sig, 2 * n + 2)
                        for b in range(2):
                            dve.tensor_tensor(mtmp[:, h, b], sig[:, h, b], ps[:, 4 * h + 2 + b, :], ALU.mult).then_inc(up_vec, 1)
                        dve.wait_ge(up_vec, 2 * n + 2)
                        dst = merged[:, bass.ds(2 * i + s, 1), h * HALF:(h + 1) * HALF].rearrange("p o t -> p (o t)")
                        dve.tensor_tensor(dst, mtmp[:, h, 0], mtmp[:, h, 1], ALU.add).then_inc(up_done, 1)
            dve.wait_ge(x_back, 16)
            dve.wait_ge(up_done, 1 + 2 * DC)
            with dve.Fori(0, DC // 2) as i:
                for s in range(2):
                    dve.wait_ge(wo_mm, 1 + 2 * i + s + 1)
                    row = xT[:, bass.ds(2 * i + s, 1), :].rearrange("p o t -> p (o t)")
                    dve.scalar_tensor_tensor(row, halves(ps, 2 * s), mod[:, bass.ds(16 + 2 * i + s, 1)], row, ALU.mult, ALU.add).then_inc(x2_done, 1)
            dve.wait_ge(x2_done, 1 + DC)
            norm_apply(1, xT, rstd, hT, amp2, mod[:, 24:32])

            def fl(x):
                return x.rearrange("p k m -> p (k m)")

            for c in range(DC):
                dve.wait_ge(h2_hi, c + 1)
                dve.tensor_tensor(h2lo[:, c], hT[:, c], h2hi[:, c].bitcast(F32), ALU.subtract).then_inc(h2_lo, 1)
            with dve.Fori(0, 8) as i:
                for s in range(2):
                    dve.wait_ge(q_hi, 2 * i + s + 1)
                    dve.tensor_tensor(fl(qs_lo[:, s]), fl(wjob[:, s]), fl(qs_hi[:, s]).bitcast(F32), ALU.subtract).then_inc(q_lo, 1)
                for s in range(2):
                    dve.wait_ge(s_mm, 1 + 2 * i + s + 1)
                    dve.wait_ge(score_out[s], 16 + 16 * i)
                    dve.tensor_copy(fl(sj[:, s]), halves(ps, 4 + 2 * s)).then_inc(s_copied, 1)

            def u_low(n, s):
                dve.wait_ge(uhi_ready, n + 1)
                dve.tensor_tensor(fl(ulo[:, s]), fl(ust[:, s]), fl(uhi[:, s]).bitcast(F32), ALU.subtract).then_inc(u_ready, 1)

            for s in range(2):
                u_low(s, s)
            with dve.Fori(0, TILES) as i:
                c_ = Chain(RTV * i)
                n = PER_TILE * i

                def top16(m, vals, idx, src, tmp):
                    def each(f):
                        dve.wait_ge(rt_vec, 1 + c_.now())
                        dve.memset(carrier[:, 0:1], 0.0)
                        for j in range(m):
                            op = f(j)
                        op.then_inc(rt_vec, c_.up())
                    each(lambda j: dve.max(vals[:, j, 0:8], src[:, j]))
                    each(lambda j: dve.max_index(idx[:, j, 0:8], vals[:, j, 0:8], src[:, j]))
                    each(lambda j: dve.match_replace(tmp[:, j], vals[:, j, 0:8], src[:, j], LOWEST))
                    each(lambda j: dve.max(vals[:, j, 8:16], tmp[:, j]))
                    each(lambda j: dve.max_index(idx[:, j, 8:16], vals[:, j, 8:16], tmp[:, j]))

                dve.wait_ge(score_in, 16 * i + 16)
                top16(16, sv, si, sc, sc2)
                u_low(n + 2, 0)
                dve.wait_ge(rt_vec, 1 + c_.now())
                dve.tensor_copy(sif[:], si[:]).then_inc(rt_vec, c_.up())
                sv4 = sv[:].rearrange("p (h two) k -> p h two k", two=2)
                shape = [P, PH, TOPK, TOPK]
                cand = sc[:].rearrange("p (h two) n -> p h (two n)", two=2)
                cand2 = sc2[:].rearrange("p (h two) n -> p h (two n)", two=2)
                dve.tensor_tensor(cand.rearrange("p h (a b) -> p h a b", b=TOPK), sv4[:, :, 0, :].unsqueeze(3).to_broadcast(shape),
                                  sv4[:, :, 1, :].unsqueeze(2).to_broadcast(shape), ALU.add).then_inc(rt_vec, c_.up())
                top16(PH, cv, ci, cand, cand2)
                assert c_.n == 12
                dve.wait_ge(rt_vec, 1 + c_.now())
                flat_ci = ci[:].rearrange("p h k -> p (h k)")
                dve.tensor_scalar(cab[:, 0], flat_ci, 4, None, ALU.logical_shift_right)
                dve.tensor_scalar(cab[:, 1], flat_ci, 15, None, ALU.bitwise_and).then_inc(rt_vec, c_.up())
                dve.wait_ge(rt_vec, 1 + c_.now())
                dve.tensor_copy(cabf[:], cab[:]).then_inc(rt_vec, c_.up())
                assert c_.n == 14
                dve.tensor_copy(gsum[:, 0], cv[:, :, 0]).then_inc(rt_vec, c_.up())
                dve.wait_ge(rt_vec, 1 + c_.now())
                top = gsum[:, 0].unsqueeze(2).to_broadcast([P, PH, TOPK])
                dve.tensor_tensor(cv[:], cv[:], top, ALU.subtract).then_inc(rt_vec, c_.up())
                assert c_.n == 16
                dve.tensor_tensor(eqa[:], cabf[:, 0].rearrange("p (h k) -> p h k", h=PH).unsqueeze(3).to_broadcast(shape),
                                  iota[:, 0:TOPK].unsqueeze(1).unsqueeze(1).to_broadcast(shape), ALU.is_equal).then_inc(rt_vec, c_.up())
                u_low(n + 3, 1)
                sif4 = sif[:].rearrange("p (h two) k -> p h two k", two=2)
                eq = cand2.rearrange("p h (k a) -> p h k a", k=TOPK)
                dve.tensor_tensor(eq, cabf[:, 1].rearrange("p (h k) -> p h k", h=PH).unsqueeze(3).to_broadcast(shape),
                                  iota[:, 0:TOPK].unsqueeze(1).unsqueeze(1).to_broadcast(shape), ALU.is_equal).then_inc(rt_vec, c_.up())
                dve.wait_ge(rt_vec, 1 + c_.now())
                dve.tensor_tensor(eq, eq, sif4[:, :, 1, :].unsqueeze(2).to_broadcast(shape), ALU.mult).then_inc(rt_vec, c_.up())
                dve.wait_ge(rt_vec, 1 + c_.now())
                dve.tensor_reduce(pick[:, 1].rearrange("p (h k) -> p h k", h=PH), eq, AX.X, ALU.add).then_inc(rt_vec, c_.up())
                dve.wait_ge(rt_exp, i + 1)
                dve.tensor_reduce(gsum[:, 1], cv[:], AX.X, ALU.add).then_inc(rt_vec, c_.up())
                dve.wait_ge(rt_vec, 1 + c_.now())
                dve.reciprocal(gsum[:, 0], gsum[:, 1]).then_inc(rt_vec, c_.up())
                dve.wait_ge(rt_vec, 1 + c_.now())
                dve.tensor_tensor(pick[:, 2].rearrange("p (h k) -> p h k", h=PH), cv[:],
                                  gsum[:, 0].unsqueeze(2).to_broadcast([P, PH, TOPK]), ALU.mult).then_inc(rt_vec, c_.up())
                dve.wait_ge(rt_pool, i + 1)
                dve.tensor_reduce(pick[:, 0].rearrange("p (h k) -> p h k", h=PH), eqa[:], AX.X, ALU.add).then_inc(rt_vec, c_.up())
                assert c_.n == RTV - 1, c_.n
                dve.wait_ge(rt_mm, i + 1)
                dve.tensor_copy(rT[:].rearrange("p r n -> p (r n)"), ps[:, 4, 0:3 * P]).then_inc(rt_vec, c_.up())
                u_low(n + 4, 0)
                dve.wait_ge(rt_vec, 1 + c_.now())
                dve.memset(carrier[:, 0:1], 0.0)
                with dve.Fori(0, P // 16) as j:
                    n0 = 16 * (8 * i + j)
                    for t in range(16):
                        if t % 4 == 0:
                            dve.wait_ge(g_mm, n0 + t + 4)
                            dve.tensor_tensor(oneL[:, t % 8:t % 8 + 4], iota.unsqueeze(1).to_broadcast([P, 4, P]),
                                              rT[:, 0, bass.ds(16 * j + t, 4)].unsqueeze(2).to_broadcast([P, 4, P]),
                                              ALU.is_equal).then_inc(left_ready, 4)
                        col = [rT[:, m, bass.ds(16 * j + t, 1)] for m in (1, 2)]
                        dve.wait_ge(g_mm, n0 + t + 1)
                        dve.tensor_scalar(oneR[:, t % 8], iota, col[0], col[1], ALU.is_equal, ALU.mult).then_inc(right_ready, 1)
                u_low(n + 5, 1)

            def weigh(j, s, first=False, landed=None):
                if landed is None:
                    dve.wait_ge(act_ready, 2 * (LEAD + j) + s + 3)
                else:
                    dve.wait_ge(act_in[s], landed)
                dve.wait_ge(gst_in[s], 16 * j + 16)
                if not first:
                    dve.wait_ge(wlo_ready, 2 * j + s - 1)
                dve.tensor_tensor(wbuf[:, s], gst[:, s], actb[:, s], ALU.mult).then_inc(w_ready, 1)

            def w_low(j, s, par):
                dve.wait_ge(whi_ready, 2 * j + s + 1)
                dve.tensor_tensor(wlo[:, par, s], wbuf[:, s], whi[:, par, s].bitcast(F32), ALU.subtract).then_inc(wlo_ready, 1)

            def v_low(j, s, hi, lo):
                dve.wait_ge(vhi_ready, 2 * j + s + 1)
                dve.tensor_tensor(lo, vst[:, s], hi.bitcast(F32), ALU.subtract).then_inc(v_ready, 1)

            def flush(j, b0=0, b1=16):
                for b in range(b0, b1):
                    dve.wait_ge(v_mm, 16 * j + b + 1)
                    o = acc[:, b // 2, (b % 2) * HALF:(b % 2 + 1) * HALF]
                    dve.tensor_tensor(o, o, ps[:, 4 + b % 4, :], ALU.add).then_inc(flushed, 1)

            def step(j, par, first=False, last=False):
                for s in range(2):
                    weigh(j, s, first)
                    if not last:
                        u_low(2 * (LEAD + j + 1) + s, s)
                    w_low(j, s, par)
                if not first:
                    flush(j - 1)
                for s in range(2):
                    v_low(j, s, vhi[:, s], vlo[:, s])

            step(0, 0, first=True)
            dve.wait_ge(acc_zero, 1)
            step(1, 1)
            with dve.Fori(1, FULL // 2 - 1) as i:
                for par in range(2):
                    step(2 * i + par, par)
            step(FULL - 2, 0)
            step(FULL - 1, 1, last=True)
            with dve.Fori(FULL // 2, GROUPS // 2) as i:
                for par in range(2):
                    j = 2 * i + par
                    hi, lo = (vhi, vlo) if par else (uhi, ulo)
                    for s in range(2):
                        weigh(j, s, landed=16 * (j - FULL) + 16)
                        w_low(j, s, par)
                        flush(j - 1, 4 * s, 4 * s + 4)
                    for s in range(2):
                        v_low(j, s, hi[:, s] if par else fl(hi[:, s]), lo[:, s] if par else fl(lo[:, s]))
                        flush(j - 1, 8 + 4 * s, 12 + 4 * s)
            flush(GROUPS - 1)

            dve.wait_ge(flushed, 16 * GROUPS)
            dve.wait_ge(x2_in, 16)
            for c in range(DC):
                dve.scalar_tensor_tensor(acc[:, c], acc[:, c], mod[:, 40 + c:41 + c], x2[:, c], ALU.mult, ALU.add).then_inc(x3_done, 1)
            dve.wait_ge(x3_done, DC)
            norm_apply(2, acc, erstd, oT, GF, None)


def constants():
    i = np.arange(P)
    f = np.float32
    keep = np.concatenate([np.eye(P), np.tile(i, (P, 1)), np.ones((P, P))], 1).astype(f)
    same = (i[:, None] // CHUNK) == (i[None, :] // CHUNK)
    tri = same & (i[:, None] <= i[None, :])
    parts = [tri, same, np.where(tri, 0.0, -BIG)]
    for s in range(6):
        w = 1 << s
        parts.append(((i[:, None] // (2 * w)) == (i[None, :] // (2 * w))) & ((i[:, None] // w) % 2 == 0) & ((i[None, :] // w) % 2 == 1))
    j = np.arange(2 * P)
    own = i[:, None] // CHUNK + 2
    kc = j[None, :] // CHUNK
    ok = (kc == own) | (kc == own - 1)
    parts.append(np.where(ok, 0.0, -BIG))
    parts.append(np.where(ok & (j[None, :] >= P), 0.0, -BIG))
    return keep, np.concatenate([np.asarray(x, f) for x in parts], 1)


def lay_out(x, c, ada_w, ada_b, norm1_gain, w_in, conv_w, dn_a_log, dn_dt_bias, dn_out_gain, swa_sinks, w_dn_up,
            w_swa_up, w_out, norm2_gain, peer_w_q, peer_sub_keys, peer_u, peer_v, final_gain):
    keep, masks = constants()

    def col(v):
        return v.reshape(-1, P).T

    def blocks(w):
        k, n = w.shape
        return w.reshape(k // P, P, n // P, P).transpose(2, 1, 0, 3)

    w = w_in[0]
    q0 = 1536 + 8 + 512
    heads = [slice(q0 + h * HD, q0 + (h + 1) * HD) for g in range(4) for h in (g, g + 4)]
    k0 = q0 + 512
    g0 = k0 + 256
    front = np.concatenate([w[:, 0:1536], w[:, 1544:1544 + 512]] + [w[:, s] for s in heads] + [w[:, k0:k0 + P]], 1)
    small = np.concatenate([w[:, 1536:1544], w[:, k0 + P:k0 + 2 * P]], 1)
    up_rows = np.concatenate([w_swa_up[0][h * HD:(h + 1) * HD] for g in range(4) for h in (g, g + 4)], 0)
    up = np.concatenate([blocks(w[:, g0:g0 + D]), blocks(w[:, g0 + D:g0 + 2 * D]), blocks(w_dn_up[0]), blocks(up_rows)], 2)
    conv = conv_w[0].reshape(12, P, 4).transpose(1, 0, 2).reshape(P, 48)
    row = np.broadcast_to(np.concatenate([dn_dt_bias[0], dn_a_log[0], swa_sinks[0]])[None, :], (P, 16))
    cols = np.concatenate([col(c[0]), col(ada_b[0]), col(norm1_gain[0]), col(norm2_gain[0]), col(final_gain), conv,
                           dn_out_gain[0].reshape(P, 1), row], 1)
    return {
        "c_keep": keep, "c_masks": masks, "p_cols": cols,
        "xT": x[0].T, "ada_w": ada_w[0],
        "w_in": blocks(front), "w_small": small.reshape(DC, P, SMALL).transpose(1, 0, 2),
        "w_up": up, "w_out": blocks(w_out[0]), "w_q": blocks(peer_w_q[0]),
        "sub_k": peer_sub_keys[0].reshape(16, NK, P).transpose(2, 0, 1),
        "u": peer_u[0].reshape(NK, NK, DC, P).transpose(1, 3, 2, 0),
        "v": peer_v[0].reshape(NK, NK, D).transpose(1, 0, 2),
    }


def kernel(**inputs):
    import concourse.bacc as _bacc
    from concourse.bass_utils import run_bass_kernel_spmd as _run

    data = {k: np.ascontiguousarray(v) for k, v in lay_out(**{k: np.asarray(v) for k, v in inputs.items()}).items()}
    nc = _bacc.Bacc("TRN2", target_bir_lowering=False, num_devices=1)
    arrays, args = {}, {}
    for name, v in data.items():
        arrays[f"in_{name}"] = v
        args[name] = nc.dram_tensor(f"in_{name}", list(v.shape), mybir.dt.from_np(v.dtype), kind="ExternalInput").ap()
    out = nc.dram_tensor("out_T", [D, T], F32, kind="ExternalOutput").ap()
    block_kernel(nc, args, out)
    r = _run(nc, [arrays], core_ids=[0])
    return np.ascontiguousarray(r.results[0]["out_T"].T).reshape(1, T, D)
```
